# Optimizing a Trainium2 kernel written in Bass

```python
import numpy as np
import jax
import jax.numpy as jnp
from jax import lax
import jax, jax.numpy as jnp

D_MODEL = 1024
BATCH = 1
SEQ = 256
DEPTH = 2

HEAD_DIM = 64
GLA_HEADS = 4
GLA_WIDTH = GLA_HEADS * HEAD_DIM
GLA_GATE_RANK = 16
GLA_TAU = 16.0
GLA_CHUNK = 64
RWKV_HEADS = 4
RWKV_WIDTH = RWKV_HEADS * HEAD_DIM
RWKV_DECAY_RANK = 64
RWKV_ICLR_RANK = 64
RWKV_VRES_RANK = 32
RWKV_GATE_RANK = 160
RWKV_GN_EPS = 64e-5
NSA_HEADS = 8
NSA_KV_HEADS = 2
NSA_WIDTH = NSA_HEADS * HEAD_DIM
NSA_KV_WIDTH = NSA_KV_HEADS * HEAD_DIM
NSA_CMP_BLOCK = 32
NSA_CMP_STRIDE = 16
NSA_CMP_HIDDEN = 256
NSA_SEL_BLOCK = 64
NSA_N_SELECT = 16
NSA_WINDOW = 512
NSA_SEL_QCHUNK = 32
NSA_WIN_QBLOCK = 128
ROPE_THETA = 10000.0
FFN_HIDDEN = ((8 * D_MODEL + 3 * 256 - 1) // (3 * 256)) * 256
DEEPNORM_ALPHA = (2 * DEPTH) ** 0.25
DEEPNORM_BETA = (8 * DEPTH) ** -0.25
LN_EPS = 1e-5
MASK_NEG = -1e30

GLA_COLS = (GLA_WIDTH, GLA_WIDTH, GLA_WIDTH, GLA_WIDTH, GLA_GATE_RANK)
RWKV_COLS = (RWKV_WIDTH, RWKV_WIDTH, RWKV_WIDTH,
             RWKV_DECAY_RANK, RWKV_ICLR_RANK, RWKV_GATE_RANK)
NSA_COLS = (NSA_WIDTH,) + (NSA_KV_WIDTH,) * 6 + (3 * NSA_HEADS,)
IN_COLS = sum(GLA_COLS) + sum(RWKV_COLS) + sum(NSA_COLS)


def _split(h, widths):
    idx = np.cumsum(np.asarray(widths))[:-1].tolist()
    return jnp.split(h, idx, axis=-1)

def _layer_norm(x, w, b):
    xf = x.astype(jnp.float32)
    mu = xf.mean(-1, keepdims=True)
    var = jnp.square(xf - mu).mean(-1, keepdims=True)
    return ((xf - mu) * lax.rsqrt(var + LN_EPS) * w + b).astype(x.dtype)

def _head_norm(x, w, b, n_heads, eps):
    shp = x.shape
    xh = x.astype(jnp.float32).reshape(shp[:-1] + (n_heads, shp[-1] // n_heads))
    mu = xh.mean(-1, keepdims=True)
    var = jnp.square(xh - mu).mean(-1, keepdims=True)
    xh = (xh - mu) * lax.rsqrt(var + eps)
    return xh.reshape(shp) * w + b

def _rope(x, pos):
    half = x.shape[-1] // 2
    inv = ROPE_THETA ** (-jnp.arange(half, dtype=jnp.float32) / half)
    ang = pos.astype(jnp.float32)[:, None] * inv
    shape = (ang.shape[0],) + (1,) * (x.ndim - 3) + (half,)
    cos = jnp.cos(ang).reshape(shape).astype(x.dtype)
    sin = jnp.sin(ang).reshape(shape).astype(x.dtype)
    x1, x2 = x[..., :half], x[..., half:]
    return jnp.concatenate([x1 * cos - x2 * sin, x1 * sin + x2 * cos], axis=-1)

def _token_shift_mix(p, mu):
    prev = jnp.pad(p, ((0, 0), (1, 0), (0, 0)))[:, :-1]
    return p + (prev - p) * mu

def _gla_mixer(q, k, v, g, a_lr, w_a2, b_a, ln_w, ln_b):
    dt = q.dtype
    B, S, _ = q.shape
    H, dk, C = GLA_HEADS, HEAD_DIM, GLA_CHUNK
    n = S // C
    f32 = jnp.float32
    log_a = jax.nn.log_sigmoid((a_lr @ w_a2 + b_a).astype(f32)) / GLA_TAU

    def chunks(t):
        return t.astype(f32).reshape(B, n, C, H, dk).transpose(1, 0, 3, 2, 4)

    qc, kc, vc, ac = chunks(q * dk ** -0.5), chunks(k), chunks(v), chunks(log_a)
    causal = jnp.tril(jnp.ones((C, C), bool))[:, :, None]

    def step(state, inp):
        qi, ki, vi, ai = inp
        b = jnp.cumsum(ai, axis=2)
        inter = jnp.einsum('bhtk,bhkv->bhtv', qi * jnp.exp(b), state)
        diff = b[:, :, :, None, :] - b[:, :, None, :, :]
        decay = jnp.exp(jnp.where(causal, diff, -jnp.inf))
        scores = jnp.einsum('bhtk,bhsk,bhtsk->bhts', qi, ki, decay)
        intra = jnp.einsum('bhts,bhsv->bhtv', scores, vi)
        b_end = b[:, :, -1:, :]
        state = (jnp.exp(b_end[:, :, 0, :, None]) * state
                 + jnp.einsum('bhsk,bhsv->bhkv', ki * jnp.exp(b_end - b), vi))
        return state, inter + intra

    s0 = jnp.zeros((B, H, dk, dk), f32)
    _, o = lax.scan(step, s0, (qc, kc, vc, ac))
    o = o.transpose(1, 0, 3, 2, 4).reshape(B, S, H * dk)
    o = _head_norm(o, ln_w, ln_b, H, LN_EPS)
    return (o * jax.nn.silu(g.astype(f32))).astype(dt)

def _rwkv7_mixer(r, k, v, w_lr, a_lr, g_lr, w0, w2, a0, a2, g2, k_k, k_a, r_k, ln_w, ln_b):
    dt = r.dtype
    B, S, _ = r.shape
    H, N = RWKV_HEADS, HEAD_DIM
    f32 = jnp.float32
    r, k, v = r.astype(f32), k.astype(f32), v.astype(f32)
    w_log = -jax.nn.softplus(-(w0 + jnp.tanh(w_lr) @ w2).astype(f32)) - 0.5
    decay = jnp.exp(-jnp.exp(w_log))
    a = jax.nn.sigmoid((a0 + a_lr @ a2).astype(f32))
    g = (jax.nn.sigmoid(g_lr) @ g2).astype(f32)
    kk = (k * k_k).reshape(B, S, H, N)
    kk = kk / jnp.maximum(jnp.sqrt(jnp.sum(kk * kk, axis=-1, keepdims=True)), 1e-12)
    k = k * (1.0 + (a - 1.0) * k_a)

    def heads(t):
        return t.reshape(B, S, H, N).transpose(1, 0, 2, 3)

    a_h = a.reshape(B, S, H, N)
    xs = (heads(r), heads(decay), heads(k), heads(v),
          (-kk).transpose(1, 0, 2, 3), (kk * a_h).transpose(1, 0, 2, 3))

    def step(state, inp):
        r_t, w_t, k_t, v_t, a_t, b_t = inp
        sa = jnp.einsum('bhvk,bhk->bhv', state, a_t)
        state = (state * w_t[:, :, None, :] + sa[..., None] * b_t[:, :, None, :]
                 + v_t[..., None] * k_t[:, :, None, :])
        return state, jnp.einsum('bhvk,bhk->bhv', state, r_t)

    s0 = jnp.zeros((B, H, N, N), f32)
    _, y = lax.scan(step, s0, xs)
    y = y.transpose(1, 0, 2, 3).reshape(B, S, H * N)
    y = _head_norm(y, ln_w, ln_b, H, RWKV_GN_EPS)
    bonus = (jnp.sum((r * k).reshape(B, S, H, N) * r_k, axis=-1, keepdims=True)
             * v.reshape(B, S, H, N)).reshape(B, S, H * N)
    return ((y + bonus) * g).astype(dt)

def _compress(t, pos_emb, w1, w2):
    B, S, G, hd = t.shape
    n_sub = NSA_CMP_BLOCK // NSA_CMP_STRIDE
    ncb = S // NSA_CMP_STRIDE
    nc = ncb - n_sub + 1
    t_s = t.reshape(B, ncb, NSA_CMP_STRIDE, G, hd)
    blocks = jnp.concatenate([t_s[:, j:j + nc] for j in range(n_sub)], axis=2)
    blocks = blocks + pos_emb[None, None, :, None, :]
    flat = blocks.transpose(0, 1, 3, 2, 4).reshape(B, nc, G, NSA_CMP_BLOCK * hd)
    return jax.nn.gelu(flat @ w1) @ w2

def _overlap_matrix(seq):
    nc = seq // NSA_CMP_STRIDE - NSA_CMP_BLOCK // NSA_CMP_STRIDE + 1
    ns = seq // NSA_SEL_BLOCK
    c0 = np.arange(nc) * NSA_CMP_STRIDE
    s0 = np.arange(ns) * NSA_SEL_BLOCK
    lo = np.maximum(c0[:, None], s0[None, :])
    hi = np.minimum(c0[:, None] + NSA_CMP_BLOCK, s0[None, :] + NSA_SEL_BLOCK)
    return (np.maximum(hi - lo, 0) / NSA_CMP_STRIDE).astype(np.float32)

def _selected_attention(q, k, v, idx, pos):
    B, S, G, HPG, hd = q.shape
    n = idx.shape[-1]
    ns = S // NSA_SEL_BLOCK
    kb = k.reshape(B, ns, NSA_SEL_BLOCK, G, hd).transpose(0, 3, 1, 2, 4)
    vb = v.reshape(B, ns, NSA_SEL_BLOCK, G, hd).transpose(0, 3, 1, 2, 4)
    qcs = NSA_SEL_QCHUNK
    nq = S // qcs
    q_ch = q.reshape(B, nq, qcs, G, HPG, hd).transpose(1, 0, 2, 3, 4, 5)
    idx_ch = idx.reshape(B, G, nq, qcs, n).transpose(2, 0, 1, 3, 4)
    pos_ch = pos.reshape(nq, qcs)
    bi = jnp.arange(B)[:, None, None, None]
    gi = jnp.arange(G)[None, :, None, None]
    offs = jnp.arange(NSA_SEL_BLOCK)

    def one(args):
        qc, ic, tc = args
        kg = kb[bi, gi, ic]
        vg = vb[bi, gi, ic]
        s = jnp.einsum('bqghd,bgqnkd->bghqnk', qc, kg).astype(jnp.float32)
        kpos = ic[..., None] * NSA_SEL_BLOCK + offs
        valid = kpos <= tc[None, None, :, None, None]
        s = jnp.where(valid[:, :, None], s, MASK_NEG).reshape(B, G, HPG, qcs, n * NSA_SEL_BLOCK)
        pr = jax.nn.softmax(s, axis=-1).reshape(B, G, HPG, qcs, n, NSA_SEL_BLOCK)
        return jnp.einsum('bghqnk,bgqnkd->bqghd', pr.astype(vg.dtype), vg)

    o = lax.map(one, (q_ch, idx_ch, pos_ch))
    return o.transpose(1, 0, 2, 3, 4, 5).reshape(B, S, G, HPG, hd)

def _window_attention(q, k, v):
    B, S, G, HPG, hd = q.shape
    qb_sz, win = NSA_WIN_QBLOCK, NSA_WINDOW
    nb = S // qb_sz
    kp = jnp.pad(k, ((0, 0), (win, 0), (0, 0), (0, 0)))
    vp = jnp.pad(v, ((0, 0), (win, 0), (0, 0), (0, 0)))
    q_bl = q.reshape(B, nb, qb_sz, G, HPG, hd).transpose(1, 0, 2, 3, 4, 5)
    rel = jnp.arange(qb_sz)[:, None] + win - jnp.arange(qb_sz + win)[None, :]

    def one(args):
        qb, i = args
        start = i * qb_sz
        kb = lax.dynamic_slice_in_dim(kp, start, qb_sz + win, axis=1)
        vb = lax.dynamic_slice_in_dim(vp, start, qb_sz + win, axis=1)
        s = jnp.einsum('bqghd,bkgd->bghqk', qb, kb).astype(jnp.float32)
        kpos = start - win + jnp.arange(qb_sz + win)
        valid = (rel >= 0) & (rel < win) & (kpos[None, :] >= 0)
        pr = jax.nn.softmax(jnp.where(valid, s, MASK_NEG), axis=-1)
        return jnp.einsum('bghqk,bkgd->bqghd', pr.astype(vb.dtype), vb)

    o = lax.map(one, (q_bl, jnp.arange(nb)))
    return o.transpose(1, 0, 2, 3, 4, 5).reshape(B, S, G, HPG, hd)

def _nsa_mixer(h, pos, pos_k, pos_v, wk1, wk2, wv1, wv2):
    dt = h.dtype
    B, S, _ = h.shape
    G, HPG, hd = NSA_KV_HEADS, NSA_HEADS // NSA_KV_HEADS, HEAD_DIM
    q, kc, vc, ks, vs, kw, vw, gate = _split(h, NSA_COLS)
    q = _rope(q.reshape(B, S, G, HPG, hd), pos) * hd ** -0.5
    kc, ks, kw = (_rope(t.reshape(B, S, G, hd), pos) for t in (kc, ks, kw))
    vc, vs, vw = (t.reshape(B, S, G, hd) for t in (vc, vs, vw))

    k_cmp = _compress(kc, pos_k, wk1, wk2)
    v_cmp = _compress(vc, pos_v, wv1, wv2)
    nc = k_cmp.shape[1]
    s_cmp = jnp.einsum('bsghd,bcgd->bghsc', q, k_cmp).astype(jnp.float32)
    block_end = jnp.arange(nc) * NSA_CMP_STRIDE + NSA_CMP_BLOCK - 1
    valid_c = block_end[None, :] <= pos[:, None]
    p_cmp = jax.nn.softmax(jnp.where(valid_c, s_cmp, MASK_NEG), axis=-1) * valid_c
    o_cmp = jnp.einsum('bghsc,bcgd->bsghd', p_cmp.astype(v_cmp.dtype), v_cmp)

    ns = S // NSA_SEL_BLOCK
    overlap = jnp.asarray(_overlap_matrix(S))
    imp = jnp.einsum('bghsc,cj->bgsj', p_cmp, overlap)
    cur = pos // NSA_SEL_BLOCK
    j = jnp.arange(ns)[None, :]
    forced = (j == 0) | (j == cur[:, None]) | (j == cur[:, None] - 1)
    sel_score = jnp.where(forced, 1e9, jnp.where(j > cur[:, None], -1e9, imp))
    _, idx = lax.top_k(sel_score, min(NSA_N_SELECT, ns))
    o_slc = _selected_attention(q, ks, vs, idx, pos)

    o_win = _window_attention(q, kw, vw)

    gt = jax.nn.sigmoid(gate.astype(jnp.float32)).reshape(B, S, G, HPG, 3)
    o = gt[..., 0:1] * o_cmp + gt[..., 1:2] * o_slc + gt[..., 2:3] * o_win
    return o.reshape(B, S, NSA_WIDTH).astype(dt)

def first_inputs(seed: int = 0) -> dict:
    key = jax.random.key(seed)
    ks = jax.random.split(key, 40)
    D, L = D_MODEL, DEPTH

    def nrm(k, shape, scale):
        return jax.random.normal(k, shape, jnp.float32) * scale

    def gain(k, shape):
        return 1.0 + 0.05 * jax.random.normal(k, shape, jnp.float32)

    rw_in = sum(RWKV_COLS)
    return {
        'x': nrm(ks[0], (BATCH, SEQ, D), 1.0),
        'w_in': nrm(ks[1], (L, D, IN_COLS), D ** -0.5),
        'w_in_vres': nrm(ks[2], (L - 1, D, RWKV_VRES_RANK), D ** -0.5),
        'gla_w_a2': nrm(ks[3], (L, GLA_GATE_RANK, GLA_WIDTH), GLA_GATE_RANK ** -0.5),
        'gla_b_a': nrm(ks[4], (L, GLA_WIDTH), 0.1),
        'gla_ln_w': gain(ks[5], (L, GLA_WIDTH)),
        'gla_ln_b': nrm(ks[6], (L, GLA_WIDTH), 0.02),
        'rwkv_mu': jax.random.uniform(ks[7], (L, rw_in), jnp.float32),
        'rwkv_mu_vres': jax.random.uniform(ks[8], (L - 1, RWKV_VRES_RANK), jnp.float32),
        'rwkv_w0': jax.random.uniform(ks[9], (L, RWKV_WIDTH), jnp.float32, -5.0, 1.0),
        'rwkv_w2': nrm(ks[10], (L, RWKV_DECAY_RANK, RWKV_WIDTH), 0.5 * RWKV_DECAY_RANK ** -0.5),
        'rwkv_a0': nrm(ks[11], (L, RWKV_WIDTH), 0.1),
        'rwkv_a2': nrm(ks[12], (L, RWKV_ICLR_RANK, RWKV_WIDTH), RWKV_ICLR_RANK ** -0.5),
        'rwkv_v0': nrm(ks[13], (L - 1, RWKV_WIDTH), 0.1),
        'rwkv_v2': nrm(ks[14], (L - 1, RWKV_VRES_RANK, RWKV_WIDTH), RWKV_VRES_RANK ** -0.5),
        'rwkv_g2': nrm(ks[15], (L, RWKV_GATE_RANK, RWKV_WIDTH), RWKV_GATE_RANK ** -0.5),
        'rwkv_k_k': 0.85 + 0.05 * jax.random.normal(ks[16], (L, RWKV_WIDTH), jnp.float32),
        'rwkv_k_a': gain(ks[17], (L, RWKV_WIDTH)),
        'rwkv_r_k': nrm(ks[18], (L, RWKV_HEADS, HEAD_DIM), 0.1),
        'rwkv_ln_w': gain(ks[19], (L, RWKV_WIDTH)),
        'rwkv_ln_b': nrm(ks[20], (L, RWKV_WIDTH), 0.02),
        'nsa_pos_k': nrm(ks[21], (L, NSA_CMP_BLOCK, HEAD_DIM), 0.02),
        'nsa_pos_v': nrm(ks[22], (L, NSA_CMP_BLOCK, HEAD_DIM), 0.02),
        'nsa_wk1': nrm(ks[23], (L, NSA_CMP_BLOCK * HEAD_DIM, NSA_CMP_HIDDEN), (NSA_CMP_BLOCK * HEAD_DIM) ** -0.5),
        'nsa_wk2': nrm(ks[24], (L, NSA_CMP_HIDDEN, HEAD_DIM), NSA_CMP_HIDDEN ** -0.5),
        'nsa_wv1': nrm(ks[25], (L, NSA_CMP_BLOCK * HEAD_DIM, NSA_CMP_HIDDEN), (NSA_CMP_BLOCK * HEAD_DIM) ** -0.5),
        'nsa_wv2': nrm(ks[26], (L, NSA_CMP_HIDDEN, HEAD_DIM), NSA_CMP_HIDDEN ** -0.5),
        'w_out': nrm(ks[27], (L, D, D), DEEPNORM_BETA * D ** -0.5),
        'ln1_w': gain(ks[28], (L, D)),
        'ln1_b': nrm(ks[29], (L, D), 0.02),
        'ffn_w_gate': nrm(ks[30], (L, D, FFN_HIDDEN), D ** -0.5),
        'ffn_w_up': nrm(ks[31], (L, D, FFN_HIDDEN), D ** -0.5),
        'ffn_w_down': nrm(ks[32], (L, FFN_HIDDEN, D), DEEPNORM_BETA * FFN_HIDDEN ** -0.5),
        'ln2_w': gain(ks[33], (L, D)),
        'ln2_b': nrm(ks[34], (L, D), 0.02),
    }

def first_block(x, w_in, w_in_vres, gla_w_a2, gla_b_a, gla_ln_w, gla_ln_b,
              rwkv_mu, rwkv_mu_vres, rwkv_w0, rwkv_w2, rwkv_a0, rwkv_a2, rwkv_v0, rwkv_v2,
              rwkv_g2, rwkv_k_k, rwkv_k_a, rwkv_r_k, rwkv_ln_w, rwkv_ln_b,
              nsa_pos_k, nsa_pos_v, nsa_wk1, nsa_wk2, nsa_wv1, nsa_wv2,
              w_out, ln1_w, ln1_b, ffn_w_gate, ffn_w_up, ffn_w_down, ln2_w, ln2_b):
    pos = jnp.arange(x.shape[1], dtype=jnp.int32)
    v_first = None
    for l in range(DEPTH):
        w_cols = w_in[l] if l == 0 else jnp.concatenate([w_in[l], w_in_vres[l - 1]], axis=1)
        h = x @ w_cols
        h_gla, h_rwkv, h_nsa, h_vres = _split(
            h, (sum(GLA_COLS), sum(RWKV_COLS), sum(NSA_COLS), h.shape[-1] - IN_COLS))

        gq, gk, gv, gg, galr = _split(h_gla, GLA_COLS)
        o_gla = _gla_mixer(gq, gk, gv, gg, galr, gla_w_a2[l], gla_b_a[l], gla_ln_w[l], gla_ln_b[l])

        rr, rk, rv, rwlr, ralr, rglr = _split(_token_shift_mix(h_rwkv, rwkv_mu[l]), RWKV_COLS)
        if l == 0:
            v_first = rv
        else:
            vlr = _token_shift_mix(h_vres, rwkv_mu_vres[l - 1])
            rv = rv + (v_first - rv) * jax.nn.sigmoid(rwkv_v0[l - 1] + vlr @ rwkv_v2[l - 1])
        o_rwkv = _rwkv7_mixer(rr, rk, rv, rwlr, ralr, rglr, rwkv_w0[l], rwkv_w2[l], rwkv_a0[l],
                              rwkv_a2[l], rwkv_g2[l], rwkv_k_k[l], rwkv_k_a[l], rwkv_r_k[l],
                              rwkv_ln_w[l], rwkv_ln_b[l])

        o_nsa = _nsa_mixer(h_nsa, pos, nsa_pos_k[l], nsa_pos_v[l], nsa_wk1[l], nsa_wk2[l],
                           nsa_wv1[l], nsa_wv2[l])

        mix = jnp.concatenate([o_gla, o_rwkv, o_nsa], axis=-1) @ w_out[l]
        x = _layer_norm(DEEPNORM_ALPHA * x + mix, ln1_w[l], ln1_b[l])

        ffn = (jax.nn.silu(x @ ffn_w_gate[l]) * (x @ ffn_w_up[l])) @ ffn_w_down[l]
        x = _layer_norm(DEEPNORM_ALPHA * x + ffn, ln2_w[l], ln2_b[l])
    return x


DEPTH_2 = 1

MIX_WIDTH = D_MODEL
ATTN_WIDTH = MIX_WIDTH // 2
N_Q_HEADS = ATTN_WIDTH // HEAD_DIM
N_KV_HEADS = 2
KV_GROUP = N_Q_HEADS // N_KV_HEADS
KV_WIDTH = N_KV_HEADS * HEAD_DIM
WINDOW = 128
ATTN_BLOCK = 128
LRU_WIDTH = MIX_WIDTH - ATTN_WIDTH
LRU_BLOCKS = 8
LRU_BLOCK_W = LRU_WIDTH // LRU_BLOCKS
CONV_WIDTH = 4
LRU_C = 8.0
IN_SPLITS = [ATTN_WIDTH, ATTN_WIDTH + KV_WIDTH, ATTN_WIDTH + 2 * KV_WIDTH, ATTN_WIDTH + 2 * KV_WIDTH + LRU_WIDTH]
IN_COLS_2 = ATTN_WIDTH + 2 * KV_WIDTH + 2 * LRU_WIDTH
N_EXPERTS = 32
TOP_K = 4
D_EXPERT = D_MODEL
SWIGLU_LIMIT = 7.0
SWIGLU_ALPHA = 1.702
MOE_BLOCK = 256
EPS = 1e-6


def rms_norm(x, g):
    xf = x.astype(jnp.float32)
    y = xf * lax.rsqrt(jnp.mean(xf * xf, axis=-1, keepdims=True) + EPS)
    return (y * g.astype(jnp.float32)).astype(x.dtype)

def causal_depthwise_conv(x, w, b):
    y = lax.conv_general_dilated(
        x, w[:, None, :].astype(x.dtype), window_strides=(1,),
        padding=[(CONV_WIDTH - 1, 0)], dimension_numbers=("NWC", "WIO", "NWC"),
        feature_group_count=x.shape[-1])
    return y + b

def rg_lru(x, w_a, b_a, w_x, b_x, lam):
    B, S, C = x.shape
    xf = x.astype(jnp.float32)
    xh = xf.reshape(B, S, LRU_BLOCKS, LRU_BLOCK_W)
    r = jax.nn.sigmoid(jnp.einsum("bshi,hij->bshj", xh, w_a.astype(jnp.float32)) + b_a).reshape(B, S, C)
    i = jax.nn.sigmoid(jnp.einsum("bshi,hij->bshj", xh, w_x.astype(jnp.float32)) + b_x).reshape(B, S, C)
    log_a = LRU_C * r * jax.nn.log_sigmoid(lam.astype(jnp.float32))
    a = jnp.exp(log_a)
    mult = jnp.sqrt(jnp.maximum(-jnp.expm1(2.0 * log_a), 0.0))
    u = mult * (i * xf)

    def combine(left, right):
        a1, b1 = left
        a2, b2 = right
        return a1 * a2, a2 * b1 + b2

    _, h = lax.associative_scan(combine, (a, u), axis=1)
    return h.astype(x.dtype)

def sliding_window_sink_attention(q, k, v, sinks):
    B, S = q.shape[0], q.shape[1]
    nblk = S // ATTN_BLOCK
    qb = q.reshape(B, nblk, ATTN_BLOCK, N_KV_HEADS, KV_GROUP, HEAD_DIM)

    def band(t):
        tp = jnp.pad(t, ((0, 0), (ATTN_BLOCK, 0), (0, 0), (0, 0)))
        prev = tp[:, :S].reshape(B, nblk, ATTN_BLOCK, N_KV_HEADS, HEAD_DIM)
        cur = t.reshape(B, nblk, ATTN_BLOCK, N_KV_HEADS, HEAD_DIM)
        return jnp.concatenate([prev, cur], axis=2)

    kw, vw = band(k), band(v)
    scores = jnp.einsum("bnqkgd,bnskd->bnkgqs", qb, kw).astype(jnp.float32) * (HEAD_DIM ** -0.5)
    qi = jnp.arange(ATTN_BLOCK)[:, None]
    sj = jnp.arange(2 * ATTN_BLOCK)[None, :]
    rel = qi + ATTN_BLOCK - sj
    key_pos = jnp.arange(nblk)[:, None, None] * ATTN_BLOCK - ATTN_BLOCK + sj[None]
    mask = ((rel >= 0) & (rel < WINDOW))[None] & (key_pos >= 0)
    scores = jnp.where(mask[None, :, None, None], scores, jnp.finfo(jnp.float32).min)
    sink = jnp.broadcast_to(sinks.astype(jnp.float32).reshape(1, 1, N_KV_HEADS, KV_GROUP, 1, 1),
                            scores.shape[:-1] + (1,))
    probs = jax.nn.softmax(jnp.concatenate([scores, sink], axis=-1), axis=-1)[..., :-1]
    out = jnp.einsum("bnkgqs,bnskd->bnqkgd", probs.astype(v.dtype), vw)
    return out.reshape(B, S, N_Q_HEADS * HEAD_DIM)

def parallel_mixer(h, w_in, conv_w, conv_b, w_rg_a, b_rg_a, w_rg_x, b_rg_x, lru_lambda,
                   sinks, g_attn_out, g_lru_out, w_out):
    B, S, _ = h.shape
    p = h @ w_in
    q, k, v, xr, xg = jnp.split(p, IN_SPLITS, axis=-1)
    attn = sliding_window_sink_attention(
        q.reshape(B, S, N_Q_HEADS, HEAD_DIM), k.reshape(B, S, N_KV_HEADS, HEAD_DIM),
        v.reshape(B, S, N_KV_HEADS, HEAD_DIM), sinks)
    xc = causal_depthwise_conv(xr, conv_w, conv_b)
    lru = rg_lru(xc, w_rg_a, b_rg_a, w_rg_x, b_rg_x, lru_lambda) * jax.nn.gelu(xg)
    merged = jnp.concatenate([rms_norm(attn, g_attn_out), rms_norm(lru, g_lru_out)], axis=-1)
    return merged @ w_out

def moe_ffn(h, w_router, b_router, w_gu, b_gu, w_down, b_down):
    B, S, D = h.shape
    T = B * S
    A = T * TOP_K
    R = ((A + N_EXPERTS * (MOE_BLOCK - 1) + MOE_BLOCK - 1) // MOE_BLOCK) * MOE_BLOCK
    nb = R // MOE_BLOCK
    hf = h.reshape(T, D)
    logits = (hf @ w_router + b_router).astype(jnp.float32)
    top_vals, top_idx = lax.top_k(logits, TOP_K)
    gates = jax.nn.softmax(top_vals, axis=-1)
    flat_e = top_idx.reshape(A).astype(jnp.int32)
    flat_tok = jnp.repeat(jnp.arange(T, dtype=jnp.int32), TOP_K)
    flat_w = gates.reshape(A)
    order = jnp.argsort(flat_e)
    se = flat_e[order]
    sizes = jnp.bincount(flat_e, length=N_EXPERTS)
    padded = ((sizes + MOE_BLOCK - 1) // MOE_BLOCK) * MOE_BLOCK
    pad_end = jnp.cumsum(padded)
    pad_start = pad_end - padded
    start = jnp.cumsum(sizes) - sizes
    dest = pad_start[se] + (jnp.arange(A, dtype=jnp.int32) - start[se])
    row_tok = jnp.zeros((R,), jnp.int32).at[dest].set(flat_tok[order])
    row_w = jnp.zeros((R,), jnp.float32).at[dest].set(flat_w[order])
    blk_e = jnp.minimum(jnp.searchsorted(pad_end, jnp.arange(nb) * MOE_BLOCK, side="right"),
                        N_EXPERTS - 1).astype(jnp.int32)
    xs = hf[row_tok].reshape(nb, MOE_BLOCK, D)

    def expert_block(args):
        xb, e = args
        gu = xb @ w_gu[e] + b_gu[e]
        gate = jnp.minimum(gu[:, :D_EXPERT], SWIGLU_LIMIT)
        up = jnp.clip(gu[:, D_EXPERT:], -SWIGLU_LIMIT, SWIGLU_LIMIT)
        glu = gate * jax.nn.sigmoid(SWIGLU_ALPHA * gate)
        return ((up + 1.0) * glu) @ w_down[e] + b_down[e]

    ys = lax.map(expert_block, (xs, blk_e)).reshape(R, D)
    ys = ys.astype(jnp.float32) * row_w[:, None]
    out = jax.ops.segment_sum(ys, row_tok, num_segments=T)
    return out.reshape(B, S, D).astype(h.dtype)

def second_inputs(seed: int = 0) -> dict:
    key = jax.random.key(seed)
    ks = jax.random.split(key, 26)
    L, D, E, F = DEPTH_2, D_MODEL, N_EXPERTS, D_EXPERT
    nrm = lambda k, shape, s: jax.random.normal(k, shape, jnp.float32) * s
    a0 = jax.random.uniform(ks[13], (L, LRU_WIDTH), jnp.float32, minval=0.9, maxval=0.999)
    root = a0 ** (1.0 / LRU_C)
    return {
        "x": nrm(ks[0], (BATCH, SEQ, D), 1.0),
        "c": nrm(ks[1], (BATCH, D), 1.0),
        "w_ada": nrm(ks[2], (L, D, 6 * D), 0.5 * D ** -0.5),
        "b_ada": nrm(ks[3], (L, 6 * D), 0.02),
        "g_mix": 1.0 + nrm(ks[4], (L, D), 0.05),
        "w_in": nrm(ks[5], (L, D, IN_COLS_2), D ** -0.5),
        "conv_w": nrm(ks[6], (L, CONV_WIDTH, LRU_WIDTH), CONV_WIDTH ** -0.5),
        "conv_b": nrm(ks[7], (L, LRU_WIDTH), 0.02),
        "w_rg_a": nrm(ks[8], (L, LRU_BLOCKS, LRU_BLOCK_W, LRU_BLOCK_W), LRU_BLOCK_W ** -0.5),
        "b_rg_a": nrm(ks[9], (L, LRU_BLOCKS, LRU_BLOCK_W), 0.02),
        "w_rg_x": nrm(ks[10], (L, LRU_BLOCKS, LRU_BLOCK_W, LRU_BLOCK_W), LRU_BLOCK_W ** -0.5),
        "b_rg_x": nrm(ks[11], (L, LRU_BLOCKS, LRU_BLOCK_W), 0.02),
        "lru_lambda": jnp.log(root) - jnp.log1p(-root),
        "sinks": nrm(ks[12], (L, N_Q_HEADS), 0.5),
        "g_attn_out": 1.0 + nrm(ks[14], (L, ATTN_WIDTH), 0.05),
        "g_lru_out": 1.0 + nrm(ks[15], (L, LRU_WIDTH), 0.05),
        "w_out": nrm(ks[16], (L, MIX_WIDTH, D), MIX_WIDTH ** -0.5),
        "g_ffn": 1.0 + nrm(ks[17], (L, D), 0.05),
        "w_router": nrm(ks[18], (L, D, E), D ** -0.5),
        "b_router": nrm(ks[19], (L, E), 0.01),
        "w_gu": nrm(ks[20], (L, E, D, 2 * F), D ** -0.5),
        "b_gu": nrm(ks[21], (L, E, 2 * F), 0.02),
        "w_down": nrm(ks[22], (L, E, F, D), F ** -0.5),
        "b_down": nrm(ks[23], (L, E, D), 0.02),
        "g_final": 1.0 + nrm(ks[24], (D,), 0.05),
    }

def second_block(x, c, w_ada, b_ada, g_mix, w_in, conv_w, conv_b, w_rg_a, b_rg_a, w_rg_x, b_rg_x,
              lru_lambda, sinks, g_attn_out, g_lru_out, w_out, g_ffn, w_router, b_router,
              w_gu, b_gu, w_down, b_down, g_final):
    for l in range(DEPTH_2):
        mod = (c @ w_ada[l] + b_ada[l])[:, None, :]
        sh1, sc1, gt1, sh2, sc2, gt2 = jnp.split(mod, 6, axis=-1)
        h = rms_norm(x, g_mix[l]) * (1.0 + sc1) + sh1
        x = x + gt1 * parallel_mixer(h, w_in[l], conv_w[l], conv_b[l], w_rg_a[l], b_rg_a[l],
                                     w_rg_x[l], b_rg_x[l], lru_lambda[l], sinks[l],
                                     g_attn_out[l], g_lru_out[l], w_out[l])
        h = rms_norm(x, g_ffn[l]) * (1.0 + sc2) + sh2
        x = x + gt2 * moe_ffn(h, w_router[l], b_router[l], w_gu[l], b_gu[l], w_down[l], b_down[l])
    return rms_norm(x, g_final)


def setup_inputs(seed=0):
    out = dict(first_inputs(seed))
    for name, value in second_inputs(seed + 1).items():
        if name != "x":
            out[name + "_2"] = value
    return out


def reference(
    x, w_in, w_in_vres, gla_w_a2, gla_b_a, gla_ln_w, gla_ln_b, rwkv_mu, rwkv_mu_vres, rwkv_w0,
    rwkv_w2, rwkv_a0, rwkv_a2, rwkv_v0, rwkv_v2, rwkv_g2, rwkv_k_k, rwkv_k_a, rwkv_r_k,
    rwkv_ln_w, rwkv_ln_b, nsa_pos_k, nsa_pos_v, nsa_wk1, nsa_wk2, nsa_wv1, nsa_wv2, w_out,
    ln1_w, ln1_b, ffn_w_gate, ffn_w_up, ffn_w_down, ln2_w, ln2_b, c_2, w_ada_2, b_ada_2,
    g_mix_2, w_in_2, conv_w_2, conv_b_2, w_rg_a_2, b_rg_a_2, w_rg_x_2, b_rg_x_2, lru_lambda_2,
    sinks_2, g_attn_out_2, g_lru_out_2, w_out_2, g_ffn_2, w_router_2, b_router_2, w_gu_2,
    b_gu_2, w_down_2, b_down_2, g_final_2,
):
    x = first_block(
        x, w_in, w_in_vres, gla_w_a2, gla_b_a, gla_ln_w, gla_ln_b, rwkv_mu, rwkv_mu_vres,
        rwkv_w0, rwkv_w2, rwkv_a0, rwkv_a2, rwkv_v0, rwkv_v2, rwkv_g2, rwkv_k_k, rwkv_k_a,
        rwkv_r_k, rwkv_ln_w, rwkv_ln_b, nsa_pos_k, nsa_pos_v, nsa_wk1, nsa_wk2, nsa_wv1,
        nsa_wv2, w_out, ln1_w, ln1_b, ffn_w_gate, ffn_w_up, ffn_w_down, ln2_w, ln2_b,
    )
    return second_block(
        x, c_2, w_ada_2, b_ada_2, g_mix_2, w_in_2, conv_w_2, conv_b_2, w_rg_a_2, b_rg_a_2,
        w_rg_x_2, b_rg_x_2, lru_lambda_2, sinks_2, g_attn_out_2, g_lru_out_2, w_out_2, g_ffn_2,
        w_router_2, b_router_2, w_gu_2, b_gu_2, w_down_2, b_down_2, g_final_2,
    )


_drawn_inputs = setup_inputs


def setup_inputs(seed=0):
    import zlib

    import numpy as np

    out = dict(_drawn_inputs(seed))
    spreads = {}
    factors = {'gla_b_a': 3.488,
     'gla_ln_w': 3.44,
     'gla_ln_b': 5.336,
     'rwkv_w2': 3.671,
     'rwkv_a0': 4.145,
     'rwkv_v0': 4.907,
     'rwkv_k_k': 3.708,
     'rwkv_k_a': 3.529,
     'rwkv_ln_w': 2.919,
     'rwkv_ln_b': 4.886,
     'nsa_pos_k': 38.733,
     'nsa_pos_v': 8.0,
     'b_rg_a_2': 24.587,
     'b_rg_x_2': 6.806,
     'sinks_2': 6.31,
     'b_router_2': 3.296,
     'b_gu_2': 8.0,
     'b_down_2': 8.0}
    for name, (base, spread) in spreads.items():
        noise = np.random.default_rng([zlib.crc32(name.encode()), seed]).standard_normal(out[name].shape)
        drawn = base * np.exp(spread * noise) if base else spread * noise
        out[name] = jnp.asarray(drawn.astype(out[name].dtype))
    for name, factor in factors.items():
        out[name] = (out[name] * factor).astype(out[name].dtype)
    return out
```

```python
from contextlib import ExitStack

import numpy as np

import concourse.bass as bass
from concourse import mybir

F32 = mybir.dt.float32
I32 = mybir.dt.int32
ALU = mybir.AluOpType
ACT = mybir.ActivationFunctionType
AX = mybir.AxisListType

P = 128
T = 256
NT = T // P
D = 1024
KT = D // P
DEPTH = 2
HD = 64
FFN = 2816
NF = FFN // P
ALPHA = float((2 * DEPTH) ** 0.25)
LN_EPS, RWKV_EPS, RMS_EPS = 1e-5, 64e-5, 1e-6
MASK_NEG = -1e30
DECAY = -float(np.exp(np.float32(-0.5)))
GLA_TAU = 16.0
QC = 32
NQC = T // QC
EXP_CAP = 1e17
NE, TOPK = 32, 4
DE = 1024
SLOTS_E = 64
MAX_OVER = 16
NITEM = NE + MAX_OVER
LIMIT, SWIGLU_ALPHA = 7.0, 1.702
LRU_C = 8.0
GELU_C, GELU_K = 0.7978845608028654, 0.044715

SLOT = 4096
RING = 4
S_IN, S_CMP, S_WO, S_GU, S_DN = 0, 7, 9, 11, 22
LAYER_SLOTS = 28
S_ADA = DEPTH * LAYER_SLOTS
S_IN2 = S_ADA + 12
S_WO2 = S_IN2 + 4
S_MOE = S_WO2 + 2
ITEM_SLOTS = 6
N_SLOTS = S_MOE + ITEM_SLOTS * NE
assert (2 * ITEM_SLOTS) % RING == 0

T_GQ, T_GK, T_R, T_K, T_V, T_WA, T_G1, T_MISC, T_VC, T_KC, T_KS, T_KW, T_Q = 0, 2, 4, 6, 8, 10, 11, 12, 13, 14, 15, 16, 17
NCT = 21
M_G2, M_VR, M_GA = 0, 32, 64


def layout(fields):
    at, offsets = 0, {}
    for name, width in fields:
        offsets[name] = (at, at + width)
        at += width
    return offsets, at


LAYER_FIELDS, LAYER_COLS = layout([
    ("mu", 9), ("b_a", 2), ("w0", 2), ("a0", 2), ("v0", 2), ("k_k", 2), ("k_a", 2), ("r_k", 8),
    ("wa", 256), ("g2", 256), ("misc", 256), ("wk2", 128), ("wv2", 128), ("pos_k", 32), ("pos_v", 32)])
SECOND_FIELDS, SECOND_COLS = layout([
    ("c", 8), ("conv_w", 16), ("conv_b", 4), ("rg_a", 512), ("rg_x", 512), ("b_a", 4), ("b_x", 4), ("lam", 4),
    ("g_attn", 4), ("g_lru", 4), ("router", 8 * NE)])
CONST_FIELDS, CONST_COLS = layout([
    ("ident", P), ("diag_add", P), ("prev_add", P), ("pairs", 4 * P), ("levels", 7 * P), ("ones", T),
    ("head_ones", P), ("rot", P), ("cos", T), ("sin", T), ("iota", P), ("cmp_add", 30), ("cmp_any", 2)])


def constants():
    f = np.float32
    c = {}
    i, j = np.arange(P)[:, None], np.arange(P)[None, :]
    c["ident"] = (i == j).astype(f)
    c["diag_add"] = np.where(j <= i, 0, MASK_NEG).astype(f)
    c["prev_add"] = np.where(j > i, 0, MASK_NEG).astype(f)
    strict, incl = (i < j).astype(f), (i <= j).astype(f)
    c["pairs"] = np.concatenate([strict, incl, strict, incl], 1)
    level = []
    for n in range(7):
        b = 1 << n
        level.append(((i // (2 * b) == j // (2 * b)) & (i // b % 2 == 0) & (j // b % 2 == 1)).astype(f))
    c["levels"] = np.concatenate(level, 1)
    c["ones"] = np.ones((P, T), f)
    c["head_ones"] = (i // HD == j // HD).astype(f)
    half = HD // 2
    rot = np.zeros((P, P), f)
    for m in range(P):
        if m % HD < half:
            rot[m + half, m] = -1
        else:
            rot[m - half, m] = 1
    c["rot"] = rot
    inv = (f(10000.0) ** (-np.arange(half, dtype=f) / f(half))).astype(f)
    ang = (np.arange(T, dtype=f)[:, None] * inv).astype(f)
    row = np.arange(P) % half
    c["cos"], c["sin"] = np.cos(ang).astype(f).T[row], np.sin(ang).astype(f).T[row]
    c["iota"] = np.broadcast_to(np.arange(P, dtype=f), (P, P))
    pos = np.arange(P)[:, None, None] + P * np.arange(NT)[None, :, None]
    seen = 16 * np.arange(15)[None, None, :] + 31 <= pos
    c["cmp_add"] = np.where(seen, 0, MASK_NEG).astype(f).reshape(P, 30)
    c["cmp_any"] = seen.any(-1).astype(f)
    out = np.zeros((P, CONST_COLS), f)
    for name, (a, b) in CONST_FIELDS.items():
        out[:, a:b] = c[name]
    return out


def program(nc, dram):
    ctx = ExitStack()
    with ctx:
        def sb(name, shape, dt=F32):
            return ctx.enter_context(nc.sbuf_tensor(name, shape, dt))

        sems = {}

        def S(name):
            if name not in sems:
                sems[name] = ctx.enter_context(nc.semaphore(name))
            return sems[name]

        ring = sb("ring", [P, RING, SLOT])
        X = sb("X", [P, NT, D])
        XT = sb("XT", [P, KT, T])
        OT = XT
        HT = sb("HT", [P, NF, T])
        TOK = sb("TOK", [P, NT, 512])
        NV = sb("NV", [P, NT, 280])
        CST = sb("CST", [P, CONST_COLS])
        PAR = sb("PAR", [P, max(LAYER_COLS, SECOND_COLS)])
        HN = sb("HN", [P, 4, 256])
        VF = sb("VF", [P, 2, T])
        SA = sb("SA", [P, 5120])
        SB = sb("SB", [P, 14336])
        SM = sb("SM", [P, 176])
        ps = ctx.enter_context(nc.psum_tensor("ps", [P, 8, 512], F32))

        ITI = SA[:, 5056:5056 + 8 + NITEM].bitcast(I32)

        def cst(name):
            a, b = CONST_FIELDS[name]
            return CST[:, a:b]

        def par(name, fields=LAYER_FIELDS):
            a, b = fields[name]
            return PAR[:, a:b]

        def par2(name):
            return par(name, SECOND_FIELDS)

        def view(region, at, shape):
            n = int(np.prod(shape))
            v = region[:, at:at + n]
            if len(shape) == 2:
                v = v.rearrange("p (a b) -> p a b", a=shape[0])
            elif len(shape) == 3:
                v = v.rearrange("p (a b c) -> p a b c", a=shape[0], b=shape[1])
            elif len(shape) == 4:
                v = v.rearrange("p (a b c d) -> p a b c d", a=shape[0], b=shape[1], c=shape[2])
            return v

        def bank(b, n=1):
            return ps[:, b:b + n, :].rearrange("p a n -> p (a n)")

        ident = cst("ident")
        LNW, LNB = view(SB, 0, [D]), view(SB, D, [D])
        SQ = view(SB, 2 * D, [D])
        arrived = [S(f"slot_arrived{b}") for b in range(RING)]

        def slot(i):
            return ring[:, i % RING, :]

        def need_slot(eng, i):
            eng.wait_ge(arrived[i % RING], 16 * (i // RING + 1))

        def released(i):
            if i < S_ADA:
                l, s = divmod(i, LAYER_SLOTS)
                if s < S_CMP:
                    return "proj_ready", 15 * l + [2, 4, 6, 8, 10, 13, 15][s]
                if s < S_WO:
                    return "cmp_hidden", 2 * l + s - S_CMP + 1
                if s < S_GU:
                    return "mix_ready", 2 * l + s - S_WO + 1
                if s < S_DN:
                    return "ffn_ready", 11 * l + s - S_GU + 1
                return "down_ready", 6 * l + s - S_DN + 1
            if i < S_IN2:
                return "mod_ready", i - S_ADA + 1
            if i < S_WO2:
                return "proj2_ready", [2, 4, 6, 8][i - S_IN2]
            return "mix2_ready", i - S_WO2 + 1

        def link(eng, name):
            n = [0]

            def step(ins):
                n[0] += 1
                ins.then_inc(S(name), 1)

            def joined(ins):
                step(ins)
                eng.wait_ge(S(name), n[0])
            return step, joined

        def stream(sp, i):
            if i >= RING:
                name, value = released(i - RING)
                sp.wait_ge(S(name), value)
            sp.dma_start(slot(i), dram["stream"][i]).then_inc(arrived[i % RING], 16)

        def layer_params(sp, l):
            if l:
                for done in ("gla_out", "rw_out", "nsa_out"):
                    sp.wait_ge(S(done), l)
            sp.dma_start(PAR[:, 0:LAYER_COLS], dram["layer"][l]).then_inc(S("par_loaded"), 16)
            sp.dma_start(HN[:].rearrange("p a b -> p (a b)"),
                         dram["head_norm"][l:l + 1, :].broadcast_to([P, 1024])).then_inc(S("hn_loaded"), 16)

        def norm_params(sp, n):
            if n % 2:
                sp.wait_ge(S("x_ready"), n)
            else:
                sp.wait_ge(S("mix_ready"), n + 1)
            sp.dma_start(LNW, dram["ln"][2 * n:2 * n + 1, :].broadcast_to([P, D])).then_inc(S("ln_loaded"), 16)
            sp.dma_start(LNB, dram["ln"][2 * n + 1:2 * n + 2, :].broadcast_to([P, D])).then_inc(S("ln_loaded"), 16)

        def first_sp(sp):
            sp.dma_start(X[:], dram["x"].rearrange("(t p) d -> p t d", p=P)).then_inc(S("x_loaded"), 16)
            sp.dma_start(CST[:], dram["const"]).then_inc(S("const_loaded"), 16)
            for l in range(DEPTH):
                for s in range(LAYER_SLOTS):
                    stream(sp, l * LAYER_SLOTS + s)
                    if l == 0 and s == 1:
                        layer_params(sp, 0)
                    if s == S_WO + RING:
                        norm_params(sp, 2 * l)
                    if s == S_GU + 8:
                        norm_params(sp, 2 * l + 1)
                        if l + 1 < DEPTH:
                            layer_params(sp, l + 1)

        def transpose_x_pe(pe, n, src, ready):
            pe.wait_ge(S(ready[0]), ready[1])
            for b in range(4):
                for k in range(2):
                    for t in range(NT):
                        m = pe.transpose(ps[:, 4 + b, (k * NT + t) * P:(k * NT + t + 1) * P],
                                         src[:, t, (2 * b + k) * P:(2 * b + k + 1) * P], ident)
                m.then_inc(S("xt_ps"), 1)

        def transpose_x_dve(v, n):
            for b in range(4):
                v.wait_ge(S("xt_ps"), 4 * n + b + 1)
                nc.vector.tensor_copy(XT[:, 2 * b:2 * b + 2, :].rearrange("p k t -> p (k t)"),
                                      ps[:, 4 + b, :]).then_inc(S("xt_ready"), 1)

        def project_pe(pe, l):
            base = l * LAYER_SLOTS
            pe.wait_ge(S("xt_ready"), 4 * (2 * l + 1))
            g = 0
            for s in range(7):
                need_slot(pe, base + s)
                w = slot(base + s).rearrange("p (k n) -> p k n", k=KT)
                if s < 5:
                    for q in range(2):
                        if g >= 4:
                            pe.wait_ge(S("proj_evac"), 15 * l + g - 3)
                        for j in range(2):
                            for k in range(KT):
                                m = pe.matmul(ps[:, g % 4, j * T:(j + 1) * T],
                                              w[:, k, (2 * q + j) * P:(2 * q + j + 1) * P],
                                              XT[:, k, :], start=k == 0, stop=k == KT - 1)
                        m.then_inc(S("proj_ready"), 1)
                        g += 1
                    continue
                if s == 5:
                    pe.wait_ge(S("proj_evac"), 15 * l + g - 3)
                    for k in range(KT):
                        m = pe.matmul(ps[:, g % 4, 0:T], w[:, k, 0:P], XT[:, k, :], start=k == 0, stop=k == KT - 1)
                    m.then_inc(S("proj_ready"), 1)
                    g += 1
                a, n = (P, 280) if s == 5 else (0, 512)
                for t in range(NT):
                    pe.wait_ge(S("proj_evac"), 15 * l + g - 3)
                    for k in range(KT):
                        m = pe.matmul(ps[:, g % 4, 0:n], XT[:, k, t * P:(t + 1) * P], w[:, k, a:a + n],
                                      start=k == 0, stop=k == KT - 1)
                    m.then_inc(S("proj_ready"), 1)
                    g += 1

        def project_act(act, l):
            for g in range(15):
                act.wait_ge(S("proj_ready"), 15 * l + g + 1)
                if g < 10:
                    to, n = HT[:, 2 * g:2 * g + 2, :].rearrange("p a t -> p (a t)"), 512
                elif g == 10:
                    to, n = HT[:, 20, :], T
                elif g < 13:
                    to, n = NV[:, g - 11, :], 280
                else:
                    to, n = TOK[:, g - 13, :], 512
                nc.scalar.activation(to, ps[:, g % 4, 0:n], ACT.Copy,
                                     scale=HD ** -0.5 if g == 0 else 1.0).then_inc(S("proj_evac"), 1)

        def mix_dve(v, l, I, L):
            v.wait_ge(S("proj_evac"), 15 * l + 7)
            v.wait_ge(S("par_loaded"), 16 * (l + 1))
            HX = HT[:, T_R:T_MISC + 1, :]
            MD = view(SB, 0, [9, T])
            I(nc.vector.tensor_tensor(MD[:, :, 1:T], HX[:, :, 0:T - 1], HX[:, :, 1:T], ALU.subtract))
            L(nc.vector.tensor_scalar(MD[:, :, 0:1], HX[:, :, 0:1], -1.0, None, ALU.mult))
            for j in range(9):
                ins = nc.vector.scalar_tensor_tensor(out=HX[:, j, :], in0=MD[:, j, :], scalar=par("mu")[:, j:j + 1],
                                                     in1=HX[:, j, :], op0=ALU.mult, op1=ALU.add)
                if j < 8:
                    I(ins)
            ins.then_inc(S("mixed"), 1)
            v.wait_ge(S("mixed"), l + 1)

        def head_norm_dve(v, I, L, src, eps, which, n, XC, SQ2):
            s8, v8, d8, r8 = (SM[:, 8 * i:8 * i + 8] for i in range(4))
            X8 = XC.rearrange("p (a b) -> p a b", b=HD)
            L(nc.vector.tensor_reduce(s8, src, AX.X, ALU.add))
            L(nc.vector.tensor_scalar(s8, s8, 1.0 / HD, None, ALU.mult))
            L(nc.vector.tensor_tensor(X8, src, s8.unsqueeze(2).broadcast_to([P, 8, HD]), ALU.subtract))
            L(nc.vector.tensor_tensor(SQ2, XC, XC, ALU.mult))
            L(nc.vector.tensor_reduce(v8, SQ2.rearrange("p (a b) -> p a b", b=HD), AX.X, ALU.add))
            nc.vector.tensor_scalar(v8, v8, 1.0 / HD, eps, ALU.mult, ALU.add).then_inc(S("head_var"), 1)
            v.wait_ge(S("head_std"), n + 1)
            L(nc.vector.reciprocal(r8, d8))
            L(nc.vector.tensor_tensor(X8, X8, r8.unsqueeze(2).broadcast_to([P, 8, HD]), ALU.mult))
            X2 = XC.rearrange("p (t c) -> p t c", t=NT)
            v.wait_ge(S("hn_loaded"), 16 * (n // 2 + 1))
            L(nc.vector.tensor_tensor(X2, X2, HN[:, which:which + 1, :].broadcast_to([P, NT, 256]), ALU.mult))
            L(nc.vector.tensor_tensor(X2, X2, HN[:, which + 1:which + 2, :].broadcast_to([P, NT, 256]), ALU.add))

        def head_norm_act(act, n):
            act.wait_ge(S("head_var"), n + 1)
            nc.scalar.activation(SM[:, 16:24], SM[:, 8:16], ACT.Sqrt).then_inc(S("head_std"), 1)

        G_LB, G_T0, G_T1 = view(SA, 0, [2, T]), view(SA, 512, [2, T]), view(SA, 1024, [2, T])
        G_EK = [view(SA, 1536 + 512 * i, [2, T]) for i in range(2)]
        G_KH = [view(SA, 2560 + 512 * i, [2, T]) for i in range(2)]
        G_ST = view(SA, 3584, [4, 384])

        def gla_gate_pe(pe, l):
            pe.wait_ge(S("mixed"), l + 1)
            pe.wait_ge(S("proj_evac"), 15 * (l + 1))
            for c in range(2):
                m = pe.matmul(ps[:, 4, c * T:(c + 1) * T], par("misc")[M_GA:M_GA + 16, c * P:(c + 1) * P],
                              HT[M_GA:M_GA + 16, T_MISC, :], start=True, stop=True)
            m.then_inc(S("gla_z"), 1)

        def gla_scores_pe(pe, l):
            for tc in range(NQC):
                pe.wait_ge(S("gla_k"), NQC * l + tc + 1)
                if tc == 0:
                    pe.wait_ge(S("gla_q"), l + 1)
                    if l:
                        pe.wait_ge(S("rw_sv"), l)
                for h in range(4):
                    c, pb = h // 2, HD * (h % 2)
                    for st in range(tc * QC // P + 1):
                        at = tc * QC if st == 0 else T + tc * QC - P
                        m = pe.matmul(ps[:, h, at:at + QC], G_KH[tc % 2][pb:pb + HD, c, st * P:(st + 1) * P],
                                      HT[pb:pb + HD, T_GQ + c, tc * QC:(tc + 1) * QC], start=True, stop=True)
                m.then_inc(S("gla_sc"), 1)

        def gla_out_pe(pe, l):
            pe.wait_ge(S("gla_st"), 3 * (l + 1))
            for t in range(NT):
                for h in range(4):
                    for s in range(t + 1):
                        at = t * P if s == 0 else T
                        m = pe.matmul(ps[:, 4, (4 * t + h) * HD:(4 * t + h + 1) * HD], G_ST[:, h, at:at + P],
                                      TOK[:, s, h * HD:(h + 1) * HD], start=s == 0, stop=s == t)
            m.then_inc(S("gla_o"), 1)

        def back_pe(pe, n, XC, b):
            pe.wait_ge(S("head_out"), n + 1)
            X2 = XC.rearrange("p (t c) -> p t c", t=NT)
            for c in range(2):
                for t in range(NT):
                    m = pe.transpose(ps[:, b, c * T + t * P:c * T + (t + 1) * P], X2[:, t, c * P:(c + 1) * P], ident)
            m.then_inc(S("back_ps"), 1)

        def gla_act(act, l, I, L):
            act.wait_ge(S("gla_zb"), l + 1)
            L(nc.scalar.activation(G_T0, G_T1, ACT.Abs))
            L(nc.scalar.activation(G_T0, G_T0, ACT.Exp, scale=-1.0))
            nc.scalar.activation(G_T0, G_T0, ACT.Ln, bias=cst("ones")[:, 0:1]).then_inc(S("gla_lp"), 1)
            act.wait_ge(S("gla_df"), l + 1)
            nc.scalar.activation(G_T0, G_T1, ACT.Exp).then_inc(S("gla_eq"), 1)
            for tc in range(NQC):
                if tc >= 2:
                    act.wait_ge(S("gla_k"), NQC * l + tc - 1)
                w, ref = (tc * QC // P + 1) * P, tc * QC + QC // 2 - 1
                for c in range(2):
                    nc.scalar.activation(G_EK[tc % 2][:, c, 0:w], G_LB[:, c, 0:w], ACT.Exp, scale=-1.0,
                                         bias=G_LB[:, c, ref:ref + 1]).then_inc(S("gla_ek"), 1)

        def gla_dve(v, l, I, L):
            v.wait_ge(S("gla_z"), l + 1)
            for c in range(2):
                ins = nc.vector.tensor_scalar(G_T1[:, c, :], ps[:, 4, c * T:(c + 1) * T], par("b_a")[:, c:c + 1], None, ALU.add)
                if c == 0:
                    I(ins)
            ins.then_inc(S("gla_zb"), 1)
            v.wait_ge(S("gla_zb"), l + 1)
            v.wait_ge(S("gla_lp"), l + 1)
            L(nc.vector.scalar_tensor_tensor(out=G_T1, in0=G_T1, scalar=0.0, in1=G_T0, op0=ALU.min, op1=ALU.subtract))
            for c in range(2):
                (I if c == 0 else L)(nc.vector.tensor_tensor_scan(G_LB[:, c, :], cst("ones"), G_T1[:, c, :], 0.0,
                                                                  ALU.mult, ALU.add))
            L(nc.vector.tensor_scalar(G_LB, G_LB, 1.0 / GLA_TAU, None, ALU.mult))
            lb4 = G_LB.rearrange("p c (n q) -> p (c n) q", q=QC)
            t14 = G_T1.rearrange("p c (n q) -> p (c n) q", q=QC)
            nc.vector.tensor_tensor(t14, lb4, lb4[:, :, QC // 2 - 1:QC // 2].broadcast_to([P, 2 * NQC, QC]),
                                    ALU.subtract).then_inc(S("gla_df"), 1)
            v.wait_ge(S("gla_eq"), l + 1)
            q = HT[:, T_GQ:T_GQ + 2, :]
            nc.vector.scalar_tensor_tensor(out=q, in0=G_T0, scalar=EXP_CAP, in1=q, op0=ALU.min,
                                           op1=ALU.mult).then_inc(S("gla_q"), 1)
            for tc in range(NQC):
                v.wait_ge(S("gla_ek"), 2 * NQC * l + 2 * tc + 2)
                if tc >= 2:
                    v.wait_ge(S("gla_sc"), NQC * l + tc - 1)
                w = (tc * QC // P + 1) * P
                nc.vector.scalar_tensor_tensor(out=G_KH[tc % 2][:, :, 0:w], in0=G_EK[tc % 2][:, :, 0:w], scalar=EXP_CAP,
                                               in1=HT[:, T_GK:T_GK + 2, 0:w], op0=ALU.min,
                                               op1=ALU.mult).then_inc(S("gla_k"), 1)
            v.wait_ge(S("gla_sc"), NQC * (l + 1))
            incl = cst("pairs")[:, P:2 * P].unsqueeze(1).broadcast_to([P, 4, P])
            nc.vector.tensor_tensor(G_ST[:, :, 0:P], ps[:, 0:4, 0:P], incl, ALU.mult).then_inc(S("gla_st"), 1)
            nc.vector.tensor_copy(G_ST[:, :, P:T], ps[:, 0:4, P:T]).then_inc(S("gla_st"), 1)
            nc.vector.tensor_tensor(G_ST[:, :, T:T + P], ps[:, 0:4, T:T + P], incl, ALU.mult).then_inc(S("gla_st"), 1)

        G_XC, G_SQ, G_SG = view(SA, 1536, [512]), view(SA, 2048, [512]), view(SA, 512, [512])

        def gla_norm_dve(v, l, I, L):
            v.wait_ge(S("gla_o"), l + 1)
            head_norm_dve(v, I, L, ps[:, 4, :].rearrange("p (a b) -> p a b", b=HD), LN_EPS, 0, 2 * l, G_XC, G_SQ)
            v.wait_ge(S("gla_sg"), l + 1)
            sg, xc = (a.rearrange("p (t c) -> p t c", t=NT) for a in (G_SG, G_XC))
            L(nc.vector.tensor_tensor(sg, sg, TOK[:, :, 256:512], ALU.mult))
            nc.vector.tensor_tensor(xc, xc, sg, ALU.mult).then_inc(S("head_out"), 1)

        def gla_end_act(act, l):
            act.wait_ge(S("gla_st"), 3 * (l + 1))
            nc.scalar.activation(G_SG.rearrange("p (t c) -> p t c", t=NT), TOK[:, :, 256:512],
                                 ACT.Sigmoid).then_inc(S("gla_sg"), 1)
            head_norm_act(act, 2 * l)

        MM = view(SB, 0, [8, 4, P])
        TM, TT = view(SB, 4096, [8, P]), view(SB, 5120, [8, P])
        ZM, MK = view(SB, 6144, [8, P]), view(SB, 7168, [8, P])
        E1, E2, E3 = (view(SB, 6144 + 512 * i, [2, T]) for i in range(3))
        DM, DM1 = view(SB, 4096, [2, T]), view(SB, 4608, [2, T])
        LW, AA, KK = (view(SB, 8192 + 512 * i, [2, T]) for i in range(3))
        XU, US = view(SB, 8704, [256]), view(SB, 8960, [256])
        RK = view(SB, 9216, [2, T])
        AR = view(SB, 9728, [2, 2, 2, P])
        BT, KTL = view(SB, 10752, [2, T]), view(SB, 11264, [2, T])
        SV = view(SB, 11776, [2, T])
        BK = view(SB, 11776, [2, 256])
        VT, GT = view(SB, 12288, [2, 256]), view(SB, 12800, [2, 256])
        S0 = view(SB, 13440, [2, 2, HD])
        LC = view(SB, 13440, [2, T])
        SCL = SM[:, 40:42]
        R_XC, R_SQ = view(SB, 9728, [512]), view(SB, 10240, [512])

        def rwkv_ranks_act(act, l, I):
            act.wait_ge(S("mixed"), l + 1)
            I(nc.scalar.activation(HT[0:64, T_WA, :], HT[0:64, T_WA, :], ACT.Tanh))
            I(nc.scalar.activation(HT[:, T_G1, :], HT[:, T_G1, :], ACT.Sigmoid))
            nc.scalar.activation(HT[0:32, T_MISC, :], HT[0:32, T_MISC, :], ACT.Sigmoid).then_inc(S("rw_rank"), 1)

        def rwkv_ranks_pe(pe, l):
            pe.wait_ge(S("rw_rank"), l + 1)
            for b, r0 in ((6, 0), (7, 64)):
                for c in range(2):
                    pe.matmul(ps[:, b, c * T:(c + 1) * T], par("wa")[r0:r0 + 64, c * P:(c + 1) * P],
                              HT[r0:r0 + 64, T_WA, :], start=True, stop=True)
            if l:
                for c in range(2):
                    pe.matmul(ps[:, 0, c * T:(c + 1) * T], par("misc")[M_VR:M_VR + 32, c * P:(c + 1) * P],
                              HT[M_VR:M_VR + 32, T_MISC, :], start=True, stop=True)
            for t in range(NT):
                pe.matmul(ps[:, 5, t * T:(t + 1) * T], HT[:, T_G1, t * P:(t + 1) * P], par("g2"), start=True, stop=False)
                m = pe.matmul(ps[:, 5, t * T:(t + 1) * T], HT[0:32, T_MISC, t * P:(t + 1) * P], par("misc")[0:32, :],
                              start=False, stop=True)
            m.then_inc(S("rw_z"), 1)

        def rwkv_gates_act(act, l, I):
            act.wait_ge(S("rw_z"), l + 1)
            for b, to, bias in ((6, LW, "w0"), (7, AA, "a0")) + (((0, SV, "v0"),) if l else ()):
                for c in range(2):
                    ins = nc.scalar.activation(to[:, c, :], ps[:, b, c * T:(c + 1) * T], ACT.Sigmoid,
                                               bias=par(bias)[:, c:c + 1])
                    if to is SV and c:
                        ins.then_inc(S("rw_sv"), 1)
                    else:
                        I(ins)
            nc.scalar.activation(GT, ps[:, 5, :].rearrange("p (t c) -> p t c", t=NT), ACT.Copy).then_inc(S("rw_gates"), 1)

        def rwkv_prepare_dve(v, l, I, L):
            HK, HR, HV = HT[:, T_K:T_K + 2, :], HT[:, T_R:T_R + 2, :], HT[:, T_V:T_V + 2, :]
            for c in range(2):
                (I if c == 0 else L)(nc.vector.tensor_scalar(KK[:, c, :], HK[:, c, :], par("k_k")[:, c:c + 1], None, ALU.mult))
            nc.vector.tensor_tensor(RK_SQ, KK, KK, ALU.mult).then_inc(S("rw_sq"), 1)
            v.wait_ge(S("rw_gates"), l + 1)
            if l == 0:
                nc.vector.tensor_copy(VF[:], HV).then_inc(S("rw_v"), 1)
            else:
                L(nc.vector.tensor_tensor(DM, VF[:], HV, ALU.subtract))
                L(nc.vector.tensor_tensor(DM, DM, SV, ALU.mult))
                nc.vector.tensor_tensor(HV, HV, DM, ALU.add).then_inc(S("rw_v"), 1)
                v.wait_ge(S("rw_v"), l + 1)
            for c in range(2):
                (I if c == 0 else L)(nc.vector.tensor_scalar(DM1[:, c, :], AA[:, c, :], 1.0, par("k_a")[:, c:c + 1],
                                                             ALU.subtract, ALU.mult))
            L(nc.vector.scalar_tensor_tensor(out=HK, in0=DM1, scalar=1.0, in1=HK, op0=ALU.add, op1=ALU.mult))
            for c in range(2):
                for j in range(2):
                    L(nc.vector.tensor_tensor_scan(LC[:, c, j * P:(j + 1) * P], cst("ones")[:, 0:P],
                                                   LW[:, c, j * P:(j + 1) * P], 0.0, ALU.mult, ALU.add))
            lc4, dm4 = (a.rearrange("p c (j s) -> p (c j) s", j=2) for a in (LC, DM))
            L(nc.vector.tensor_tensor(dm4, lc4, lc4[:, :, 63:64].broadcast_to([P, 4, P]), ALU.subtract))
            I(nc.vector.tensor_tensor(SCL.unsqueeze(2), DM[:, :, 127:128], LC[:, :, P + 63:P + 64], ALU.add))
            nc.vector.tensor_tensor(DM1, DM, LW, ALU.subtract).then_inc(S("rw_dm"), 1)
            v.wait_ge(S("rw_ss"), l + 1)
            nc.vector.tensor_scalar(RK_SQ.rearrange("p c t -> p (c t)"), ps[:, 6, :], 1e-24, None,
                                    ALU.max).then_inc(S("rw_ssm"), 1)
            v.wait_ge(S("rw_norm"), l + 1)
            L(nc.vector.reciprocal(RK_SQ, RK_SQ))
            L(nc.vector.tensor_tensor(KK, KK, RK_SQ, ALU.mult))
            ar = AR.rearrange("p c j w s -> p (c j) w s")
            f4 = lambda a: a.rearrange("p c (j s) -> p (c j) s", j=2)
            I(nc.vector.scalar_tensor_tensor(out=ar[:, :, 0, :], in0=f4(KK), scalar=-1.0, in1=f4(E3), op0=ALU.mult, op1=ALU.mult))
            I(nc.vector.tensor_tensor(ar[:, :, 1, :], f4(HR), f4(E1), ALU.mult))
            L(nc.vector.tensor_tensor(BT, KK, AA, ALU.mult))
            I(nc.vector.tensor_tensor(BT, BT, E2, ALU.mult))
            I(nc.vector.tensor_tensor(RK, HR, HK, ALU.mult))
            nc.vector.tensor_tensor(KTL, HK, E2, ALU.mult).then_inc(S("rw_ops"), 1)

        RK_SQ = view(SB, 10240, [2, T])

        def rwkv_decay_act(act, l, I):
            act.wait_ge(S("rw_dm"), l + 1)
            I(nc.scalar.activation(E1, DM, ACT.Exp, scale=DECAY))
            I(nc.scalar.activation(E2, DM, ACT.Exp, scale=-DECAY))
            I(nc.scalar.activation(E3, DM1, ACT.Exp, scale=DECAY))
            I(nc.scalar.activation(SCL, SCL, ACT.Exp, scale=DECAY))
            act.wait_ge(S("rw_ssm"), l + 1)
            nc.scalar.activation(RK_SQ, RK_SQ, ACT.Sqrt).then_inc(S("rw_norm"), 1)

        def rwkv_norm_pe(pe, l):
            pe.wait_ge(S("rw_sq"), l + 1)
            pe.wait_ge(S("rw_gates"), l + 1)
            m = pe.matmul(ps[:, 6, :], cst("head_ones"), RK_SQ.rearrange("p c t -> p (c t)"), start=True, stop=True)
            m.then_inc(S("rw_ss"), 1)
            pe.wait_ge(S("rw_v"), l + 1)
            for t in range(NT):
                for c in range(2):
                    m = pe.transpose(ps[:, 7, t * T + c * P:t * T + (c + 1) * P], HT[:, T_V + c, t * P:(t + 1) * P], ident)
            m.then_inc(S("rw_vt_ps"), 1)

        def rwkv_values_act(act, l):
            act.wait_ge(S("rw_vt_ps"), l + 1)
            nc.scalar.activation(VT, ps[:, 7, :].rearrange("p (t c) -> p t c", t=NT), ACT.Copy).then_inc(S("rw_vt"), 1)

        def rwkv_pairs_pe(pe, l):
            pe.wait_ge(S("rw_ops"), l + 1)
            pe.wait_ge(S("rw_vt"), l + 1)
            for i, (tl, c) in enumerate((a, c) for a in (BT, KTL) for c in range(2)):
                m = pe.transpose(ps[:, 7, i * P:(i + 1) * P], tl[:, c, 0:P], ident)
            m.then_inc(S("rw_bk_ps"), 1)
            for t in range(NT):
                for c in range(2):
                    m = pe.matmul(ps[:, 5, 4 * t:4 * t + 4], RK[:, c, t * P:(t + 1) * P], par("r_k")[:, 4 * c:4 * c + 4],
                                  start=c == 0, stop=c == 1)
            m.then_inc(S("rw_bonus"), 1)
            for u in range(8):
                j, h = divmod(u, 4)
                c, pb = h // 2, HD * (h % 2)
                if u == 0:
                    pe.wait_ge(S("gla_st"), 3 * (l + 1))
                if u >= 4:
                    pe.wait_ge(S("rw_mm"), 8 * l + u - 3)
                rhs = AR[pb:pb + HD, c, j, :, :].rearrange("p w s -> p (w s)")
                for w, tl in enumerate((BT, KTL)):
                    m = pe.matmul(ps[:, u % 4, w * 256:(w + 1) * 256], tl[pb:pb + HD, c, j * P:(j + 1) * P], rhs,
                                  start=True, stop=True)
                m.then_inc(S("rw_pairs"), 1)

        def rwkv_bk_act(act, l):
            act.wait_ge(S("rw_bk_ps"), l + 1)
            nc.scalar.activation(BK, ps[:, 7, :].rearrange("p (t c) -> p t c", t=2), ACT.Copy).then_inc(S("rw_bk"), 1)

        def rwkv_inverse_dve(v, l, I, L):
            v.wait_ge(S("rw_bonus"), l + 1)
            I(nc.vector.memset(S0, 0.0))
            L(nc.vector.tensor_copy(SM[:, 32:40], ps[:, 5, 0:8]))
            idb = ident.unsqueeze(1).broadcast_to([P, 8, P])
            I(nc.vector.tensor_copy(TM, idb))
            nc.vector.tensor_copy(TT, idb).then_inc(S("rw_init"), 1)
            for u in range(8):
                v.wait_ge(S("rw_pairs"), 8 * l + u + 1)
                nc.vector.tensor_tensor(MM[:, u, :, :].rearrange("p a s -> p (a s)"), ps[:, u % 4, :], cst("pairs"),
                                        ALU.mult).then_inc(S("rw_mm"), 1)
            v.wait_ge(S("rw_init"), l + 1)
            v.wait_ge(S("rw_mm"), 8 * (l + 1))
            for n in range(7):
                for g in range(2):
                    at = 14 * l + 2 * n + g
                    us = slice(4 * g, 4 * g + 4)
                    if n:
                        v.wait_ge(S("rw_z_ps"), at - 1)
                    lev = cst("levels")[:, n * P:(n + 1) * P].unsqueeze(1).broadcast_to([P, 4, P])
                    nc.vector.tensor_tensor(MK[:, us, :], MM[:, us, 0, :], lev, ALU.mult).then_inc(S("rw_mk"), 1)
                for g in range(2):
                    at = 14 * l + 2 * n + g
                    us = slice(4 * g, 4 * g + 4)
                    v.wait_ge(S("rw_dt"), at + 1)
                    nc.vector.tensor_tensor(TM[:, us, :], TM[:, us, :],
                                            ps[:, 2 + g, :].rearrange("p (u s) -> p u s", u=4), ALU.add).then_inc(S("rw_tm"), 1)
                    nc.vector.tensor_tensor(TT[:, us, :], TT[:, us, :],
                                            ps[:, 4 + g, :].rearrange("p (u s) -> p u s", u=4), ALU.add).then_inc(S("rw_tm"), 1)
                    v.wait_ge(S("rw_tm"), 2 * at + 2)

        def rwkv_inverse_pe(pe, l):
            pe.wait_ge(S("rw_init"), l + 1)
            for n in range(7):
                for g in range(2):
                    at = 14 * l + 2 * n + g
                    pe.wait_ge(S("rw_mk"), at + 1)
                    if n:
                        pe.wait_ge(S("rw_tm"), 2 * (at - 1))
                    for i in range(4):
                        u = 4 * g + i
                        m = pe.matmul(ps[:, g, i * P:(i + 1) * P], MK[:, u, :], TM[:, u, :], start=True, stop=True)
                    m.then_inc(S("rw_z_ps"), 1)
                for g in range(2):
                    at = 14 * l + 2 * n + g
                    pe.wait_ge(S("rw_zc"), at + 1)
                    for i in range(4):
                        u = 4 * g + i
                        pe.matmul(ps[:, 2 + g, i * P:(i + 1) * P], TT[:, u, :], ZM[:, u, :], start=True, stop=True)
                    for i in range(4):
                        u = 4 * g + i
                        m = pe.matmul(ps[:, 4 + g, i * P:(i + 1) * P], ZM[:, u, :], TT[:, u, :], start=True, stop=True)
                    m.then_inc(S("rw_dt"), 1)

        def rwkv_inverse_act(act, l):
            for n in range(7):
                for g in range(2):
                    at = 14 * l + 2 * n + g
                    act.wait_ge(S("rw_z_ps"), at + 1)
                    if n == 0 and g == 0:
                        act.wait_ge(S("rw_ops"), l + 1)
                    nc.scalar.activation(ZM[:, 4 * g:4 * g + 4, :].rearrange("p u s -> p (u s)"), ps[:, g, :],
                                         ACT.Copy).then_inc(S("rw_zc"), 1)

        def rwkv_chunks_pe(pe, l):
            pe.wait_ge(S("rw_tm"), 28 * (l + 1))
            pe.wait_ge(S("rw_bk"), l + 1)
            for j in range(2):
                for c in range(2):
                    if j:
                        pe.matmul(ps[:, 6, c * P:(c + 1) * P], AR[:, c, 1, 0, :], S0[:, c, :, :].rearrange("p h d -> p (h d)"),
                                  start=True, stop=False, skip_group_check=True)
                    for h in range(2 * c, 2 * c + 2):
                        m = pe.matmul(ps[:, 6, h * HD:(h + 1) * HD], MM[:, 4 * j + h, 2, :], VT[:, j, h * HD:(h + 1) * HD],
                                      start=j == 0, stop=True, skip_group_check=True)
                m.then_inc(S("rw_x_ps"), 1)
                pe.wait_ge(S("rw_x"), 2 * l + j + 1)
                for h in range(4):
                    m = pe.matmul(ps[:, 6, 256 + h * HD:256 + (h + 1) * HD], TT[:, 4 * j + h, :], XU[:, h * HD:(h + 1) * HD],
                                  start=True, stop=True)
                m.then_inc(S("rw_u_ps"), 1)
                pe.wait_ge(S("rw_u"), 2 * l + j + 1)
                if j == 0:
                    for h in range(4):
                        c, pb = h // 2, HD * (h % 2)
                        pe.matmul(ps[pb:pb + HD, 5, c * HD:(c + 1) * HD], BK[:, 0, h * HD:(h + 1) * HD],
                                  US[:, h * HD:(h + 1) * HD], start=True, stop=False)
                        m = pe.matmul(ps[pb:pb + HD, 5, c * HD:(c + 1) * HD], BK[:, 1, h * HD:(h + 1) * HD],
                                      VT[:, 0, h * HD:(h + 1) * HD], start=False, stop=True)
                    m.then_inc(S("rw_s_ps"), 1)
                for c in range(2):
                    if j:
                        pe.matmul(ps[:, 7, 256 + c * P:256 + (c + 1) * P], AR[:, c, 1, 1, :],
                                  S0[:, c, :, :].rearrange("p h d -> p (h d)"), start=True, stop=False, skip_group_check=True)
                    for h in range(2 * c, 2 * c + 2):
                        to = ps[:, 7, (4 * j + h) * HD:(4 * j + h + 1) * HD]
                        pe.matmul(to, MM[:, 4 * j + h, 1, :], US[:, h * HD:(h + 1) * HD], start=j == 0, stop=False,
                                  skip_group_check=True)
                        m = pe.matmul(to, MM[:, 4 * j + h, 3, :], VT[:, j, h * HD:(h + 1) * HD], start=False, stop=True,
                                      skip_group_check=True)
                m.then_inc(S("rw_y"), 1)
                if j == 0:
                    pe.wait_ge(S("rw_s"), l + 1)

        def rwkv_chunks_dve(v, l, I, L):
            for j in range(2):
                v.wait_ge(S("rw_x_ps"), 2 * l + j + 1)
                nc.vector.tensor_copy(XU, ps[:, 6, 0:256]).then_inc(S("rw_x"), 1)
                v.wait_ge(S("rw_u_ps"), 2 * l + j + 1)
                if j:
                    v.wait_ge(S("rw_y"), 2 * l + 1)
                nc.vector.tensor_copy(US, ps[:, 6, 256:512]).then_inc(S("rw_u"), 1)
                if j == 0:
                    v.wait_ge(S("rw_s_ps"), l + 1)
                    for h in range(4):
                        c, rows = h // 2, slice(HD * (h % 2), HD * (h % 2) + HD)
                        ins = nc.vector.tensor_scalar(S0[rows, c, h % 2, :], ps[rows, 5, c * HD:(c + 1) * HD],
                                                      SCL[rows, c:c + 1], None, ALU.mult)
                        if h < 3:
                            I(ins)
                    ins.then_inc(S("rw_s"), 1)
            v.wait_ge(S("rw_y"), 2 * (l + 1))
            head_norm_dve(v, I, L, ps[:, 7, :].rearrange("p (a b) -> p a b", b=HD), RWKV_EPS, 2, 2 * l + 1, R_XC, R_SQ)
            bonus = SM[:, 32:40].unsqueeze(2).broadcast_to([P, 8, HD])
            L(nc.vector.tensor_tensor(R_SQ.rearrange("p (a b) -> p a b", b=HD),
                                      VT.rearrange("p t (h b) -> p (t h) b", b=HD), bonus, ALU.mult))
            L(nc.vector.tensor_tensor(R_XC, R_XC, R_SQ, ALU.add))
            nc.vector.tensor_tensor(R_XC, R_XC, GT.rearrange("p t c -> p (t c)"), ALU.mult).then_inc(S("head_out"), 1)

        N_RT = view(SA, 0, [7, T])
        N_FL = [view(SB, 480 * i, [16, 30]) for i in range(2)]
        N_GE = [view(SB, 960 + 512 * i, [512]) for i in range(3)]
        N_HID = view(SB, 2496, [4, 30])
        N_KC, N_VC = view(SB, 2616, [15]), view(SB, 2631, [2, HD])
        N_GT = view(SB, 2759, [NT, 24])
        N_P, N_PT = view(SA, 2048, [8, T]), view(SA, 0, [4, 512])
        MX, RS, RG = SM[:, 48:56], SM[:, 56:64], SM[:, 64:72]

        def rope_pe(pe, l):
            pe.wait_ge(S("proj_evac"), 15 * (l + 1))
            pe.wait_ge(S("rw_out"), l + 1)
            for j in range(7):
                m = pe.matmul(ps[:, j // 2, (j % 2) * T:(j % 2 + 1) * T], cst("rot"), HT[:, T_KC + j, :], start=True, stop=True)
            m.then_inc(S("rope_ps"), 1)

        def rope_dve(v, l, I, L):
            v.wait_ge(S("rope_ps"), l + 1)
            x = HT[:, T_KC:T_KC + 7, :]
            cos, sin = (cst(n).unsqueeze(1).broadcast_to([P, 7, T]) for n in ("cos", "sin"))
            I(nc.vector.tensor_tensor(N_RT, bank(0, 4)[:, 0:7 * T].rearrange("p (j t) -> p j t", t=T), sin, ALU.mult))
            L(nc.vector.tensor_tensor(x, x, cos, ALU.mult))
            nc.vector.tensor_tensor(x, x, N_RT, ALU.add).then_inc(S("rope"), 1)
            v.wait_ge(S("rope"), l + 1)

        def cmp_pool(pool, l):
            pool.wait_ge(S("rope"), l + 1)
            pool.wait_ge(S("par_loaded"), 16 * (l + 1))
            for i, (tile, emb) in enumerate(((T_KC, "pos_k"), (T_VC, "pos_v"))):
                for g in range(2):
                    rows = slice(HD * g, HD * (g + 1))
                    src = HT[rows, tile, :].rearrange("p (c j w) -> p w j c", j=8, w=2)
                    pos = par(emb)[rows, :].rearrange("p (j w) -> p w j", w=2)
                    for w in range(2):
                        for half in range(2):
                            ins = nc.gpsimd.tensor_tensor(
                                N_FL[i][HD * w:HD * (w + 1), 8 * half:8 * half + 8, 15 * g:15 * g + 15],
                                src[:, w, :, half:half + 15],
                                pos[:, w, 8 * half:8 * half + 8].unsqueeze(2).broadcast_to([HD, 8, 15]), ALU.add)
                            ins.then_inc(S("cmp_blocks"), 1)

        def cmp_pe(pe, l):
            base = l * LAYER_SLOTS
            for i in range(2):
                need_slot(pe, base + S_CMP + i)
                pe.wait_ge(S("cmp_blocks"), 16 * l + 8 * (i + 1))
                w = slot(base + S_CMP + i).rearrange("p (j n) -> p j n", j=16)
                for j in range(16):
                    m = pe.matmul(ps[0:30, 4, i * 256:(i + 1) * 256], N_FL[i][:, j, :], w[:, j, :], start=j == 0, stop=j == 15)
                m.then_inc(S("cmp_hidden"), 1)
            pe.wait_ge(S("gelu"), l + 1)
            for i in range(4):
                m = pe.transpose(ps[:, 5, i * 30:(i + 1) * 30], N_GE[0][0:30, i * P:(i + 1) * P], ident[0:30, 0:30])
            m.then_inc(S("cmp_hid_ps"), 1)
            pe.wait_ge(S("cmp_hid"), l + 1)
            wk, wv = (par(n).rearrange("p (a d) -> p a d", a=2) for n in ("wk2", "wv2"))
            for g in range(2):
                cols = slice(15 * g, 15 * g + 15)
                for a in range(2):
                    pe.matmul(ps[HD * g:HD * (g + 1), 5, 128:143], wk[:, a, :], N_HID[:, a, cols], start=a == 0, stop=a == 1)
            for g in range(2):
                cols = slice(15 * g, 15 * g + 15)
                for a in range(2):
                    m = pe.matmul(ps[0:15, 4, HD * g:HD * (g + 1)], N_HID[:, 2 + a, cols], wv[:, a, :], start=a == 0, stop=a == 1)
            m.then_inc(S("cmp_kv_ps"), 1)

        def gelu_dve(v, L, n, x, y, t, to):
            L(nc.vector.tensor_tensor(y, x, x, ALU.mult))
            L(nc.vector.tensor_scalar(y, y, GELU_K, 1.0, ALU.mult, ALU.add))
            nc.vector.tensor_tensor(y, y, x, ALU.mult).then_inc(S("tanh_in"), 1)
            v.wait_ge(S("tanh"), n + 1)
            L(nc.vector.scalar_tensor_tensor(out=t, in0=t, scalar=1.0, in1=x, op0=ALU.add, op1=ALU.mult))
            nc.vector.tensor_scalar(to, t, 0.5, None, ALU.mult).then_inc(S("gelu"), 1)

        def cmp_dve(v, l, I, L):
            v.wait_ge(S("cmp_hidden"), 2 * (l + 1))
            x, y, t = (a[0:30, :] for a in N_GE)
            L(nc.vector.tensor_copy(x, ps[0:30, 4, :]))
            gelu_dve(v, L, l, x, y, t, x)
            v.wait_ge(S("cmp_hid_ps"), l + 1)
            nc.vector.tensor_copy(N_HID.rearrange("p a b -> p (a b)"), ps[:, 5, 0:120]).then_inc(S("cmp_hid"), 1)
            v.wait_ge(S("cmp_kv_ps"), l + 1)
            I(nc.vector.tensor_copy(N_KC, ps[:, 5, 128:143]))
            nc.vector.tensor_copy(N_VC[0:15, :, :], ps[0:15, 4, 0:P].rearrange("p (g d) -> p g d", g=2)).then_inc(S("cmp_kv"), 1)

        def cmp_act(act, l):
            act.wait_ge(S("tanh_in"), l + 1)
            nc.scalar.activation(N_GE[2][0:30, :], N_GE[1][0:30, :], ACT.Tanh, scale=GELU_C).then_inc(S("tanh"), 1)
            nc.scalar.activation(N_GT, NV[:, :, 256:280], ACT.Sigmoid).then_inc(S("nsa_gate"), 1)

        def width(kind, t):
            return 15 if kind == 0 else P * (t + 1)

        def attention_keys(kind, g, l):
            rows = slice(HD * g, HD * (g + 1))
            if kind == 0:
                return N_KC[rows, :]
            return HT[rows, {1: T_KS, 2: T_KW, 3: 4}[kind], :]

        def attention_values(kind, g, k):
            if kind == 0:
                return N_VC[0:15, g, :]
            if kind == 3:
                return V2[:, k, HD * g:HD * (g + 1)]
            return NV[:, k, (kind - 1) * P + HD * g:(kind - 1) * P + HD * (g + 1)]

        def attention_pe(pe, kinds, l, n0, q0):
            for n, (kind, t) in enumerate(((kind, t) for kind in kinds for t in range(NT)), n0):
                w = width(kind, t)
                if n > n0:
                    pe.wait_ge(S("att_raw"), n)
                for i in range(8):
                    g, j = divmod(i, 4)
                    rows = slice(HD * g, HD * (g + 1))
                    at = 512 * g + 16 * j if kind == 0 else i * w
                    m = pe.matmul(bank(0, 4)[:, at:at + w], HT[rows, q0 + j, t * P:(t + 1) * P],
                                  attention_keys(kind, g, l)[:, 0:w], start=True, stop=True)
                m.then_inc(S("att_scores"), 1)
                pe.wait_ge(S("att_p"), n + 1)
                blocks = 1 if kind == 0 else t + 1
                for k in range(blocks):
                    kw = min(w, P)
                    for half in range(2):
                        x = attention_count(kinds, n - n0, k, half) + attention_base(n0)
                        if x >= 2:
                            pe.wait_ge(S("att_pt"), x - 1)
                        for i in range(4):
                            m = pe.transpose(ps[0:kw, 4 + half, i * P:(i + 1) * P],
                                             N_P[:, 4 * half + i, k * P:k * P + kw], ident)
                        m.then_inc(S("att_t_ps"), 1)
                    for half in range(2):
                        x = attention_count(kinds, n - n0, k, half) + attention_base(n0)
                        pe.wait_ge(S("att_pt"), x + 1)
                        for i in range(4):
                            g, j = half, i
                            first = n - n0 == 0 and k == 0 and j % 2 == 0
                            m = pe.matmul(ps[HD * g:HD * (g + 1), 6 + j // 2, (j % 2) * T + t * P:(j % 2) * T + (t + 1) * P],
                                          attention_values(kind, g, k), N_PT[0:kw, x % 4, i * P:(i + 1) * P],
                                          start=first, stop=True, skip_group_check=True)
                        m.then_inc(S("att_pv"), 1)

        def attention_count(kinds, n, k, half):
            passes = [(kind, t) for kind in kinds for t in range(NT)]
            return 2 * sum(1 if kind == 0 else t + 1 for kind, t in passes[:n]) + 2 * k + half

        def attention_base(n0):
            return (n0 // 6) * 16

        def attention_act(act, kinds, n0, sink):
            for n, (kind, t) in enumerate(((kind, t) for kind in kinds for t in range(NT)), n0):
                w = width(kind, t)
                act.wait_ge(S("att_max"), n + 1)
                if sink:
                    nc.scalar.activation(RG, RG, ACT.Exp).then_inc(S("att_sink"), 1)
                for i in range(8):
                    nc.scalar.activation(N_P[:, i, 0:w], N_P[:, i, 0:w], ACT.Exp, scale=HD ** -0.5, bias=MX[:, i:i + 1],
                                         accum_out=RS[:, i:i + 1]).then_inc(S("att_exp"), 1)
                blocks = 1 if kind == 0 else t + 1
                for k in range(blocks):
                    kw = min(w, P)
                    for half in range(2):
                        x = attention_count(kinds, n - n0, k, half) + attention_base(n0)
                        act.wait_ge(S("att_t_ps"), x + 1)
                        if x >= 4:
                            act.wait_ge(S("att_pv"), x - 3)
                        nc.scalar.activation(N_PT[0:kw, x % 4, :], ps[0:kw, 4 + half, :], ACT.Copy).then_inc(S("att_pt"), 1)

        def attention_dve(v, kinds, n0, I, L, sink=None):
            for n, (kind, t) in enumerate(((kind, t) for kind in kinds for t in range(NT)), n0):
                w = width(kind, t)
                v.wait_ge(S("att_scores"), n + 1)
                if n > n0:
                    x = attention_count(kinds, n - n0, 0, 0) + attention_base(n0)
                    v.wait_ge(S("att_t_ps"), x)
                if kind == 0:
                    cm = cst("cmp_add")[:, 15 * t:15 * t + 15].unsqueeze(1).broadcast_to([P, 4, 15])
                    for g in range(2):
                        raw = ps[:, g, 0:64].rearrange("p (j k) -> p j k", j=4)
                        ins = nc.vector.tensor_tensor(N_P[:, 4 * g:4 * g + 4, 0:15], raw[:, :, 0:15], cm, ALU.add)
                        if g == 0:
                            I(ins)
                    ins.then_inc(S("att_raw"), 1)
                else:
                    raw = bank(0, 4)[:, 0:8 * w].rearrange("p (i k) -> p i k", i=8)
                    diag = cst("diag_add").unsqueeze(1).broadcast_to([P, 8, P])
                    if t:
                        if kind == 3:
                            prev = cst("prev_add").unsqueeze(1).broadcast_to([P, 8, P])
                            I(nc.vector.tensor_tensor(N_P[:, :, 0:P], raw[:, :, 0:P], prev, ALU.add))
                        else:
                            I(nc.vector.tensor_copy(N_P[:, :, 0:P], raw[:, :, 0:P]))
                    nc.vector.tensor_tensor(N_P[:, :, w - P:w], raw[:, :, w - P:w], diag, ALU.add).then_inc(S("att_raw"), 1)
                v.wait_ge(S("att_raw"), n + 1)
                L(nc.vector.tensor_reduce(MX, N_P[:, :, 0:w], AX.X, ALU.max))
                if sink is not None:
                    L(nc.vector.tensor_scalar(MX, MX, HD ** -0.5, None, ALU.mult))
                    L(nc.vector.tensor_tensor(MX, MX, sink, ALU.max))
                    I(nc.vector.tensor_tensor(RG, sink, MX, ALU.subtract))
                    nc.vector.tensor_scalar(MX, MX, -1.0, None, ALU.mult).then_inc(S("att_max"), 1)
                else:
                    nc.vector.tensor_scalar(MX, MX, -(HD ** -0.5), None, ALU.mult).then_inc(S("att_max"), 1)
                v.wait_ge(S("att_exp"), 8 * (n + 1))
                if sink is not None:
                    v.wait_ge(S("att_sink"), n - n0 + 1)
                    L(nc.vector.tensor_tensor(RS, RS, RG, ALU.add))
                L(nc.vector.reciprocal(RG, RS))
                if kind != 3:
                    gate = N_GT[:, t, :].rearrange("p (i b) -> p i b", b=3)[:, :, kind]
                    L(nc.vector.tensor_tensor(RG, RG, gate, ALU.mult))
                if kind == 0:
                    L(nc.vector.tensor_scalar(RG, RG, cst("cmp_any")[:, t:t + 1], None, ALU.mult))
                nc.vector.tensor_tensor(N_P[:, :, 0:w], N_P[:, :, 0:w], RG.unsqueeze(2).broadcast_to([P, 8, w]),
                                        ALU.mult).then_inc(S("att_p"), 1)
                v.wait_ge(S("att_p"), n + 1)

        def mix_out_pe(pe, l):
            for done in ("gla_out", "rw_out", "nsa_out"):
                pe.wait_ge(S(done), l + 1)
            for c in range(2):
                i = l * LAYER_SLOTS + S_WO + c
                need_slot(pe, i)
                w = slot(i).rearrange("p (k n) -> p k n", k=KT)
                for t in range(NT):
                    for k in range(KT):
                        m = pe.matmul(ps[:, 2 * t + c, :], OT[:, k, t * P:(t + 1) * P], w[:, k, :], start=k == 0, stop=k == KT - 1)
                m.then_inc(S("mix_ready"), 1)

        def layer_norm_dve(v, n, b0, ready, I, L):
            v.wait_ge(S(ready[0]), ready[1])
            for t in range(NT):
                s, q, r = SM[:, 80 + t:81 + t], SM[:, 84 + t:85 + t], SM[:, 88 + t:89 + t]
                L(nc.vector.scalar_tensor_tensor(out=X[:, t, :], in0=X[:, t, :], scalar=ALPHA, in1=bank(b0 + 2 * t, 2),
                                                 op0=ALU.mult, op1=ALU.add, accum_out=s))
                nc.vector.tensor_scalar(s, s, -1.0 / D, None, ALU.mult).then_inc(S("ln_mean"), 1)
            for t in range(NT):
                s, q, r = SM[:, 80 + t:81 + t], SM[:, 84 + t:85 + t], SM[:, 88 + t:89 + t]
                v.wait_ge(S("ln_sq"), 2 * n + t + 1)
                nc.vector.tensor_scalar(q, q, 1.0 / D, LN_EPS, ALU.mult, ALU.add).then_inc(S("ln_var"), 1)
                v.wait_ge(S("ln_std"), 2 * n + t + 1)
                L(nc.vector.reciprocal(r, r))
                L(nc.vector.tensor_scalar(X[:, t, :], X[:, t, :], s, r, ALU.add, ALU.mult))
                if t == 0:
                    v.wait_ge(S("ln_loaded"), 32 * (n + 1))
                L(nc.vector.tensor_tensor(X[:, t, :], X[:, t, :], LNW, ALU.mult))
                ins = nc.vector.tensor_tensor(X[:, t, :], X[:, t, :], LNB, ALU.add)
                if t == 0:
                    I(ins)
            ins.then_inc(S("x_ready"), 1)
            v.wait_ge(S("x_ready"), n + 1)

        def layer_norm_act(act, n):
            for t in range(NT):
                s, q, r = SM[:, 80 + t:81 + t], SM[:, 84 + t:85 + t], SM[:, 88 + t:89 + t]
                act.wait_ge(S("ln_mean"), 2 * n + t + 1)
                nc.scalar.activation(SQ, X[:, t, :], ACT.Square, bias=s, accum_out=q).then_inc(S("ln_sq"), 1)
                act.wait_ge(S("ln_var"), 2 * n + t + 1)
                nc.scalar.activation(r, q, ACT.Sqrt).then_inc(S("ln_std"), 1)

        SG = [view(SA, 512 * i, [512]) for i in range(2)]

        def ffn_pe(pe, l):
            pe.wait_ge(S("xt_ready"), 4 * (2 * l + 2))
            for f in range(11):
                i = l * LAYER_SLOTS + S_GU + f
                need_slot(pe, i)
                if f >= 2:
                    pe.wait_ge(S("ffn_evac"), 11 * l + f - 1)
                w = slot(i).rearrange("p (k a n) -> p k a n", k=KT, a=2)
                for a in range(2):
                    for j in range(2):
                        for k in range(KT):
                            m = pe.matmul(ps[:, 2 * a + f % 2, j * T:(j + 1) * T], w[:, k, a, j * P:(j + 1) * P], XT[:, k, :],
                                          start=k == 0, stop=k == KT - 1)
                m.then_inc(S("ffn_ready"), 1)
            for s in range(6):
                i = l * LAYER_SLOTS + S_DN + s
                need_slot(pe, i)
                pe.wait_ge(S("ffn_evac"), 11 * l + min(2 * s + 2, 11))
                w = slot(i).rearrange("p (k n) -> p k n", k=4)
                for k in range(4 * s, min(4 * s + 4, NF)):
                    for t in range(NT):
                        for c in range(2):
                            m = pe.matmul(ps[:, 4 + 2 * t + c, :], HT[:, k, t * P:(t + 1) * P],
                                          w[:, k - 4 * s, c * 512:(c + 1) * 512], start=k == 0, stop=k == NF - 1)
                m.then_inc(S("down_ready"), 1)

        def ffn_act(act, l):
            for f in range(11):
                act.wait_ge(S("ffn_ready"), 11 * l + f + 1)
                if f >= 2:
                    act.wait_ge(S("ffn_evac"), 11 * l + f - 1)
                nc.scalar.activation(SG[f % 2], ps[:, f % 2, :], ACT.Silu).then_inc(S("ffn_silu"), 1)

        def ffn_dve(v, l):
            for f in range(11):
                v.wait_ge(S("ffn_silu"), 11 * l + f + 1)
                nc.vector.tensor_tensor(HT[:, 2 * f:2 * f + 2, :].rearrange("p a t -> p (a t)"), SG[f % 2], ps[:, 2 + f % 2, :],
                                        ALU.mult).then_inc(S("ffn_evac"), 1)

        MOD = view(SB, 4096, [6, D])
        CR = view(SA, 0, [KT, P])
        HF = view(SA, 2048, [NT, D])
        V2 = NV[:, :, 0:P]
        XC2, RA, RI, AE = (view(SB, at, [4, T]) for at in (10240, 11264, 12288, 13312))
        SQM = view(SB, 10240, [8, T])
        YT = view(SB, 12288, [D])
        BR, SNK = SM[:, 128:160], SM[:, 160:168]
        BD = view(SB, 2 * D, [D])

        def second_sp(sp):
            for done in ("gla_out", "rw_out", "nsa_out"):
                sp.wait_ge(S(done), DEPTH)
            sp.dma_start(PAR[:, 0:SECOND_COLS], dram["second"]).then_inc(S("par2_loaded"), 16)
            sp.dma_start(MOD.rearrange("p a d -> p (a d)"), dram["b_ada"].broadcast_to([P, 6 * D])).then_inc(S("par2_loaded"), 16)
            sp.dma_start(SM[:, 128:168], dram["small"].broadcast_to([P, 40])).then_inc(S("par2_loaded"), 16)
            for i in range(S_ADA, S_MOE):
                stream(sp, i)
                if i == S_ADA + 2 * RING:
                    sp.wait_ge(S("x_ready"), 2 * DEPTH)
                    sp.dma_start(LNW, dram["gains"][0:1, :].broadcast_to([P, D])).then_inc(S("gain_loaded"), 16)
                    sp.dma_start(LNB, dram["gains"][1:2, :].broadcast_to([P, D])).then_inc(S("gain_loaded"), 16)
            sp.wait_ge(S("h_ready"), 1)
            sp.dma_start(LNW, dram["gains"][2:3, :].broadcast_to([P, D])).then_inc(S("gain_loaded"), 16)

        def modulation_pe(pe):
            pe.wait_ge(S("cond"), 1)
            for n in range(12):
                need_slot(pe, S_ADA + n)
                w = slot(S_ADA + n).rearrange("p (k n) -> p k n", k=KT)
                if n >= 4:
                    pe.wait_ge(S("mod"), n - 3)
                for k in range(KT):
                    m = pe.matmul(ps[:, n % 4, :], CR[:, k, :], w[:, k, :], start=k == 0, stop=k == KT - 1)
                m.then_inc(S("mod_ready"), 1)

        def modulation_dve(v, I, L):
            v.wait_ge(S("par2_loaded"), 48)
            nc.vector.tensor_copy(CR, par2("c").unsqueeze(2).broadcast_to([P, KT, P])).then_inc(S("cond"), 1)
            flat = MOD.rearrange("p a d -> p (a d)")
            for n in range(12):
                v.wait_ge(S("mod_ready"), n + 1)
                to = flat[:, n * 512:(n + 1) * 512]
                nc.vector.tensor_tensor(to, to, ps[:, n % 4, :], ALU.add).then_inc(S("mod"), 1)
            v.wait_ge(S("mod"), 12)

        def rms_act(act, n, ready):
            act.wait_ge(S(ready[0]), ready[1])
            for t in range(NT):
                if 2 * n + t:
                    act.wait_ge(S("rms_sq"), 2 * n + t)
                nc.scalar.activation(SQ2, X[:, t, :], ACT.Square, accum_out=SM[:, 92 + t:93 + t]).then_inc(S("rms_sq"), 1)
            act.wait_ge(S("rms_var"), n + (2 if n else 1))
            nc.scalar.activation(SM[:, 96:98], SM[:, 94:96], ACT.Sqrt).then_inc(S("rms_std"), 1)

        SQ2 = view(SB, 3 * D, [D])

        def rms_dve(v, n, L):
            v.wait_ge(S("rms_sq"), 2 * (n + 1))
            nc.vector.tensor_scalar(SM[:, 94:96], SM[:, 92:94], 1.0 / D, RMS_EPS, ALU.mult, ALU.add).then_inc(S("rms_var"), 1)
            v.wait_ge(S("rms_std"), n + (2 if n else 1))
            L(nc.vector.reciprocal(SM[:, 98:100], SM[:, 96:98]))

        def modulated_dve(v, n, I, L):
            v.wait_ge(S("gain_loaded"), 32)
            scale, shift = MOD[:, 3 * n + 1, :], MOD[:, 3 * n, :]
            L(nc.vector.scalar_tensor_tensor(out=scale, in0=scale, scalar=1.0, in1=(LNW, LNB)[n], op0=ALU.add, op1=ALU.mult))
            rms_dve(v, n, L)
            for t in range(NT):
                L(nc.vector.scalar_tensor_tensor(out=HF[:, t, :], in0=X[:, t, :], scalar=SM[:, 98 + t:99 + t], in1=scale,
                                                 op0=ALU.mult, op1=ALU.mult))
                ins = nc.vector.tensor_tensor(HF[:, t, :], HF[:, t, :], shift, ALU.add)
                if t == 0:
                    I(ins)
            ins.then_inc(S("h_ready"), 1)

        def project2_pe(pe):
            pe.wait_ge(S("xt_ready"), 4 * 5)
            pe.wait_ge(S("mod"), 12)
            g = 0
            for s in range(4):
                need_slot(pe, S_IN2 + s)
                w = slot(S_IN2 + s).rearrange("p (k n) -> p k n", k=KT)
                for q in range(2):
                    if g >= 4:
                        pe.wait_ge(S("proj2_evac"), g - 3)
                    for j in range(2):
                        for k in range(KT):
                            if g < 6 or (g == 6 and j == 0):
                                m = pe.matmul(ps[:, g % 4, j * T:(j + 1) * T], w[:, k, (2 * q + j) * P:(2 * q + j + 1) * P],
                                              XT[:, k, :], start=k == 0, stop=k == KT - 1)
                            elif g == 7:
                                m = pe.matmul(ps[:, g % 4, j * P:(j + 1) * P], XT[:, k, j * P:(j + 1) * P], w[:, k, P:2 * P],
                                              start=k == 0, stop=k == KT - 1)
                    m.then_inc(S("proj2_ready"), 1)
                    g += 1

        def project2_act(act):
            for g in range(8):
                act.wait_ge(S("proj2_ready"), g + 1)
                n = 512 if g < 6 else T
                if g < 7:
                    to = HT[:, 2 * g:2 * g + n // T, :].rearrange("p a t -> p (a t)")
                    src = ps[:, g % 4, 0:n]
                else:
                    to, src = V2, ps[:, g % 4, 0:T].rearrange("p (t d) -> p t d", t=NT)
                nc.scalar.activation(to, src, ACT.Copy).then_inc(S("proj2_evac"), 1)

        LSL = SM[:, 100:104]

        def lru_act(act, I, L):
            lam = par2("lam")
            act.wait_ge(S("par2_loaded"), 48)
            L(nc.scalar.activation(SM[:, 104:108], lam, ACT.Abs))
            L(nc.scalar.activation(SM[:, 104:108], SM[:, 104:108], ACT.Exp, scale=-1.0))
            nc.scalar.activation(SM[:, 104:108], SM[:, 104:108], ACT.Ln, bias=cst("ones")[:, 0:1]).then_inc(S("lam_ln"), 1)
            act.wait_ge(S("rg"), 1)
            for a, (to, bias) in enumerate(((RA, "b_a"), (RI, "b_x"))):
                for c in range(4):
                    nc.scalar.activation(to[:, c, :], ps[:, 2 * a + c // 2, (c % 2) * T:(c % 2 + 1) * T], ACT.Sigmoid,
                                         bias=par2(bias)[:, c:c + 1]).then_inc(S("rg_gates"), 1)
            act.wait_ge(S("log_a"), 1)
            I(nc.scalar.activation(AE, RA, ACT.Exp))
            nc.scalar.activation(RA, RA, ACT.Tanh, scale=-1.0).then_inc(S("lru_decay"), 1)
            act.wait_ge(S("mult2"), 1)
            nc.scalar.activation(RA, RA, ACT.Sqrt).then_inc(S("lru_mult"), 1)
            act.wait_ge(S("tanh_in"), DEPTH + 1)
            nc.scalar.activation(RI, RA, ACT.Tanh, scale=GELU_C).then_inc(S("tanh"), 1)

        def rg_pe(pe):
            pe.wait_ge(S("conv"), 1)
            for a, name in enumerate(("rg_a", "rg_x")):
                for c in range(4):
                    m = pe.matmul(ps[:, 2 * a + c // 2, (c % 2) * T:(c % 2 + 1) * T], par2(name)[:, c * P:(c + 1) * P],
                                  XC2[:, c, :], start=True, stop=True)
            m.then_inc(S("rg"), 1)

        def lru_dve(v, I, L):
            v.wait_ge(S("proj2_evac"), 8)
            xr, xg = HT[:, 5:9, :], HT[:, 9:13, :]
            cw = par2("conv_w")
            for c in range(4):
                (L if c == 3 else I)(nc.vector.tensor_scalar(XC2[:, c, :], xr[:, c, :], cw[:, 4 * c + 3:4 * c + 4],
                                                             par2("conv_b")[:, c:c + 1], ALU.mult, ALU.add))
            for d in range(1, 4):
                for c in range(4):
                    ins = nc.vector.scalar_tensor_tensor(out=XC2[:, c, d:T], in0=xr[:, c, 0:T - d],
                                                         scalar=cw[:, 4 * c + 3 - d:4 * c + 4 - d], in1=XC2[:, c, d:T],
                                                         op0=ALU.mult, op1=ALU.add)
                    if d < 3:
                        (L if c == 3 else I)(ins)
                    elif c < 3:
                        I(ins)
            ins.then_inc(S("conv"), 1)
            v.wait_ge(S("lam_ln"), 1)
            L(nc.vector.tensor_scalar(LSL, par2("lam"), 0.0, None, ALU.min))
            L(nc.vector.tensor_tensor(LSL, LSL, SM[:, 104:108], ALU.subtract))
            L(nc.vector.tensor_scalar(LSL, LSL, LRU_C, None, ALU.mult))
            v.wait_ge(S("rg_gates"), 8)
            for c in range(4):
                ins = nc.vector.tensor_scalar(RA[:, c, :], RA[:, c, :], LSL[:, c:c + 1], None, ALU.mult)
                if c < 3:
                    I(ins)
            ins.then_inc(S("log_a"), 1)
            L(nc.vector.tensor_tensor(RI, RI, XC2, ALU.mult))
            v.wait_ge(S("lru_decay"), 1)
            L(nc.vector.tensor_scalar(XC2, RA, 1.0, None, ALU.add))
            L(nc.vector.reciprocal(XC2, XC2))
            L(nc.vector.scalar_tensor_tensor(out=RA, in0=RA, scalar=2.0, in1=XC2, op0=ALU.mult, op1=ALU.mult))
            nc.vector.tensor_scalar(RA, RA, 0.0, None, ALU.max).then_inc(S("mult2"), 1)
            v.wait_ge(S("lru_mult"), 1)
            L(nc.vector.tensor_tensor(RI, RI, RA, ALU.mult))
            for c in range(4):
                (L if c == 3 else I)(nc.vector.tensor_tensor_scan(XC2[:, c, :], AE[:, c, :], RI[:, c, :], 0.0, ALU.mult, ALU.add))
            gelu_dve(v, L, DEPTH, xg, RA, RI, RI)
            v.wait_ge(S("gelu"), DEPTH + 1)
            nc.vector.tensor_tensor(OT[:, 4:8, :], XC2, RI, ALU.mult).then_inc(S("lru_out"), 1)

        def merge_dve(v, I, L):
            nc.vector.tensor_copy(OT[:, 0:4, :].rearrange("p c t -> p (c t)"), bank(6, 2)).then_inc(S("nsa_out"), 1)
            v.wait_ge(S("nsa_out"), DEPTH + 1)
            v.wait_ge(S("lru_out"), 1)
            nc.vector.tensor_tensor(SQM, OT[:], OT[:], ALU.mult).then_inc(S("merge_sq"), 1)
            v.wait_ge(S("merge_sq"), 1)
            for c in range(8):
                g = par2("g_attn")[:, c:c + 1] if c < 4 else par2("g_lru")[:, c - 4:c - 3]
                ins = nc.vector.tensor_scalar(OT[:, c, :], OT[:, c, :], g, None, ALU.mult)
                if c < 7:
                    I(ins)
            ins.then_inc(S("merge_sq"), 1)
            v.wait_ge(S("merge_ss"), 1)
            nc.vector.tensor_scalar(SM[:, 112:116], ps[:, 5, 0:4], 1.0 / 512, RMS_EPS, ALU.mult, ALU.add).then_inc(S("rms_var"), 1)
            v.wait_ge(S("rms_std"), 2)
            L(nc.vector.reciprocal(SM[:, 116:120], SM[:, 112:116]))
            v.wait_ge(S("mix2_ready"), 2)
            v.sem_inc(S("moe_slot"), RING)
            for t in range(NT):
                L(nc.vector.tensor_scalar(YT, bank(2 * t, 2), SM[:, 116 + t:117 + t], None, ALU.mult))
                L(nc.vector.scalar_tensor_tensor(out=YT, in0=bank(4 + 2 * t, 2), scalar=SM[:, 118 + t:119 + t], in1=YT,
                                                 op0=ALU.mult, op1=ALU.add))
                L(nc.vector.tensor_tensor(YT, YT, MOD[:, 2, :], ALU.mult))
                ins = nc.vector.tensor_tensor(X[:, t, :], X[:, t, :], YT, ALU.add)
                if t == 0:
                    L(ins)
            ins.then_inc(S("x_ready"), 1)
            v.wait_ge(S("x_ready"), 2 * DEPTH + 1)

        def merge_act(act):
            act.wait_ge(S("rms_var"), 2)
            nc.scalar.activation(SM[:, 112:116], SM[:, 112:116], ACT.Sqrt).then_inc(S("rms_std"), 1)

        def merge_pe(pe):
            pe.wait_ge(S("merge_sq"), 1)
            for a in range(2):
                for t in range(NT):
                    for c in range(4):
                        m = pe.matmul(ps[:, 5, 2 * a + t:2 * a + t + 1], SQM[:, 4 * a + c, t * P:(t + 1) * P],
                                      cst("ones")[:, 0:1], start=c == 0, stop=c == 3)
            m.then_inc(S("merge_ss"), 1)
            pe.wait_ge(S("merge_sq"), 2)
            pe.wait_ge(S("rms_var"), 2)
            for c in range(2):
                need_slot(pe, S_WO2 + c)
                w = slot(S_WO2 + c).rearrange("p (k n) -> p k n", k=KT)
                for a in range(2):
                    for t in range(NT):
                        for k in range(4):
                            m = pe.matmul(ps[:, 4 * a + 2 * t + c, :], OT[:, 4 * a + k, t * P:(t + 1) * P], w[:, 4 * a + k, :],
                                          start=k == 0, stop=k == 3)
                m.then_inc(S("mix2_ready"), 1)

        LG, SEL, GT2, RNK = (view(SA, 4096 + 64 * i, [NT, NE]) for i in range(4))
        RANK, GATE = view(SA, 4352, [NT, NITEM]), view(SA, 4448, [NT, NITEM])
        M8 = view(SA, 4544, [NT, 8])
        TMP, CUM = view(SA, 4560, [NE]), view(SA, 4592, [NE])
        NXT, CE, EXC = (view(SA, 4624 + 32 * i, [NE]) for i in range(3))
        REM, NEGM, RSUM = SM[:, 170:171], SM[:, 172:174], SM[:, 174:176]
        EID = view(SA, 4720, [64])
        OH, OW, OX = (view(SB, 12288 + 512 * i, [MAX_OVER, NE]) for i in range(3))
        GTT = view(SA, 4800, [T])

        def router_pe(pe):
            pe.wait_ge(S("xt_ready"), 4 * 6)
            pe.wait_ge(S("x_ready"), 2 * DEPTH + 1)
            w = par2("router").rearrange("p (k e) -> p k e", k=KT)
            for t in range(NT):
                for k in range(KT):
                    m = pe.matmul(ps[:, 0, t * NE:(t + 1) * NE], XT[:, k, t * P:(t + 1) * P], w[:, k, :],
                                  start=k == 0, stop=k == KT - 1)
            m.then_inc(S("counts"), 1)
            pe.wait_ge(S("selected"), NT)
            strict, ones = cst("pairs")[:, 0:P], cst("ones")[:, 0:P]
            pe.matmul(ps[:, 1, 0:NE], strict, SEL[:, 0, :], start=True, stop=True)
            pe.matmul(ps[:, 1, NE:2 * NE], strict, SEL[:, 1, :], start=True, stop=False)
            pe.matmul(ps[:, 1, NE:2 * NE], ones, SEL[:, 0, :], start=False, stop=True)
            pe.matmul(ps[:, 1, 2 * NE:3 * NE], ones, SEL[:, 0, :], start=True, stop=False)
            m = pe.matmul(ps[:, 1, 2 * NE:3 * NE], ones, SEL[:, 1, :], start=False, stop=True)
            m.then_inc(S("counts"), 1)
            pe.wait_ge(S("gates"), 1)
            for t in range(NT):
                m = pe.transpose(ps[0:NE, 2, t * P:(t + 1) * P], GT2[:, t, :], ident)
            m.then_inc(S("gates_t_ps"), 1)
            pe.wait_ge(S("gates_t"), 1)
            pe.wait_ge(S("par2_loaded"), 64)              
            for t in range(NT):
                for c in range(2):
                    pe.matmul(ps[:, 4 + 2 * t + c, :], GTT[0:NE, t * P:(t + 1) * P], BD[0:NE, c * 512:(c + 1) * 512],
                                  start=True, stop=True)

        def router_act(act):
            for t in range(NT):
                act.wait_ge(S("top"), t + 1)
                nc.scalar.activation(GT2[:, t, :], LG[:, t, :], ACT.Exp, bias=NEGM[:, t:t + 1]).then_inc(S("gate_exp"), 1)

        def router_dve(v, I, L):
            v.wait_ge(S("counts"), 1)
            L(nc.vector.tensor_tensor(LG, ps[:, 0, 0:2 * NE].rearrange("p (t e) -> p t e", t=NT),
                                      BR.unsqueeze(1).broadcast_to([P, NT, NE]), ALU.add))
            for t in range(NT):
                lg, sel, v4 = LG[:, t, :], SEL[:, t, :], M8[:, t, TOPK - 1:TOPK]
                L(nc.vector.max(M8[:, t, :], lg))
                nc.vector.tensor_scalar(NEGM[:, t:t + 1], M8[:, t, 0:1], -1.0, None, ALU.mult).then_inc(S("top"), 1)
                L(nc.vector.tensor_scalar(sel, lg, v4, None, ALU.is_gt))
                L(nc.vector.tensor_reduce(REM, sel, AX.X, ALU.add))
                L(nc.vector.tensor_scalar(REM, REM, -1.0, float(TOPK), ALU.mult, ALU.add))
                L(nc.vector.tensor_scalar(TMP, lg, v4, None, ALU.is_equal))
                L(nc.vector.tensor_tensor_scan(CUM, cst("ones")[:, 0:NE], TMP, 0.0, ALU.mult, ALU.add))
                L(nc.vector.scalar_tensor_tensor(out=TMP, in0=CUM, scalar=REM, in1=TMP, op0=ALU.is_le, op1=ALU.mult))
                nc.vector.tensor_tensor(sel, sel, TMP, ALU.add).then_inc(S("selected"), 1)
                v.wait_ge(S("selected"), t + 1)
            v.wait_ge(S("gate_exp"), NT)
            L(nc.vector.tensor_tensor(GT2, GT2, SEL, ALU.mult))
            L(nc.vector.tensor_reduce(RSUM, GT2, AX.X, ALU.add))
            L(nc.vector.reciprocal(RSUM, RSUM))
            nc.vector.tensor_tensor(GT2, GT2, RSUM.unsqueeze(2).broadcast_to([P, NT, NE]), ALU.mult).then_inc(S("gates"), 1)
            v.wait_ge(S("gates"), 1)
            I(nc.vector.tensor_copy(GATE[:, :, 0:NE], GT2))
            v.wait_ge(S("counts"), 2)
            cnt = ps[:, 1, 0:2 * NE].rearrange("p (t e) -> p t e", t=NT)
            L(nc.vector.scalar_tensor_tensor(out=RNK, in0=cnt, scalar=2000.0, in1=SEL, op0=ALU.add, op1=ALU.mult))
            L(nc.vector.tensor_scalar(RANK[:, :, 0:NE], RNK, 2000.0, None, ALU.subtract))
            total = ps[:, 1, 2 * NE:3 * NE]
            L(nc.vector.tensor_scalar(NXT, total, float(SLOTS_E), None, ALU.is_gt))
            for r in (2, 3):
                L(nc.vector.tensor_scalar(TMP, total, float(r * SLOTS_E), None, ALU.is_gt))
                L(nc.vector.tensor_tensor(NXT, NXT, TMP, ALU.add))
            L(nc.vector.tensor_tensor_scan(CE, cst("ones")[:, 0:NE], NXT, 0.0, ALU.mult, ALU.add))
            L(nc.vector.tensor_tensor(EXC, CE, NXT, ALU.subtract))
            shape = [P, MAX_OVER, NE]
            item = cst("iota")[:, 0:MAX_OVER].unsqueeze(2).broadcast_to(shape)
            exc, ce = (a.unsqueeze(1).broadcast_to(shape) for a in (EXC, CE))
            I(nc.vector.tensor_tensor(OX, item, exc, ALU.subtract))
            L(nc.vector.tensor_tensor(OH, item, ce, ALU.is_lt))
            L(nc.vector.tensor_scalar(OW, OX, 0.0, None, ALU.is_ge))
            L(nc.vector.tensor_tensor(OH, OH, OW, ALU.mult))
            L(nc.vector.scalar_tensor_tensor(out=OX, in0=OX, scalar=1.0, in1=OH, op0=ALU.add, op1=ALU.mult))
            L(nc.vector.tensor_reduce(CUM[:, 0:MAX_OVER], OX, AX.X, ALU.add))
            L(nc.vector.tensor_scalar(CUM[:, 0:MAX_OVER], CUM[:, 0:MAX_OVER], float(SLOTS_E), 2000.0, ALU.mult, ALU.add))
            for t in range(NT):
                L(nc.vector.tensor_tensor(OW, OH, RNK[:, t:t + 1, :].broadcast_to(shape), ALU.mult))
                L(nc.vector.tensor_reduce(RANK[:, t, NE:NITEM], OW, AX.X, ALU.add))
                L(nc.vector.tensor_tensor(RANK[:, t, NE:NITEM], RANK[:, t, NE:NITEM], CUM[:, 0:MAX_OVER], ALU.subtract))
                L(nc.vector.tensor_tensor(OW, OH, GT2[:, t:t + 1, :].broadcast_to(shape), ALU.mult))
                L(nc.vector.tensor_reduce(GATE[:, t, NE:NITEM], OW, AX.X, ALU.add))
            L(nc.vector.tensor_tensor(OW, OH, cst("iota")[:, 0:NE].unsqueeze(1).broadcast_to(shape), ALU.mult))
            I(nc.vector.tensor_reduce(EID[:, 8 + NE:8 + NITEM], OW, AX.X, ALU.add))
            I(nc.vector.tensor_copy(EID[:, 8:8 + NE], cst("iota")[:, 0:NE]))
            L(nc.vector.tensor_scalar(TMP[:, 0:8], cst("iota")[:, 0:8], 2.0, CE[:, NE - 1:NE], ALU.mult, ALU.is_lt))
            L(nc.vector.tensor_reduce(EID[:, 0:1], TMP[:, 0:8], AX.X, ALU.add))
            I(nc.vector.tensor_scalar(EID[:, 0:1], EID[:, 0:1], float(NE // 2), None, ALU.add))
            L(nc.vector.memset(EID[:, 1:8], 0.0))
            nc.vector.tensor_copy(ITI[:, 0:8 + NITEM], EID[:, 0:8 + NITEM]).then_inc(S("items"), 1)
            v.wait_ge(S("gates_t_ps"), 1)
            nc.vector.tensor_copy(GTT[0:NE, :], ps[0:NE, 2, 0:T]).then_inc(S("gates_t"), 1)

        hid = HT[:].rearrange("p a t -> p (a t)")
        XE = view(hid, 0, [KT, P])
        EH, EHT, EY = view(hid, 1024, [512]), view(hid, 1536, [4, P]), view(hid, 2048, [512])
        EPT = view(hid, 2560, [T])
        EG, EU, ES = (view(hid, 2816 + 512 * i, [512]) for i in range(3))
        EP0 = view(hid, 4352, [NT, 2, SLOTS_E])
        EPW = view(hid, 4608, [2, NT, 2, SLOTS_E])
        BG = [view(SB, 10240 + 1024 * q, [2, 512]) for q in range(2)]
        PAIR_SLOTS = 2 * ITEM_SLOTS

        def moe_pairs(eng):
            eng.wait_ge(S("items"), 1)
            return eng.value_load(ITI[0:1, 0:1], min_val=NE // 2, max_val=NITEM // 2)

        def moe_sp(sp):
            sp.wait_ge(S("h_ready"), 2)
            sp.dma_start(BD[0:NE, :], dram["b_down"]).then_inc(S("par2_loaded"), 16)
            with sp.Fori(0, moe_pairs(sp)) as it:
                for q in range(2):
                    e = sp.value_load(ITI[0:1, bass.ds(it * 2 + 8 + q, 1)], min_val=0, max_val=NE - 1)
                    for b in range(ITEM_SLOTS):
                        k = q * ITEM_SLOTS + b
                        sp.wait_ge(S("moe_slot"), it * PAIR_SLOTS + k + 1)
                        sp.dma_start(slot(S_MOE + k), dram["stream"][bass.ds(e * ITEM_SLOTS + S_MOE + b, 1), :, :]
                                     .rearrange("a p n -> (a p) n")).then_inc(arrived[(S_MOE + k) % RING], 16)
                        if b == 0:
                            sp.wait_ge(S("moe_bias_used"), it * 2 + q + 1)
                            for half in range(2):
                                sp.dma_start(BG[q][HD * half:HD * (half + 1), :, :].rearrange("p a n -> p (a n)"),
                                             dram["b_gu"][bass.ds(e * 2 + half, 1), :].broadcast_to([SLOTS_E, 1024])
                                             ).then_inc(S("moe_bias"), 16)

        def need_moe_slot(pe, it, k):
            i = S_MOE + k
            pe.wait_ge(arrived[i % RING], it * (16 * PAIR_SLOTS // RING) + 16 * (i // RING + 1))

        def moe_pe(pe):
            with pe.Fori(0, moe_pairs(pe)) as it:
                for q in range(2):
                    if q == 0:
                        pe.wait_ge(S("moe_p"), it + 1)
                        pe.wait_ge(S("moe_y_evac"), it * 2 + 1)
                        for k in range(KT):
                            for t in range(NT):
                                m = pe.matmul(ps[:, 2 + k // 4, (k % 4) * P:(k % 4 + 1) * P], HF[:, t, k * P:(k + 1) * P],
                                              EP0[:, t, :, :].rearrange("p a s -> p (a s)"), start=t == 0, stop=t == NT - 1)
                        m.then_inc(S("moe_xe_ps"), 1)
                        pe.wait_ge(S("moe_xe"), it * 2 + 2)
                    pe.wait_ge(S("moe_gu_evac"), it * 2 + q + 1)
                    for b in range(4):
                        need_moe_slot(pe, it, q * ITEM_SLOTS + b)
                        w = slot(S_MOE + q * ITEM_SLOTS + b).rearrange("p (k a h n) -> p k a h n", k=2, a=2, h=2)
                        for k in range(2):
                            for a in range(2):
                                for half in range(2):
                                    m = pe.matmul(ps[HD * half:HD * (half + 1), a, :],
                                                  XE[:, 2 * b + k, q * SLOTS_E:(q + 1) * SLOTS_E], w[:, k, a, half, :],
                                                  start=b + k == 0, stop=b + k == 4, skip_group_check=True)
                        m.then_inc(S("moe_slot"), 1)
                    pe.wait_ge(S("moe_h"), it * 2 + q + 1)
                    for f in range(4):
                        m = pe.transpose(ps[:, 2, f * P:(f + 1) * P], EH[:, f * P:(f + 1) * P], ident)
                    m.then_inc(S("moe_ht_ps"), 1)
                    pe.wait_ge(S("moe_ht"), it * 2 + q + 1)
                    for t in range(NT):
                        m = pe.transpose(ps[:, 2, t * P:(t + 1) * P], EPW[:, q, t, :, :].rearrange("p h s -> p (h s)"), ident)
                    m.then_inc(S("moe_pt_ps"), 1)
                    pe.wait_ge(S("moe_y_evac"), it * 2 + q + 1)
                    for b in range(2):
                        need_moe_slot(pe, it, q * ITEM_SLOTS + 4 + b)
                        w = slot(S_MOE + q * ITEM_SLOTS + 4 + b).rearrange("p (k c n) -> p k c n", k=4, c=2)
                        for k in range(4):
                            for c in range(2):
                                m = pe.matmul(ps[HD * c:HD * (c + 1), 3, :], EHT[:, k, HD * b:HD * (b + 1)], w[:, k, c, :],
                                              start=b + k == 0, stop=b + k == 4, skip_group_check=True)
                        m.then_inc(S("moe_slot"), 1)
                    pe.wait_ge(S("moe_pt"), it * 2 + q + 1)
                    pe.wait_ge(S("moe_y_evac"), it * 2 + q + 2)
                    for t in range(NT):
                        for c in range(2):
                            rows = slice(HD * c, HD * (c + 1))
                            m = pe.matmul(ps[:, 4 + 2 * t + c, :], EPT[rows, t * P:(t + 1) * P], EY[rows, :],
                                          start=False, stop=True, skip_group_check=True)
                    m.then_inc(S("moe_sc"), 1)
            pe.wait_ge(S("moe_last"), 1)
            for t in range(1):
                pe.transpose(ps[:, 0, 0:P], ident, ident).then_inc(S("moe_done"), 1)

        def moe_act(act):
            with act.Fori(0, moe_pairs(act)) as it:
                for q in range(2):
                    if q == 0:
                        act.wait_ge(S("moe_xe_ps"), it + 1)
                        for g in range(2):
                            nc.scalar.activation(XE[:, 4 * g:4 * g + 4, :].rearrange("p k s -> p (k s)"), ps[:, 2 + g, :],
                                                 ACT.Copy).then_inc(S("moe_xe"), 1)
                    act.wait_ge(S("moe_g"), it * 2 + q + 1)
                    nc.scalar.activation(ES, EG, ACT.Sigmoid, scale=SWIGLU_ALPHA).then_inc(S("moe_sig"), 1)
                    act.wait_ge(S("moe_ht_ps"), it * 2 + q + 1)
                    nc.scalar.activation(EHT.rearrange("p f s -> p (f s)"), ps[:, 2, :], ACT.Copy).then_inc(S("moe_ht"), 1)
                    act.wait_ge(S("moe_pt_ps"), it * 2 + q + 1)
                    act.wait_ge(S("moe_sc"), it * 2 + q + 1)
                    nc.scalar.activation(EPT, ps[:, 2, 0:T], ACT.Copy).then_inc(S("moe_pt"), 1)

        def moe_dve(v):
            v.sem_inc(S("moe_gu_evac"), 1)
            v.sem_inc(S("moe_y_evac"), 1)
            v.sem_inc(S("moe_sc"), 1)
            v.sem_inc(S("moe_bias_used"), 2)
            pairs = moe_pairs(v)
            iota = cst("iota")[:, 0:SLOTS_E]
            both = iota.unsqueeze(1).broadcast_to([P, 2, SLOTS_E])
            with v.Fori(0, pairs) as it:
                for q in range(2):
                    for t in range(NT):
                        nc.vector.tensor_scalar(EPW[:, q, t, :, :], both, RANK[:, t, bass.ds(it * 2 + q, 1)],
                                                GATE[:, t, bass.ds(it * 2 + q, 1)], ALU.is_equal, ALU.mult)
                for q in range(2):
                    for t in range(NT):
                        ins = nc.vector.tensor_scalar(EP0[:, t, q, :], iota, RANK[:, t, bass.ds(it * 2 + q, 1)], None, ALU.is_equal)
                ins.then_inc(S("moe_p"), 1)
                for q in range(2):
                    v.wait_ge(S("moe_slot"), it * PAIR_SLOTS + (RING + q * ITEM_SLOTS + 4))
                    v.wait_ge(S("moe_bias"), it * 64 + 32 * (q + 1))
                    nc.vector.tensor_tensor(EG, ps[:, 0, :], BG[q][:, 0, :], ALU.add).then_inc(S("moe_v"), 1)
                    nc.vector.tensor_tensor(EU, ps[:, 1, :], BG[q][:, 1, :], ALU.add).then_inc(S("moe_gu_evac"), 1)
                    v.wait_ge(S("moe_v"), it * 4 + 2 * q + 1)
                    nc.vector.tensor_scalar(EG, EG, LIMIT, None, ALU.min).then_inc(S("moe_g"), 1)
                    v.wait_ge(S("moe_gu_evac"), it * 2 + q + 2)
                    nc.vector.tensor_scalar(EU, EU, LIMIT, -LIMIT, ALU.min, ALU.max).then_inc(S("moe_bias_used"), 1)
                    v.wait_ge(S("moe_bias_used"), it * 2 + q + 3)
                    v.wait_ge(S("moe_g"), it * 2 + q + 1)
                    nc.vector.scalar_tensor_tensor(out=EU, in0=EU, scalar=1.0, in1=EG, op0=ALU.add,
                                                   op1=ALU.mult).then_inc(S("moe_v"), 1)
                    v.wait_ge(S("moe_v"), it * 4 + 2 * q + 2)
                    v.wait_ge(S("moe_sig"), it * 2 + q + 1)
                    nc.vector.tensor_tensor(EH, EU, ES, ALU.mult).then_inc(S("moe_h"), 1)
                    v.wait_ge(S("moe_slot"), it * PAIR_SLOTS + (RING + q * ITEM_SLOTS + 6))
                    v.wait_ge(S("moe_sc"), it * 2 + q + 1)
                    nc.vector.tensor_copy(EY, ps[:, 3, :]).then_inc(S("moe_y_evac"), 1)
            v.sem_inc(S("moe_last"), 1)

        def final_dve(v, I, L):
            v.wait_ge(S("moe_done"), 1)
            for t in range(NT):
                L(nc.vector.tensor_tensor(YT, bank(4 + 2 * t, 2), MOD[:, 5, :], ALU.mult))
                ins = nc.vector.tensor_tensor(X[:, t, :], X[:, t, :], YT, ALU.add)
                if t == 0:
                    L(ins)
            ins.then_inc(S("x_ready"), 1)
            v.wait_ge(S("x_ready"), 2 * DEPTH + 2)
            rms_dve(v, 2, L)
            v.wait_ge(S("gain_loaded"), 48)
            for t in range(NT):
                nc.vector.scalar_tensor_tensor(out=X[:, t, :], in0=X[:, t, :], scalar=SM[:, 98 + t:99 + t], in1=LNW,
                                               op0=ALU.mult, op1=ALU.mult).then_inc(S("final"), 1)

        block = ctx.enter_context(nc.Block())

        @block.sync
        def _(sp):
            first_sp(sp)
            second_sp(sp)
            moe_sp(sp)
            sp.wait_ge(S("final"), NT)
            sp.dma_start(dram["out"].rearrange("(t p) d -> p t d", p=P), X[:]).then_inc(S("stored"), 16)
            sp.wait_ge(S("stored"), 16)

        @block.gpsimd
        def _(pool):
            for l in range(DEPTH):
                cmp_pool(pool, l)

        @block.tensor
        def _(pe):
            pe.wait_ge(S("const_loaded"), 16)
            for l in range(DEPTH):
                transpose_x_pe(pe, 2 * l, X, ("x_ready", 2 * l) if l else ("x_loaded", 16))
                project_pe(pe, l)
                gla_gate_pe(pe, l)
                rwkv_ranks_pe(pe, l)
                gla_scores_pe(pe, l)
                gla_out_pe(pe, l)
                pe.wait_ge(S("rw_gates"), l + 1)
                back_pe(pe, 2 * l, G_XC, 5)
                rwkv_norm_pe(pe, l)
                pe.wait_ge(S("gla_out"), l + 1)
                rwkv_pairs_pe(pe, l)
                rwkv_inverse_pe(pe, l)
                rwkv_chunks_pe(pe, l)
                back_pe(pe, 2 * l + 1, R_XC, 4)
                rope_pe(pe, l)
                cmp_pe(pe, l)
                pe.wait_ge(S("rope"), l + 1)
                pe.wait_ge(S("cmp_kv"), l + 1)
                attention_pe(pe, (0, 1, 2), l, 6 * l, T_Q)
                mix_out_pe(pe, l)
                transpose_x_pe(pe, 2 * l + 1, X, ("x_ready", 2 * l + 1))
                ffn_pe(pe, l)
            modulation_pe(pe)
            transpose_x_pe(pe, 4, HF, ("h_ready", 1))
            project2_pe(pe)
            rg_pe(pe)
            pe.wait_ge(S("rg_gates"), 8)
            pe.wait_ge(S("proj2_evac"), 8)
            attention_pe(pe, (3,), 0, 12, 0)
            merge_pe(pe)
            transpose_x_pe(pe, 5, HF, ("h_ready", 2))
            router_pe(pe)
            moe_pe(pe)

        @block.scalar
        def _(act):
            I, L = link(act, "act_step")
            act.wait_ge(S("const_loaded"), 16)
            for l in range(DEPTH):
                act.wait_ge(S("par_loaded"), 16 * (l + 1))
                project_act(act, l)
                rwkv_ranks_act(act, l, I)
                rwkv_gates_act(act, l, I)
                gla_act(act, l, I, L)
                gla_end_act(act, l)
                rwkv_decay_act(act, l, I)
                rwkv_values_act(act, l)
                rwkv_bk_act(act, l)
                rwkv_inverse_act(act, l)
                head_norm_act(act, 2 * l + 1)
                cmp_act(act, l)
                attention_act(act, (0, 1, 2), 6 * l, False)
                layer_norm_act(act, 2 * l)
                ffn_act(act, l)
                layer_norm_act(act, 2 * l + 1)
            rms_act(act, 0, ("x_ready", 2 * DEPTH))
            project2_act(act)
            lru_act(act, I, L)
            attention_act(act, (3,), 12, True)
            merge_act(act)
            rms_act(act, 1, ("x_ready", 2 * DEPTH + 1))
            router_act(act)
            moe_act(act)
            rms_act(act, 2, ("x_ready", 2 * DEPTH + 2))

        @block.vector
        def _(v):
            I, L = link(v, "dve_step")
            v.wait_ge(S("const_loaded"), 16)
            for l in range(DEPTH):
                transpose_x_dve(v, 2 * l)
                mix_dve(v, l, I, L)
                gla_dve(v, l, I, L)
                gla_norm_dve(v, l, I, L)
                v.wait_ge(S("back_ps"), 2 * l + 1)
                nc.vector.tensor_copy(OT[:, 0:2, :].rearrange("p c t -> p (c t)"), ps[:, 5, :]).then_inc(S("gla_out"), 1)
                rwkv_prepare_dve(v, l, I, L)
                rwkv_inverse_dve(v, l, I, L)
                rwkv_chunks_dve(v, l, I, L)
                v.wait_ge(S("back_ps"), 2 * l + 2)
                nc.vector.tensor_copy(OT[:, 2:4, :].rearrange("p c t -> p (c t)"), ps[:, 4, :]).then_inc(S("rw_out"), 1)
                rope_dve(v, l, I, L)
                cmp_dve(v, l, I, L)
                v.wait_ge(S("nsa_gate"), l + 1)
                attention_dve(v, (0, 1, 2), 6 * l, I, L)
                v.wait_ge(S("att_pv"), 16 * (l + 1))
                nc.vector.tensor_copy(OT[:, 4:8, :].rearrange("p c t -> p (c t)"), bank(6, 2)).then_inc(S("nsa_out"), 1)
                if l == 0:
                    v.wait_ge(S("x_loaded"), 16)
                layer_norm_dve(v, 2 * l, 0, ("mix_ready", 2 * (l + 1)), I, L)
                transpose_x_dve(v, 2 * l + 1)
                ffn_dve(v, l)
                layer_norm_dve(v, 2 * l + 1, 4, ("down_ready", 6 * (l + 1)), I, L)
            modulation_dve(v, I, L)
            modulated_dve(v, 0, I, L)
            transpose_x_dve(v, 4)
            lru_dve(v, I, L)
            attention_dve(v, (3,), 12, I, L, sink=SNK)
            v.wait_ge(S("att_pv"), 38)
            merge_dve(v, I, L)
            modulated_dve(v, 1, I, L)
            transpose_x_dve(v, 5)
            router_dve(v, I, L)
            moe_dve(v)
            final_dve(v, I, L)


def slots_of(w, cols):
    k, n = w.shape
    return w.reshape(k // P, P, n // cols, cols).transpose(2, 1, 0, 3).reshape(n // cols, P, SLOT)


def channels(v):
    return np.asarray(v).reshape(-1, P).T


def lay_out(a):
    f = np.float32
    a = {k: np.asarray(v) for k, v in a.items()}
    heads = np.arange(8)
    qperm = np.concatenate([np.arange(HD) + HD * (g * 4 + j) for j in range(4) for g in range(2)])
    stream = np.zeros((N_SLOTS, P, SLOT), f)
    layer = np.zeros((DEPTH, P, LAYER_COLS), f)
    head_norm = np.zeros((DEPTH, 4 * 256), f)

    def put(to, fields, name, value, rows=slice(0, P), at=0):
        x = fields[name][0] + at
        to[rows, x:x + value.shape[1]] = value

    for l in range(DEPTH):
        w = a["w_in"][l]
        gla, rw, nsa = w[:, :1040], w[:, 1040:2096], w[:, 2096:3400]
        zero = lambda n: np.zeros((D, n), f)
        vres = a["w_in_vres"][l - 1] if l else zero(32)
        kv = [nsa[:, 512 + P * i:512 + P * (i + 1)] for i in range(6)]
        misc = np.concatenate([rw[:, 1024:1056], vres, gla[:, 1024:1040], zero(48)], 1)
        cols = np.concatenate([gla[:, 0:512], rw[:, 0:512], rw[:, 512:768], rw[:, 768:896], rw[:, 896:1024], misc,
                               kv[1], kv[0], kv[2], kv[4], nsa[:, qperm][:, 0:512],
                               kv[3], kv[5], nsa[:, 1280:1304], zero(104), gla[:, 512:1024]], 1)
        s = l * LAYER_SLOTS
        stream[s:s + 7] = slots_of(cols, 512)
        for i, name in enumerate(("nsa_wk1", "nsa_wv1")):
            stream[s + S_CMP + i] = a[name][l].reshape(16, P, 256).transpose(1, 0, 2).reshape(P, SLOT)
        rows = np.concatenate([np.arange(512), 512 + qperm])
        stream[s + S_WO:s + S_GU] = slots_of(a["w_out"][l][rows], 512)
        g, u = (a[n][l].reshape(D, 11, 256) for n in ("ffn_w_gate", "ffn_w_up"))
        stream[s + S_GU:s + S_DN] = slots_of(np.stack([g, u], 2).reshape(D, 11 * 512), 512)
        down = np.zeros((24, P, D), f)
        down[:NF] = a["ffn_w_down"][l].reshape(NF, P, D)
        stream[s + S_DN:s + LAYER_SLOTS] = down.reshape(6, 4, P, D).transpose(0, 2, 1, 3).reshape(6, P, SLOT)
        to = layer[l]
        mu = np.zeros(9 * P, f)
        mu[0:1024], mu[1024:1056] = a["rwkv_mu"][l][0:1024], a["rwkv_mu"][l][1024:1056]
        if l:
            mu[1056:1088] = a["rwkv_mu_vres"][l - 1]
        put(to, LAYER_FIELDS, "mu", channels(mu))
        for field, name in (("b_a", "gla_b_a"), ("w0", "rwkv_w0"), ("a0", "rwkv_a0"), ("k_k", "rwkv_k_k"), ("k_a", "rwkv_k_a")):
            put(to, LAYER_FIELDS, field, channels(a[name][l]))
        rk = np.zeros((2, P, 4), f)
        for h in range(4):
            rk[h // 2, HD * (h % 2):HD * (h % 2 + 1), h] = a["rwkv_r_k"][l][h]
        put(to, LAYER_FIELDS, "r_k", rk.transpose(1, 0, 2).reshape(P, 8))
        put(to, LAYER_FIELDS, "wa", a["rwkv_w2"][l], slice(0, 64))
        put(to, LAYER_FIELDS, "wa", a["rwkv_a2"][l], slice(64, 128))
        put(to, LAYER_FIELDS, "g2", a["rwkv_g2"][l][0:P])
        put(to, LAYER_FIELDS, "misc", a["rwkv_g2"][l][P:160], slice(M_G2, M_G2 + 32))
        if l:
            put(to, LAYER_FIELDS, "misc", a["rwkv_v2"][l - 1], slice(M_VR, M_VR + 32))
            put(to, LAYER_FIELDS, "v0", channels(a["rwkv_v0"][l - 1]))
        put(to, LAYER_FIELDS, "misc", a["gla_w_a2"][l], slice(M_GA, M_GA + 16))
        for field, name in (("wk2", "nsa_wk2"), ("wv2", "nsa_wv2")):
            put(to, LAYER_FIELDS, field, a[name][l].reshape(2, P, HD).transpose(1, 0, 2).reshape(P, P))
        for field, name in (("pos_k", "nsa_pos_k"), ("pos_v", "nsa_pos_v")):
            put(to, LAYER_FIELDS, field, np.concatenate([a[name][l].T] * 2, 0))
        head_norm[l] = np.concatenate([a[n][l] for n in ("gla_ln_w", "gla_ln_b", "rwkv_ln_w", "rwkv_ln_b")])
    stream[S_ADA:S_IN2] = slots_of(a["w_ada_2"][0], 512)
    w = a["w_in_2"][0]
    cols = np.concatenate([w[:, qperm], w[:, 512:640], w[:, 768:1280], w[:, 1280:1792], w[:, 640:768], np.zeros((D, 256), f)], 1)
    stream[S_IN2:S_WO2] = slots_of(cols, 512)
    rows = np.concatenate([qperm, 512 + np.arange(512)])
    stream[S_WO2:S_MOE] = slots_of(a["w_out_2"][0][rows], 512)
    moe = stream[S_MOE:].reshape(NE, ITEM_SLOTS, P, SLOT)
    moe[:, 0:4] = a["w_gu_2"][0].reshape(NE, 4, 2, P, 2 * DE).transpose(0, 1, 3, 2, 4).reshape(NE, 4, P, SLOT)
    moe[:, 4:6] = a["w_down_2"][0].reshape(NE, 2, 4, P, D).transpose(0, 1, 3, 2, 4).reshape(NE, 2, P, SLOT)
    second = np.zeros((P, SECOND_COLS), f)
    F2 = SECOND_FIELDS
    put(second, F2, "c", channels(a["c_2"][0]))
    put(second, F2, "conv_w", a["conv_w_2"][0].reshape(4, 4, P).transpose(2, 1, 0).reshape(P, 16))
    put(second, F2, "conv_b", channels(a["conv_b_2"][0]))
    for field, name in (("rg_a", "w_rg_a_2"), ("rg_x", "w_rg_x_2")):
        for c in range(4):
            for h in range(2):
                put(second, F2, field, a[name][0][2 * c + h], slice(HD * h, HD * (h + 1)), c * P + h * HD)
    put(second, F2, "b_a", channels(a["b_rg_a_2"][0]))
    put(second, F2, "b_x", channels(a["b_rg_x_2"][0]))
    put(second, F2, "lam", channels(a["lru_lambda_2"][0]))
    put(second, F2, "g_attn", channels(a["g_attn_out_2"][0][qperm]))
    put(second, F2, "g_lru", channels(a["g_lru_out_2"][0]))
    put(second, F2, "router", a["w_router_2"][0].reshape(KT, P, NE).transpose(1, 0, 2).reshape(P, KT * NE))
    return {
        "x": a["x"][0], "stream": stream, "layer": layer, "head_norm": head_norm, "second": second,
        "ln": np.stack([a[n][l] for l in range(DEPTH) for n in ("ln1_w", "ln1_b", "ln2_w", "ln2_b")]),
        "b_ada": a["b_ada_2"], "small": np.concatenate([a["b_router_2"][0], a["sinks_2"][0]])[None],
        "gains": np.stack([a["g_mix_2"][0], a["g_ffn_2"][0], a["g_final_2"]]),
        "b_down": a["b_down_2"][0],
        "b_gu": a["b_gu_2"][0].reshape(NE, 2, 2, 512).transpose(0, 2, 1, 3).reshape(2 * NE, 1024),
        "const": constants(),
    }


def kernel(**inputs):
    import concourse.bacc as bacc
    from concourse.bass_utils import run_bass_kernel_spmd

    nc = bacc.Bacc("TRN2", target_bir_lowering=False, num_devices=1)
    arrays = {f"in_{k}": np.ascontiguousarray(v) for k, v in lay_out(inputs).items()}
    dram = {k[3:]: nc.dram_tensor(k, v.shape, F32, kind="ExternalInput").ap() for k, v in arrays.items()}
    dram["out"] = nc.dram_tensor("out_0", (T, D), F32, kind="ExternalOutput").ap()
    program(nc, dram)
    r = run_bass_kernel_spmd(nc, [arrays], core_ids=[0])
    return r.results[0]["out_0"].reshape(1, T, D)
```

```python
from contextlib import ExitStack

import numpy as np

import concourse.bass as bass
from concourse import mybir

F32 = mybir.dt.float32
I32 = mybir.dt.int32
ALU = mybir.AluOpType
ACT = mybir.ActivationFunctionType
AX = mybir.AxisListType

P = 128
T = 256
NT = T // P
D = 1024
KT = D // P
DEPTH = 2
HD = 64
FFN = 2816
NF = FFN // P
ALPHA = float((2 * DEPTH) ** 0.25)
LN_EPS, RWKV_EPS, RMS_EPS = 1e-5, 64e-5, 1e-6
MASK_NEG = -1e30
DECAY = -float(np.exp(np.float32(-0.5)))
GLA_TAU = 16.0
QC = 32
NQC = T // QC
EXP_CAP = 1e17
NE, TOPK = 32, 4
DE = 1024
SLOTS_E = 64
NITEM = NE + T * TOPK // SLOTS_E
MIN_ITEM = T * TOPK // SLOTS_E
LIMIT, SWIGLU_ALPHA = 7.0, 1.702
LRU_C = 8.0
GELU_C, GELU_K = 0.7978845608028654, 0.044715

SLOT = 4096
RING = 4
S_IN, S_CMP, S_WO, S_GU, S_DN = 0, 7, 9, 11, 22
LAYER_SLOTS = 28
S_ADA = DEPTH * LAYER_SLOTS
S_IN2 = S_ADA + 12
S_WO2 = S_IN2 + 4
S_MOE = S_WO2 + 2
ITEM_SLOTS = 6
N_SLOTS = S_MOE + ITEM_SLOTS * NE
assert (2 * ITEM_SLOTS) % RING == 0

T_GQ, T_GK, T_R, T_K, T_V, T_WA, T_G1, T_MISC, T_VC, T_KC, T_KS, T_KW, T_Q = 0, 2, 4, 6, 8, 10, 11, 12, 13, 14, 15, 16, 17
NCT = 21
M_G2, M_VR, M_GA = 0, 32, 64


def layout(fields):
    at, offsets = 0, {}
    for name, width in fields:
        offsets[name] = (at, at + width)
        at += width
    return offsets, at


LAYER_FIELDS, LAYER_COLS = layout([
    ("mu", 9), ("b_a", 2), ("w0", 2), ("a0", 2), ("v0", 2), ("k_k", 2), ("k_a", 2), ("r_k", 8),
    ("wa", 256), ("g2", 256), ("misc", 256), ("wk2", 128), ("wv2", 128), ("pos_k", 32), ("pos_v", 32)])
SECOND_FIELDS, SECOND_COLS = layout([
    ("c", 8), ("conv_w", 16), ("conv_b", 4), ("rg_a", 512), ("rg_x", 512), ("b_a", 4), ("b_x", 4), ("lam", 4),
    ("g_attn", 4), ("g_lru", 4), ("router", 8 * NE)])
CONST_FIELDS, CONST_COLS = layout([
    ("ident", P), ("diag_add", P), ("prev_add", P), ("pairs", 4 * P), ("levels", 7 * P), ("ones", T),
    ("head_ones", P), ("rot", P), ("cos", T), ("sin", T), ("iota", P), ("cmp_add", 30), ("cmp_any", 2)])


def constants():
    f = np.float32
    c = {}
    i, j = np.arange(P)[:, None], np.arange(P)[None, :]
    c["ident"] = (i == j).astype(f)
    c["diag_add"] = np.where(j <= i, 0, MASK_NEG).astype(f)
    c["prev_add"] = np.where(j > i, 0, MASK_NEG).astype(f)
    strict, incl = (i < j).astype(f), (i <= j).astype(f)
    c["pairs"] = np.concatenate([strict, incl, strict, incl], 1)
    level = []
    for n in range(7):
        b = 1 << n
        level.append(((i // (2 * b) == j // (2 * b)) & (i // b % 2 == 0) & (j // b % 2 == 1)).astype(f))
    c["levels"] = np.concatenate(level, 1)
    c["ones"] = np.ones((P, T), f)
    c["head_ones"] = (i // HD == j // HD).astype(f)
    half = HD // 2
    rot = np.zeros((P, P), f)
    for m in range(P):
        if m % HD < half:
            rot[m + half, m] = -1
        else:
            rot[m - half, m] = 1
    c["rot"] = rot
    inv = (f(10000.0) ** (-np.arange(half, dtype=f) / f(half))).astype(f)
    ang = (np.arange(T, dtype=f)[:, None] * inv).astype(f)
    row = np.arange(P) % half
    c["cos"], c["sin"] = np.cos(ang).astype(f).T[row], np.sin(ang).astype(f).T[row]
    c["iota"] = np.broadcast_to(np.arange(P, dtype=f), (P, P))
    pos = np.arange(P)[:, None, None] + P * np.arange(NT)[None, :, None]
    seen = 16 * np.arange(15)[None, None, :] + 31 <= pos
    c["cmp_add"] = np.where(seen, 0, MASK_NEG).astype(f).reshape(P, 30)
    c["cmp_any"] = seen.any(-1).astype(f)
    out = np.zeros((P, CONST_COLS), f)
    for name, (a, b) in CONST_FIELDS.items():
        out[:, a:b] = c[name]
    return out


def program(nc, dram):
    ctx = ExitStack()
    with ctx:
        def sb(name, shape, dt=F32):
            return ctx.enter_context(nc.sbuf_tensor(name, shape, dt))

        sems = {}

        def S(name):
            if name not in sems:
                sems[name] = ctx.enter_context(nc.semaphore(name))
            return sems[name]

        ring = sb("ring", [P, RING, SLOT])
        X = sb("X", [P, NT, D])
        XT = sb("XT", [P, KT, T])
        OT = XT
        HT = sb("HT", [P, NF, T])
        TOK = sb("TOK", [P, NT, 512])
        NV = sb("NV", [P, NT, 280])
        CST = sb("CST", [P, CONST_COLS])
        PAR = sb("PAR", [P, max(LAYER_COLS, SECOND_COLS)])
        HN = sb("HN", [P, 4, 256])
        VF = sb("VF", [P, 2, T])
        SA = sb("SA", [P, 5120])
        SB = sb("SB", [P, 14336])
        SM = sb("SM", [P, 176])
        ps = ctx.enter_context(nc.psum_tensor("ps", [P, 8, 512], F32))

        ITI = SA[:, 5056:5056 + 8 + NITEM].bitcast(I32)

        def cst(name):
            a, b = CONST_FIELDS[name]
            return CST[:, a:b]

        def par(name, fields=LAYER_FIELDS):
            a, b = fields[name]
            return PAR[:, a:b]

        def par2(name):
            return par(name, SECOND_FIELDS)

        def view(region, at, shape):
            n = int(np.prod(shape))
            v = region[:, at:at + n]
            if len(shape) == 2:
                v = v.rearrange("p (a b) -> p a b", a=shape[0])
            elif len(shape) == 3:
                v = v.rearrange("p (a b c) -> p a b c", a=shape[0], b=shape[1])
            elif len(shape) == 4:
                v = v.rearrange("p (a b c d) -> p a b c d", a=shape[0], b=shape[1], c=shape[2])
            return v

        def bank(b, n=1):
            return ps[:, b:b + n, :].rearrange("p a n -> p (a n)")

        ident = cst("ident")
        LNW, LNB = view(SB, 0, [D]), view(SB, D, [D])
        SQ = view(SB, 2 * D, [D])
        arrived = [S(f"slot_arrived{b}") for b in range(RING)]

        def slot(i):
            return ring[:, i % RING, :]

        def need_slot(eng, i):
            eng.wait_ge(arrived[i % RING], 16 * (i // RING + 1))

        def released(i):
            if i < S_ADA:
                l, s = divmod(i, LAYER_SLOTS)
                if s < S_CMP:
                    return "proj_ready", 15 * l + [2, 4, 6, 8, 10, 13, 15][s]
                if s < S_WO:
                    return "cmp_hidden", l + 1
                if s < S_GU:
                    return "mix_ready", 2 * l + s - S_WO + 1
                if s < S_DN:
                    return "ffn_ready", 11 * l + s - S_GU + 1
                return "down_ready", 6 * l + s - S_DN + 1
            if i < S_IN2:
                return "mod_ready", i - S_ADA + 1
            if i < S_WO2:
                return "proj2_ready", [2, 4, 6, 8][i - S_IN2]
            return "mix2_ready", i - S_WO2 + 1

        def link(eng, name):
            n = [0]

            def step(ins):
                n[0] += 1
                ins.then_inc(S(name), 1)

            def joined(ins):
                step(ins)
                eng.wait_ge(S(name), n[0])
            return step, joined

        def stream(sp, i):
            if i >= RING:
                name, value = released(i - RING)
                sp.wait_ge(S(name), value)
            sp.dma_start(slot(i), dram["stream"][i]).then_inc(arrived[i % RING], 16)

        def layer_params(sp, l):
            if l:
                for done in ("gla_out", "rw_out", "nsa_out"):
                    sp.wait_ge(S(done), l)
            sp.dma_start(PAR[:, 0:LAYER_COLS], dram["layer"][l]).then_inc(S("par_loaded"), 16)
            sp.dma_start(HN[:].rearrange("p a b -> p (a b)"),
                         dram["head_norm"][l:l + 1, :].broadcast_to([P, 1024])).then_inc(S("hn_loaded"), 16)

        def norm_params(sp, n):
            if n % 2:
                sp.wait_ge(S("x_ready"), n)
            else:
                sp.wait_ge(S("mix_ready"), n + 1)
            sp.dma_start(LNW, dram["ln"][2 * n:2 * n + 1, :].broadcast_to([P, D])).then_inc(S("ln_loaded"), 16)
            sp.dma_start(LNB, dram["ln"][2 * n + 1:2 * n + 2, :].broadcast_to([P, D])).then_inc(S("ln_loaded"), 16)

        def first_sp(sp):
            sp.dma_start(X[:], dram["x"].rearrange("(t p) d -> p t d", p=P)).then_inc(S("x_loaded"), 16)
            sp.dma_start(CST[:], dram["const"]).then_inc(S("const_loaded"), 16)
            for l in range(DEPTH):
                for s in range(LAYER_SLOTS):
                    stream(sp, l * LAYER_SLOTS + s)
                    if l == 0 and s == 1:
                        layer_params(sp, 0)
                    if s == S_WO + RING:
                        norm_params(sp, 2 * l)
                    if s == S_GU + 8:
                        norm_params(sp, 2 * l + 1)
                        if l + 1 < DEPTH:
                            layer_params(sp, l + 1)

        def transpose_x_pe(pe, n, src, ready):
            pe.wait_ge(S(ready[0]), ready[1])
            for b in range(4):
                for k in range(2):
                    for t in range(NT):
                        m = pe.transpose(ps[:, 4 + b, (k * NT + t) * P:(k * NT + t + 1) * P],
                                         src[:, t, (2 * b + k) * P:(2 * b + k + 1) * P], ident)
                m.then_inc(S("xt_ps"), 1)

        def transpose_x_dve(v, n):
            for b in range(4):
                v.wait_ge(S("xt_ps"), 4 * n + b + 1)
                nc.vector.tensor_copy(XT[:, 2 * b:2 * b + 2, :].rearrange("p k t -> p (k t)"),
                                      ps[:, 4 + b, :]).then_inc(S("xt_ready"), 1)

        def proj_bank(g):
            return g % 4 if g < 13 else g - 9

        def project_pe(pe, l, slots):
            base = l * LAYER_SLOTS
            pe.wait_ge(S("xt_ready"), 4 * (2 * l + 1))

            def bank_free(g):
                if g >= 13:
                    pe.wait_ge(S("gla_zb"), l + 1)
                    pe.wait_ge(S("rw_gates"), l + 1)
                elif g >= 4:
                    pe.wait_ge(S("proj_evac"), 15 * l + g - 3)

            for s in slots:
                need_slot(pe, base + s)
                w = slot(base + s).rearrange("p (k n) -> p k n", k=KT)
                if s < 5:
                    for g in (2 * s, 2 * s + 1):
                        bank_free(g)
                        for j in range(2):
                            for k in range(KT):
                                m = pe.matmul(ps[:, proj_bank(g), j * T:(j + 1) * T],
                                              w[:, k, (2 * (g % 2) + j) * P:(2 * (g % 2) + j + 1) * P],
                                              XT[:, k, :], start=k == 0, stop=k == KT - 1)
                        m.then_inc(S("proj_ready"), 1)
                    continue
                if s == 5:
                    bank_free(10)
                    for k in range(KT):
                        m = pe.matmul(ps[:, proj_bank(10), 0:T], w[:, k, 0:P], XT[:, k, :], start=k == 0, stop=k == KT - 1)
                    m.then_inc(S("proj_ready"), 1)
                a, n, g0 = (P, 280, 11) if s == 5 else (0, 512, 13)
                for t in range(NT):
                    bank_free(g0 + t)
                    for k in range(KT):
                        m = pe.matmul(ps[:, proj_bank(g0 + t), 0:n], XT[:, k, t * P:(t + 1) * P], w[:, k, a:a + n],
                                      start=k == 0, stop=k == KT - 1)
                    m.then_inc(S("proj_ready"), 1)

        def project_act(act, l, groups):
            for g in groups:
                act.wait_ge(S("proj_ready"), 15 * l + g + 1)
                if g < 10:
                    to, n = HT[:, 2 * g:2 * g + 2, :].rearrange("p a t -> p (a t)"), 512
                elif g == 10:
                    to, n = HT[:, 20, :], T
                elif g < 13:
                    to, n = NV[:, g - 11, :], 280
                else:
                    to, n = TOK[:, g - 13, :], 512
                nc.scalar.activation(to, ps[:, proj_bank(g), 0:n], ACT.Copy,
                                     scale=HD ** -0.5 if g == 0 else 1.0).then_inc(S("proj_evac"), 1)

        def mix_dve(v, l, I, L):
            v.wait_ge(S("proj_evac"), 15 * l + 7)
            v.wait_ge(S("par_loaded"), 16 * (l + 1))
            HX = HT[:, T_R:T_MISC + 1, :]
            MD = view(SB, 0, [9, T])
            I(nc.vector.tensor_tensor(MD[:, :, 1:T], HX[:, :, 0:T - 1], HX[:, :, 1:T], ALU.subtract))
            L(nc.vector.tensor_scalar(MD[:, :, 0:1], HX[:, :, 0:1], -1.0, None, ALU.mult))
            for j in range(9):
                ins = nc.vector.scalar_tensor_tensor(out=HX[:, j, :], in0=MD[:, j, :], scalar=par("mu")[:, j:j + 1],
                                                     in1=HX[:, j, :], op0=ALU.mult, op1=ALU.add)
                if j < 8:
                    I(ins)
            ins.then_inc(S("mixed"), 1)
            v.wait_ge(S("mixed"), l + 1)

        def head_norm_dve(v, I, L, src, eps, which, n, XC, SQ2):
            s8, v8, d8, r8 = (SM[:, 8 * i:8 * i + 8] for i in range(4))
            X8 = XC.rearrange("p (a b) -> p a b", b=HD)
            L(nc.vector.tensor_reduce(s8, src, AX.X, ALU.add))
            L(nc.vector.tensor_scalar(s8, s8, 1.0 / HD, None, ALU.mult))
            L(nc.vector.tensor_tensor(X8, src, s8.unsqueeze(2).broadcast_to([P, 8, HD]), ALU.subtract))
            L(nc.vector.tensor_tensor(SQ2, XC, XC, ALU.mult))
            L(nc.vector.tensor_reduce(v8, SQ2.rearrange("p (a b) -> p a b", b=HD), AX.X, ALU.add))
            nc.vector.tensor_scalar(v8, v8, 1.0 / HD, eps, ALU.mult, ALU.add).then_inc(S("head_var"), 1)
            v.wait_ge(S("head_std"), n + 1)
            L(nc.vector.reciprocal(r8, d8))
            L(nc.vector.tensor_tensor(X8, X8, r8.unsqueeze(2).broadcast_to([P, 8, HD]), ALU.mult))
            X2 = XC.rearrange("p (t c) -> p t c", t=NT)
            v.wait_ge(S("hn_loaded"), 16 * (n // 2 + 1))
            L(nc.vector.tensor_tensor(X2, X2, HN[:, which:which + 1, :].broadcast_to([P, NT, 256]), ALU.mult))
            L(nc.vector.tensor_tensor(X2, X2, HN[:, which + 1:which + 2, :].broadcast_to([P, NT, 256]), ALU.add))

        def head_norm_act(act, n):
            act.wait_ge(S("head_var"), n + 1)
            nc.scalar.activation(SM[:, 16:24], SM[:, 8:16], ACT.Sqrt).then_inc(S("head_std"), 1)

        G_LB, G_T0, G_T1 = view(SA, 0, [2, T]), view(SA, 512, [2, T]), view(SA, 1024, [2, T])
        G_EK = [view(SA, 1536 + 512 * i, [2, T]) for i in range(2)]
        G_KH = [view(SA, 2560 + 512 * i, [2, T]) for i in range(2)]
        G_ST = view(SA, 3584, [4, 384])

        def gla_gate_pe(pe, l):
            pe.wait_ge(S("mixed"), l + 1)
            for c in range(2):
                m = pe.matmul(ps[:, 4, c * T:(c + 1) * T], par("misc")[M_GA:M_GA + 16, c * P:(c + 1) * P],
                              HT[M_GA:M_GA + 16, T_MISC, :], start=True, stop=True)
            m.then_inc(S("gla_z"), 1)

        def gla_scores_pe(pe, l, tc):
            pe.wait_ge(S("gla_k"), NQC * l + tc + 1)
            if tc == 0:
                pe.wait_ge(S("proj_evac"), 15 * l + 13)
            for h in range(4):
                c, pb = h // 2, HD * (h % 2)
                for st in range(tc * QC // P + 1):
                    at = tc * QC if st == 0 else T + tc * QC - P
                    m = pe.matmul(ps[:, h, at:at + QC], G_KH[tc % 2][pb:pb + HD, c, st * P:(st + 1) * P],
                                  HT[pb:pb + HD, T_GQ + c, tc * QC:(tc + 1) * QC], start=True, stop=True)
            m.then_inc(S("gla_sc"), 1)

        def gla_out_pe(pe, l):
            pe.wait_ge(S("gla_st"), 3 * (l + 1))
            pe.wait_ge(S("proj_evac"), 15 * (l + 1))
            pe.wait_ge(S("rw_init"), l + 1)
            for t in range(NT):
                for h in range(4):
                    for s in range(t + 1):
                        at = t * P if s == 0 else T
                        m = pe.matmul(ps[:, 4, (4 * t + h) * HD:(4 * t + h + 1) * HD], G_ST[:, h, at:at + P],
                                      TOK[:, s, h * HD:(h + 1) * HD], start=s == 0, stop=s == t)
            m.then_inc(S("gla_o"), 1)

        def back_pe(pe, n, XC, b):
            pe.wait_ge(S("head_out"), n + 1)
            X2 = XC.rearrange("p (t c) -> p t c", t=NT)
            for c in range(2):
                for t in range(NT):
                    m = pe.transpose(ps[:, b, c * T + t * P:c * T + (t + 1) * P], X2[:, t, c * P:(c + 1) * P], ident)
            m.then_inc(S("back_ps"), 1)

        def gla_decay_act(act, l, L):
            act.wait_ge(S("gla_zb"), l + 1)
            L(nc.scalar.activation(G_T0, G_T1, ACT.Abs))
            L(nc.scalar.activation(G_T0, G_T0, ACT.Exp, scale=-1.0))
            nc.scalar.activation(G_T0, G_T0, ACT.Ln, bias=cst("ones")[:, 0:1]).then_inc(S("gla_lp"), 1)

        def gla_query_act(act, l):
            act.wait_ge(S("gla_df"), l + 1)
            nc.scalar.activation(G_T0, G_T1, ACT.Exp).then_inc(S("gla_eq"), 1)

        def gla_key_act(act, l, tc):
            if tc >= 2:
                act.wait_ge(S("gla_k"), NQC * l + tc - 1)
            w, ref = (tc * QC // P + 1) * P, tc * QC + QC // 2 - 1
            for c in range(2):
                nc.scalar.activation(G_EK[tc % 2][:, c, 0:w], G_LB[:, c, 0:w], ACT.Exp, scale=-1.0,
                                     bias=G_LB[:, c, ref:ref + 1]).then_inc(S("gla_ek"), 1)

        def gla_decay_dve(v, l, I, L):
            v.wait_ge(S("gla_z"), l + 1)
            for c in range(2):
                ins = nc.vector.tensor_scalar(G_T1[:, c, :], ps[:, 4, c * T:(c + 1) * T], par("b_a")[:, c:c + 1], None, ALU.add)
                if c == 0:
                    I(ins)
            ins.then_inc(S("gla_zb"), 1)
            v.wait_ge(S("gla_zb"), l + 1)
            v.wait_ge(S("gla_lp"), l + 1)
            L(nc.vector.scalar_tensor_tensor(out=G_T1, in0=G_T1, scalar=0.0, in1=G_T0, op0=ALU.min, op1=ALU.subtract))
            for c in range(2):
                (I if c == 0 else L)(nc.vector.tensor_tensor_scan(G_LB[:, c, :], cst("ones"), G_T1[:, c, :], 0.0,
                                                                  ALU.mult, ALU.add))
            L(nc.vector.tensor_scalar(G_LB, G_LB, 1.0 / GLA_TAU, None, ALU.mult))
            lb4 = G_LB.rearrange("p c (n q) -> p (c n) q", q=QC)
            t14 = G_T1.rearrange("p c (n q) -> p (c n) q", q=QC)
            nc.vector.tensor_tensor(t14, lb4, lb4[:, :, QC // 2 - 1:QC // 2].broadcast_to([P, 2 * NQC, QC]),
                                    ALU.subtract).then_inc(S("gla_df"), 1)
            v.wait_ge(S("gla_eq"), l + 1)
            q = HT[:, T_GQ:T_GQ + 2, :]
            nc.vector.scalar_tensor_tensor(out=q, in0=G_T0, scalar=EXP_CAP, in1=q, op0=ALU.min,
                                           op1=ALU.mult).then_inc(S("gla_q"), 1)

        def gla_key_dve(v, l, tc):
            v.wait_ge(S("gla_ek"), 2 * NQC * l + 2 * tc + 2)
            if tc >= 2:
                v.wait_ge(S("gla_sc"), NQC * l + tc - 1)
            w = (tc * QC // P + 1) * P
            nc.vector.scalar_tensor_tensor(out=G_KH[tc % 2][:, :, 0:w], in0=G_EK[tc % 2][:, :, 0:w], scalar=EXP_CAP,
                                           in1=HT[:, T_GK:T_GK + 2, 0:w], op0=ALU.min, op1=ALU.mult).then_inc(S("gla_k"), 1)

        def gla_mask_dve(v, l):
            v.wait_ge(S("gla_sc"), NQC * (l + 1))
            incl = cst("pairs")[:, P:2 * P].unsqueeze(1).broadcast_to([P, 4, P])
            nc.vector.tensor_tensor(G_ST[:, :, 0:P], ps[:, 0:4, 0:P], incl, ALU.mult).then_inc(S("gla_st"), 1)
            nc.vector.tensor_copy(G_ST[:, :, P:T], ps[:, 0:4, P:T]).then_inc(S("gla_st"), 1)
            nc.vector.tensor_tensor(G_ST[:, :, T:T + P], ps[:, 0:4, T:T + P], incl, ALU.mult).then_inc(S("gla_st"), 1)

        G_XC, G_SQ, G_SG = view(SA, 1536, [512]), view(SA, 2048, [512]), view(SA, 512, [512])

        def gla_norm_dve(v, l, I, L):
            v.wait_ge(S("gla_o"), l + 1)
            head_norm_dve(v, I, L, ps[:, 4, :].rearrange("p (a b) -> p a b", b=HD), LN_EPS, 0, 2 * l, G_XC, G_SQ)
            v.wait_ge(S("gla_sg"), l + 1)
            sg, xc = (a.rearrange("p (t c) -> p t c", t=NT) for a in (G_SG, G_XC))
            L(nc.vector.tensor_tensor(sg, sg, TOK[:, :, 256:512], ALU.mult))
            nc.vector.tensor_tensor(xc, xc, sg, ALU.mult).then_inc(S("head_out"), 1)

        def gla_gate_act(act, l):
            act.wait_ge(S("gla_st"), 3 * (l + 1))
            nc.scalar.activation(G_SG.rearrange("p (t c) -> p t c", t=NT), TOK[:, :, 256:512],
                                 ACT.Sigmoid).then_inc(S("gla_sg"), 1)

        MM = view(SB, 0, [8, 4, P])
        TM, TT = view(SB, 4096, [8, P]), view(SB, 5120, [8, P])
        ZM, MK = view(SB, 6144, [8, P]), view(SB, 7168, [8, P])
        E1, E2, E3 = (view(SB, 6144 + 512 * i, [2, T]) for i in range(3))
        DM, DM1 = view(SB, 4096, [2, T]), view(SB, 4608, [2, T])
        LW, AA, KK = (view(SB, 8192 + 512 * i, [2, T]) for i in range(3))
        XU, US = view(SB, 8704, [256]), view(SB, 8960, [256])
        RK = view(SB, 9216, [2, T])
        AR = view(SB, 9728, [2, 2, 2, P])
        BT, KTL = view(SB, 10752, [2, T]), view(SB, 11264, [2, T])
        SV = view(SB, 11776, [2, T])
        BK = view(SB, 11776, [2, 256])
        VT, GT = view(SB, 12288, [2, 256]), view(SB, 12800, [2, 256])
        S0 = view(SB, 13440, [2, 2, HD])
        LC = view(SB, 13440, [2, T])
        SCL = SM[:, 40:42]
        R_XC, R_SQ = view(SB, 9728, [512]), view(SB, 10240, [512])

        def rwkv_ranks_act(act, l, I):
            act.wait_ge(S("mixed"), l + 1)
            I(nc.scalar.activation(HT[0:64, T_WA, :], HT[0:64, T_WA, :], ACT.Tanh))
            I(nc.scalar.activation(HT[:, T_G1, :], HT[:, T_G1, :], ACT.Sigmoid))
            nc.scalar.activation(HT[0:32, T_MISC, :], HT[0:32, T_MISC, :], ACT.Sigmoid).then_inc(S("rw_rank"), 1)

        def rwkv_ranks_pe(pe, l):
            pe.wait_ge(S("rw_rank"), l + 1)
            for b, r0 in ((6, 0), (7, 64)):
                for c in range(2):
                    pe.matmul(ps[:, b, c * T:(c + 1) * T], par("wa")[r0:r0 + 64, c * P:(c + 1) * P],
                              HT[r0:r0 + 64, T_WA, :], start=True, stop=True)
            if l:
                pe.wait_ge(S("gla_zb"), l + 1)
                for c in range(2):
                    pe.matmul(ps[:, 4, c * T:(c + 1) * T], par("misc")[M_VR:M_VR + 32, c * P:(c + 1) * P],
                              HT[M_VR:M_VR + 32, T_MISC, :], start=True, stop=True)
            for t in range(NT):
                pe.matmul(ps[:, 5, t * T:(t + 1) * T], HT[:, T_G1, t * P:(t + 1) * P], par("g2"), start=True, stop=False)
                m = pe.matmul(ps[:, 5, t * T:(t + 1) * T], HT[0:32, T_MISC, t * P:(t + 1) * P], par("misc")[0:32, :],
                              start=False, stop=True)
            m.then_inc(S("rw_z"), 1)

        def rwkv_gates_act(act, l, I):
            act.wait_ge(S("rw_z"), l + 1)
            for b, to, bias in ((6, LW, "w0"), (7, AA, "a0")) + (((4, SV, "v0"),) if l else ()):
                for c in range(2):
                    ins = nc.scalar.activation(to[:, c, :], ps[:, b, c * T:(c + 1) * T], ACT.Sigmoid,
                                               bias=par(bias)[:, c:c + 1])
                    I(ins)
            nc.scalar.activation(GT, ps[:, 5, :].rearrange("p (t c) -> p t c", t=NT), ACT.Copy).then_inc(S("rw_gates"), 1)

        def rwkv_square_dve(v, l, I, L):
            HK = HT[:, T_K:T_K + 2, :]
            for c in range(2):
                (I if c == 0 else L)(nc.vector.tensor_scalar(KK[:, c, :], HK[:, c, :], par("k_k")[:, c:c + 1], None, ALU.mult))
            nc.vector.tensor_tensor(RK_SQ, KK, KK, ALU.mult).then_inc(S("rw_sq"), 1)

        def rwkv_prepare_dve(v, l, I, L):
            HK, HR, HV = HT[:, T_K:T_K + 2, :], HT[:, T_R:T_R + 2, :], HT[:, T_V:T_V + 2, :]
            v.wait_ge(S("rw_gates"), l + 1)
            if l == 0:
                nc.vector.tensor_copy(VF[:], HV).then_inc(S("rw_v"), 1)
            else:
                L(nc.vector.tensor_tensor(DM, VF[:], HV, ALU.subtract))
                L(nc.vector.tensor_tensor(DM, DM, SV, ALU.mult))
                nc.vector.tensor_tensor(HV, HV, DM, ALU.add).then_inc(S("rw_v"), 1)
                v.wait_ge(S("rw_v"), l + 1)
            for c in range(2):
                (I if c == 0 else L)(nc.vector.tensor_scalar(DM1[:, c, :], AA[:, c, :], 1.0, par("k_a")[:, c:c + 1],
                                                             ALU.subtract, ALU.mult))
            L(nc.vector.scalar_tensor_tensor(out=HK, in0=DM1, scalar=1.0, in1=HK, op0=ALU.add, op1=ALU.mult))
            for c in range(2):
                for j in range(2):
                    L(nc.vector.tensor_tensor_scan(LC[:, c, j * P:(j + 1) * P], cst("ones")[:, 0:P],
                                                   LW[:, c, j * P:(j + 1) * P], 0.0, ALU.mult, ALU.add))
            lc4, dm4 = (a.rearrange("p c (j s) -> p (c j) s", j=2) for a in (LC, DM))
            L(nc.vector.tensor_tensor(dm4, lc4, lc4[:, :, 63:64].broadcast_to([P, 4, P]), ALU.subtract))
            I(nc.vector.tensor_tensor(SCL.unsqueeze(2), DM[:, :, 127:128], LC[:, :, P + 63:P + 64], ALU.add))
            nc.vector.tensor_tensor(DM1, DM, LW, ALU.subtract).then_inc(S("rw_dm"), 1)
            v.wait_ge(S("rw_ss"), l + 1)
            nc.vector.tensor_scalar(RK_SQ.rearrange("p c t -> p (c t)"), ps[:, 6, :], 1e-24, None,
                                    ALU.max).then_inc(S("rw_ssm"), 1)
            v.wait_ge(S("rw_norm"), l + 1)
            L(nc.vector.reciprocal(RK_SQ, RK_SQ))
            L(nc.vector.tensor_tensor(KK, KK, RK_SQ, ALU.mult))
            ar = AR.rearrange("p c j w s -> p (c j) w s")
            f4 = lambda a: a.rearrange("p c (j s) -> p (c j) s", j=2)
            I(nc.vector.scalar_tensor_tensor(out=ar[:, :, 0, :], in0=f4(KK), scalar=-1.0, in1=f4(E3), op0=ALU.mult, op1=ALU.mult))
            I(nc.vector.tensor_tensor(ar[:, :, 1, :], f4(HR), f4(E1), ALU.mult))
            L(nc.vector.tensor_tensor(BT, KK, AA, ALU.mult))
            I(nc.vector.tensor_tensor(BT, BT, E2, ALU.mult))
            I(nc.vector.tensor_tensor(RK, HR, HK, ALU.mult))
            nc.vector.tensor_tensor(KTL, HK, E2, ALU.mult).then_inc(S("rw_ops"), 1)

        RK_SQ = view(SB, 10240, [2, T])

        def rwkv_decay_act(act, l, I):
            act.wait_ge(S("rw_dm"), l + 1)
            I(nc.scalar.activation(E1, DM, ACT.Exp, scale=DECAY))
            I(nc.scalar.activation(E2, DM, ACT.Exp, scale=-DECAY))
            I(nc.scalar.activation(E3, DM1, ACT.Exp, scale=DECAY))
            I(nc.scalar.activation(SCL, SCL, ACT.Exp, scale=DECAY))
            act.wait_ge(S("rw_ssm"), l + 1)
            nc.scalar.activation(RK_SQ, RK_SQ, ACT.Sqrt).then_inc(S("rw_norm"), 1)

        def rwkv_norm_pe(pe, l):
            pe.wait_ge(S("rw_sq"), l + 1)
            pe.wait_ge(S("rw_gates"), l + 1)
            m = pe.matmul(ps[:, 6, :], cst("head_ones"), RK_SQ.rearrange("p c t -> p (c t)"), start=True, stop=True)
            m.then_inc(S("rw_ss"), 1)
            pe.wait_ge(S("rw_v"), l + 1)
            for t in range(NT):
                for c in range(2):
                    m = pe.transpose(ps[:, 7, t * T + c * P:t * T + (c + 1) * P], HT[:, T_V + c, t * P:(t + 1) * P], ident)
            m.then_inc(S("rw_vt_ps"), 1)

        def rwkv_values_act(act, l):
            act.wait_ge(S("rw_vt_ps"), l + 1)
            nc.scalar.activation(VT, ps[:, 7, :].rearrange("p (t c) -> p t c", t=NT), ACT.Copy).then_inc(S("rw_vt"), 1)

        def rwkv_bonus_pe(pe, l):
            pe.wait_ge(S("rw_ops"), l + 1)
            pe.wait_ge(S("rw_vt"), l + 1)
            for i, (tl, c) in enumerate((a, c) for a in (BT, KTL) for c in range(2)):
                m = pe.transpose(ps[:, 7, i * P:(i + 1) * P], tl[:, c, 0:P], ident)
            m.then_inc(S("rw_bk_ps"), 1)
            pe.wait_ge(S("proj_evac"), 15 * (l + 1))
            for t in range(NT):
                for c in range(2):
                    m = pe.matmul(ps[:, 4, 4 * t:4 * t + 4], RK[:, c, t * P:(t + 1) * P], par("r_k")[:, 4 * c:4 * c + 4],
                                  start=c == 0, stop=c == 1)
            m.then_inc(S("rw_bonus"), 1)

        def rwkv_pairs_pe(pe, l, u):
            j, h = divmod(u, 4)
            c, pb = h // 2, HD * (h % 2)
            if u >= 2:
                pe.wait_ge(S("rw_mm"), 8 * l + u - 1)
            rhs = AR[pb:pb + HD, c, j, :, :].rearrange("p w s -> p (w s)")
            for w, tl in enumerate((BT, KTL)):
                m = pe.matmul(ps[:, 5 + u % 2, w * 256:(w + 1) * 256], tl[pb:pb + HD, c, j * P:(j + 1) * P], rhs,
                              start=True, stop=True)
            m.then_inc(S("rw_pairs"), 1)

        def rwkv_bk_act(act, l):
            act.wait_ge(S("rw_bk_ps"), l + 1)
            nc.scalar.activation(BK, ps[:, 7, :].rearrange("p (t c) -> p t c", t=2), ACT.Copy).then_inc(S("rw_bk"), 1)

        def rwkv_init_dve(v, l, I, L):
            v.wait_ge(S("rw_bonus"), l + 1)
            I(nc.vector.memset(S0, 0.0))
            L(nc.vector.tensor_copy(SM[:, 32:40], ps[:, 4, 0:8]))
            idb = ident.unsqueeze(1).broadcast_to([P, 8, P])
            I(nc.vector.tensor_copy(TM, idb))
            nc.vector.tensor_copy(TT, idb).then_inc(S("rw_init"), 1)

        def rwkv_mask_dve(v, l, u):
            v.wait_ge(S("rw_pairs"), 8 * l + u + 1)
            nc.vector.tensor_tensor(MM[:, u, :, :].rearrange("p a s -> p (a s)"), ps[:, 5 + u % 2, :], cst("pairs"),
                                    ALU.mult).then_inc(S("rw_mm"), 1)

        def inverse_level_dve(v, l, s):
            n, us = s // 2, slice(4 * (s % 2), 4 * (s % 2) + 4)
            if s >= 2:
                v.wait_ge(S("rw_z_ps"), 14 * l + s - 1)
            lev = cst("levels")[:, n * P:(n + 1) * P].unsqueeze(1).broadcast_to([P, 4, P])
            nc.vector.tensor_tensor(MK[:, us, :], MM[:, us, 0, :], lev, ALU.mult).then_inc(S("rw_mk"), 1)

        def inverse_update_dve(v, l, s):
            us = slice(4 * (s % 2), 4 * (s % 2) + 4)
            v.wait_ge(S("rw_dt"), 14 * l + s + 1)
            if s >= 2:
                v.wait_ge(S("rw_tm"), 28 * l + 2 * s - 2)
            for to, b in ((TM, 6), (TT, 7)):
                nc.vector.tensor_tensor(to[:, us, :], to[:, us, :], ps[:, b, :].rearrange("p (u s) -> p u s", u=4),
                                        ALU.add).then_inc(S("rw_tm"), 1)

        def inverse_product_pe(pe, l, s):
            if s == 0:
                pe.wait_ge(S("rw_init"), l + 1)
                pe.wait_ge(S("rw_bk"), l + 1)
            pe.wait_ge(S("rw_mk"), 14 * l + s + 1)
            if s:
                pe.wait_ge(S("rw_zc"), 14 * l + s)
            if s >= 2:
                pe.wait_ge(S("rw_tm"), 28 * l + 2 * (s - 1))
            for i in range(4):
                u = 4 * (s % 2) + i
                m = pe.matmul(ps[:, 5, i * P:(i + 1) * P], MK[:, u, :], TM[:, u, :], start=True, stop=True)
            m.then_inc(S("rw_z_ps"), 1)

        def inverse_update_pe(pe, l, s):
            pe.wait_ge(S("rw_zc"), 14 * l + s + 1)
            if s:
                pe.wait_ge(S("rw_tm"), 28 * l + 2 * s)
            for i in range(4):
                u = 4 * (s % 2) + i
                pe.matmul(ps[:, 6, i * P:(i + 1) * P], TT[:, u, :], ZM[:, u, :], start=True, stop=True)
            for i in range(4):
                u = 4 * (s % 2) + i
                m = pe.matmul(ps[:, 7, i * P:(i + 1) * P], ZM[:, u, :], TT[:, u, :], start=True, stop=True)
            m.then_inc(S("rw_dt"), 1)

        def inverse_product_act(act, l, s):
            act.wait_ge(S("rw_z_ps"), 14 * l + s + 1)
            if s >= 2:
                act.wait_ge(S("rw_dt"), 14 * l + s - 1)
            g = 4 * (s % 2)
            nc.scalar.activation(ZM[:, g:g + 4, :].rearrange("p u s -> p (u s)"), ps[:, 5, :], ACT.Copy).then_inc(S("rw_zc"), 1)

        def chunk_removed_pe(pe, l, j):
            if j == 0:
                pe.wait_ge(S("rw_tm"), 28 * (l + 1))
            else:
                pe.wait_ge(S("rw_s"), l + 1)
            for c in range(2):
                if j:
                    pe.matmul(ps[:, 6, c * P:(c + 1) * P], AR[:, c, 1, 0, :], S0[:, c, :, :].rearrange("p h d -> p (h d)"),
                              start=True, stop=False, skip_group_check=True)
                for h in range(2 * c, 2 * c + 2):
                    m = pe.matmul(ps[:, 6, h * HD:(h + 1) * HD], MM[:, 4 * j + h, 2, :], VT[:, j, h * HD:(h + 1) * HD],
                                  start=j == 0, stop=True, skip_group_check=True)
            m.then_inc(S("rw_x_ps"), 1)

        def chunk_solve_pe(pe, l, j):
            pe.wait_ge(S("rw_x"), 2 * l + j + 1)
            for h in range(4):
                m = pe.matmul(ps[:, 6, 256 + h * HD:256 + (h + 1) * HD], TT[:, 4 * j + h, :], XU[:, h * HD:(h + 1) * HD],
                              start=True, stop=True)
            m.then_inc(S("rw_u_ps"), 1)

        def chunk_out_pe(pe, l, j):
            pe.wait_ge(S("rw_u"), 2 * l + j + 1)
            if j == 0:
                for h in range(4):
                    c, pb = h // 2, HD * (h % 2)
                    pe.matmul(ps[pb:pb + HD, 5, c * HD:(c + 1) * HD], BK[:, 0, h * HD:(h + 1) * HD],
                              US[:, h * HD:(h + 1) * HD], start=True, stop=False)
                    m = pe.matmul(ps[pb:pb + HD, 5, c * HD:(c + 1) * HD], BK[:, 1, h * HD:(h + 1) * HD],
                                  VT[:, 0, h * HD:(h + 1) * HD], start=False, stop=True)
                m.then_inc(S("rw_s_ps"), 1)
            for c in range(2):
                if j:
                    pe.matmul(ps[:, 7, 256 + c * P:256 + (c + 1) * P], AR[:, c, 1, 1, :],
                              S0[:, c, :, :].rearrange("p h d -> p (h d)"), start=True, stop=False, skip_group_check=True)
                for h in range(2 * c, 2 * c + 2):
                    to = ps[:, 7, (4 * j + h) * HD:(4 * j + h + 1) * HD]
                    pe.matmul(to, MM[:, 4 * j + h, 1, :], US[:, h * HD:(h + 1) * HD], start=j == 0, stop=False,
                              skip_group_check=True)
                    m = pe.matmul(to, MM[:, 4 * j + h, 3, :], VT[:, j, h * HD:(h + 1) * HD], start=False, stop=True,
                                  skip_group_check=True)
            m.then_inc(S("rw_y"), 1)

        def chunk_removed_dve(v, l, j):
            v.wait_ge(S("rw_x_ps"), 2 * l + j + 1)
            if j:
                v.wait_ge(S("rw_x"), 2 * l + j)
            nc.vector.tensor_copy(XU, ps[:, 6, 0:256]).then_inc(S("rw_x"), 1)

        def chunk_solve_dve(v, l, j):
            v.wait_ge(S("rw_u_ps"), 2 * l + j + 1)
            if j:
                v.wait_ge(S("rw_y"), 2 * l + 1)
            nc.vector.tensor_copy(US, ps[:, 6, 256:512]).then_inc(S("rw_u"), 1)

        def chunk_state_dve(v, l, I):
            v.wait_ge(S("rw_s_ps"), l + 1)
            for h in range(4):
                c, rows = h // 2, slice(HD * (h % 2), HD * (h % 2) + HD)
                ins = nc.vector.tensor_scalar(S0[rows, c, h % 2, :], ps[rows, 5, c * HD:(c + 1) * HD],
                                              SCL[rows, c:c + 1], None, ALU.mult)
                if h < 3:
                    I(ins)
            ins.then_inc(S("rw_s"), 1)

        def rwkv_norm_dve(v, l, I, L):
            v.wait_ge(S("rw_y"), 2 * (l + 1))
            head_norm_dve(v, I, L, ps[:, 7, :].rearrange("p (a b) -> p a b", b=HD), RWKV_EPS, 2, 2 * l + 1, R_XC, R_SQ)
            bonus = SM[:, 32:40].unsqueeze(2).broadcast_to([P, 8, HD])
            L(nc.vector.tensor_tensor(R_SQ.rearrange("p (a b) -> p a b", b=HD),
                                      VT.rearrange("p t (h b) -> p (t h) b", b=HD), bonus, ALU.mult))
            L(nc.vector.tensor_tensor(R_XC, R_XC, R_SQ, ALU.add))
            nc.vector.tensor_tensor(R_XC, R_XC, GT.rearrange("p t c -> p (t c)"), ALU.mult).then_inc(S("head_out"), 1)

        flat_xt = XT[:].rearrange("p k t -> p (k t)")
        N_FL = [view(SA, 4096 + 512 * i, [16, 32]) for i in range(2)]
        N_GE = [view(flat_xt, 512 + 256 * i, [256]) for i in range(3)]
        N_HID, N_KC, N_VC = view(SB, 13952, [2, 64]), view(SB, 14080, [15]), view(SB, 14095, [2, HD])
        N_GT = view(SB, 14223, [NT, 24])
        N_P, N_PT = view(SA, 2048, [2, 4, T]), view(SA, 0, [4, 512])
        MX, RS, RG = (view(SM, 48 + 8 * i, [2, 4]) for i in range(3))

        def rope_pe(pe, l):
            pe.wait_ge(S("proj_evac"), 15 * (l + 1))
            pe.wait_ge(S("gla_st"), 3 * (l + 1))
            for j in range(7):
                m = pe.matmul(ps[:, j // 2, (j % 2) * T:(j % 2 + 1) * T], cst("rot"), HT[:, T_KC + j, :], start=True, stop=True)
            m.then_inc(S("rope_ps"), 1)

        def rope_dve(v, l, I, L):
            v.wait_ge(S("rope_ps"), l + 1)
            x = HT[:, T_KC:T_KC + 7, :]
            cos, sin = (cst(n).unsqueeze(1).broadcast_to([P, 7, T]) for n in ("cos", "sin"))
            turned = bank(0, 4)[:, 0:7 * T].rearrange("p (j t) -> p j t", t=T)
            I(nc.vector.tensor_tensor(turned, turned, sin, ALU.mult))
            L(nc.vector.tensor_tensor(x, x, cos, ALU.mult))
            nc.vector.tensor_tensor(x, x, turned, ALU.add).then_inc(S("rope"), 1)
            v.wait_ge(S("rope"), l + 1)

        def cmp_pool(pool, l):
            pool.wait_ge(S("rope"), l + 1)
            pool.wait_ge(S("gla_o"), l + 1)
            pool.wait_ge(S("par_loaded"), 16 * (l + 1))
            for i in range(2):
                nc.gpsimd.memset(N_FL[i][:, :, 30:32], 0.0).then_inc(S("cmp_blocks"), 1)
                pool.wait_ge(S("cmp_blocks"), 18 * l + i + 1)
            for i, (tile, emb) in enumerate(((T_KC, "pos_k"), (T_VC, "pos_v"))):
                for g in range(2):
                    rows = slice(HD * g, HD * (g + 1))
                    src = HT[rows, tile, :].rearrange("p (c j w) -> p w j c", j=8, w=2)
                    pos = par(emb)[rows, :].rearrange("p (j w) -> p w j", w=2)
                    for w in range(2):
                        for half in range(2):
                            ins = nc.gpsimd.tensor_tensor(
                                N_FL[i][HD * w:HD * (w + 1), 8 * half:8 * half + 8, 15 * g:15 * g + 15],
                                src[:, w, :, half:half + 15],
                                pos[:, w, 8 * half:8 * half + 8].unsqueeze(2).broadcast_to([HD, 8, 15]), ALU.add)
                            ins.then_inc(S("cmp_blocks"), 1)

        def cmp_hidden_pe(pe, l):
            pe.wait_ge(S("gla_out"), l + 1)
            pe.wait_ge(S("cmp_blocks"), 18 * (l + 1))
            w = []
            for i in range(2):
                need_slot(pe, l * LAYER_SLOTS + S_CMP + i)
                w.append(slot(l * LAYER_SLOTS + S_CMP + i).rearrange("p (j n) -> p j n", j=16))
            for j in range(16):
                for i in range(2):
                    m = pe.matmul(ps[32 * i:32 * (i + 1), 4, 0:256], N_FL[i][:, j, :], w[i][:, j, :], start=j == 0, stop=j == 15)
            m.then_inc(S("cmp_hidden"), 1)

        def cmp_turn_pe(pe, l):
            pe.wait_ge(S("gelu"), l + 1)
            for i in range(2):
                m = pe.transpose(ps[:, 4, i * 64:(i + 1) * 64], N_GE[0][0:64, i * P:(i + 1) * P], ident[0:64, 0:64])
            m.then_inc(S("cmp_hid_ps"), 1)

        def cmp_out_pe(pe, l):
            pe.wait_ge(S("cmp_hid"), l + 1)
            wk, wv = (par(n).rearrange("p (a d) -> p a d", a=2) for n in ("wk2", "wv2"))
            for g in range(2):
                for a in range(2):
                    pe.matmul(ps[HD * g:HD * (g + 1), 4, 128:143], wk[:, a, :], N_HID[:, a, 15 * g:15 * g + 15],
                              start=a == 0, stop=a == 1)
            for g in range(2):
                for a in range(2):
                    m = pe.matmul(ps[0:15, 4, 256 + HD * g:256 + HD * (g + 1)], N_HID[:, a, 32 + 15 * g:32 + 15 * g + 15],
                                  wv[:, a, :], start=a == 0, stop=a == 1)
            m.then_inc(S("cmp_kv_ps"), 1)

        def gelu_dve(v, L, n, x, y, t, to):
            L(nc.vector.tensor_tensor(y, x, x, ALU.mult))
            L(nc.vector.tensor_scalar(y, y, GELU_K, 1.0, ALU.mult, ALU.add))
            nc.vector.tensor_tensor(y, y, x, ALU.mult).then_inc(S("tanh_in"), 1)
            v.wait_ge(S("tanh"), n + 1)
            L(nc.vector.scalar_tensor_tensor(out=t, in0=t, scalar=1.0, in1=x, op0=ALU.add, op1=ALU.mult))
            nc.vector.tensor_scalar(to, t, 0.5, None, ALU.mult).then_inc(S("gelu"), 1)

        def cmp_hidden_dve(v, l, L):
            v.wait_ge(S("cmp_hidden"), l + 1)
            x, y, t = (a[0:64, :] for a in N_GE)
            L(nc.vector.tensor_copy(x, ps[0:64, 4, 0:256]))
            gelu_dve(v, L, l, x, y, t, x)

        def cmp_turn_dve(v, l):
            v.wait_ge(S("cmp_hid_ps"), l + 1)
            nc.vector.tensor_copy(N_HID.rearrange("p a b -> p (a b)"), ps[:, 4, 0:128]).then_inc(S("cmp_hid"), 1)

        def cmp_out_dve(v, l, I):
            v.wait_ge(S("cmp_kv_ps"), l + 1)
            I(nc.vector.tensor_copy(N_KC, ps[:, 4, 128:143]))
            nc.vector.tensor_copy(N_VC[0:15, :, :], ps[0:15, 4, 256:384].rearrange("p (g d) -> p g d", g=2)).then_inc(S("cmp_kv"), 1)

        def cmp_act(act, l):
            act.wait_ge(S("tanh_in"), l + 1)
            nc.scalar.activation(N_GE[2][0:64, :], N_GE[1][0:64, :], ACT.Tanh, scale=GELU_C).then_inc(S("tanh"), 1)

        def nsa_gate_act(act, l):
            nc.scalar.activation(N_GT, NV[:, :, 256:280], ACT.Sigmoid).then_inc(S("nsa_gate"), 1)

        FIRST_UNITS = [(kind, t, g) for kind, t in ((1, 1), (2, 1), (1, 0), (2, 0), (0, 0), (0, 1)) for g in range(2)]
        UNITS = FIRST_UNITS * DEPTH + [(3, t, g) for t in (1, 0) for g in range(2)]
        NU = len(FIRST_UNITS)

        def key_tiles(n):
            kind, t, g = UNITS[n]
            return 1 if kind == 0 else t + 1

        def tiles_before(n):
            return sum(key_tiles(m) for m in range(n))

        def width(kind, t):
            return 15 if kind == 0 else P * (t + 1)

        def attention_keys(kind, g):
            rows = slice(HD * g, HD * (g + 1))
            if kind == 0:
                return N_KC[rows, :]
            return HT[rows, {1: T_KS, 2: T_KW, 3: 4}[kind], :]

        def attention_values(kind, g, k):
            if kind == 0:
                return N_VC[0:15, g, :]
            if kind == 3:
                return V2[:, k, HD * g:HD * (g + 1)]
            return NV[:, k, (kind - 1) * P + HD * g:(kind - 1) * P + HD * (g + 1)]

        def attention_scores_pe(pe, n):
            kind, t, g = UNITS[n]
            w, q0 = width(kind, t), 0 if kind == 3 else T_Q
            pe.wait_ge(S("att_raw"), n)
            rows = slice(HD * g, HD * (g + 1))
            for j in range(4):
                m = pe.matmul(bank(0, 2)[:, j * w:(j + 1) * w], HT[rows, q0 + j, t * P:(t + 1) * P],
                              attention_keys(kind, g)[:, 0:w], start=True, stop=True)
            m.then_inc(S("att_scores"), 1)

        def turn_bank(n, k):
            return 2 + k

        def attention_turn_pe(pe, n):
            kind, t, g = UNITS[n]
            pe.wait_ge(S("att_p"), n + 1)
            kw = min(width(kind, t), P)
            for k in range(key_tiles(n)):
                x = tiles_before(n) + k
                free = x if key_tiles(n) == 1 else x - 1
                if free > 0:
                    pe.wait_ge(S("att_pt"), free)
                for j in range(4):
                    m = pe.transpose(ps[0:kw, turn_bank(n, k), j * P:(j + 1) * P], N_P[:, n % 2, j, k * P:k * P + kw], ident)
                m.then_inc(S("att_t_ps"), 1)

        def attention_out_pe(pe, n):
            kind, t, g = UNITS[n]
            kw = min(width(kind, t), P)
            for k in range(key_tiles(n)):
                x = tiles_before(n) + k
                pe.wait_ge(S("att_pt"), x + 1)
                first = k == 0 and kind in (1, 3)
                for j in range(4):
                    m = pe.matmul(ps[HD * g:HD * (g + 1), 3 + t, j * P:(j + 1) * P], attention_values(kind, g, k),
                                  N_PT[0:kw, x % 4, j * P:(j + 1) * P], start=first and j == 0, stop=True, skip_group_check=True)
                m.then_inc(S("att_pv"), 1)

        def attention_exp_act(act, n):
            kind, t, g = UNITS[n]
            w = width(kind, t)
            act.wait_ge(S("att_max"), n + 1)
            if kind == 3:
                nc.scalar.activation(RG[:, n % 2, :], RG[:, n % 2, :], ACT.Exp).then_inc(S("att_sink"), 1)
            for j in range(4):
                nc.scalar.activation(N_P[:, n % 2, j, 0:w], N_P[:, n % 2, j, 0:w], ACT.Exp, scale=HD ** -0.5,
                                     bias=MX[:, n % 2, j:j + 1], accum_out=RS[:, n % 2, j:j + 1]).then_inc(S("att_exp"), 1)

        def attention_out_act(act, n):
            kind, t, g = UNITS[n]
            kw = min(width(kind, t), P)
            for k in range(key_tiles(n)):
                x = tiles_before(n) + k
                act.wait_ge(S("att_t_ps"), x + 1)
                if x >= 4:
                    act.wait_ge(S("att_pv"), x - 3)
                nc.scalar.activation(N_PT[0:kw, x % 4, :], ps[0:kw, turn_bank(n, k), :], ACT.Copy).then_inc(S("att_pt"), 1)

        def attention_scores_dve(v, n, I, L):
            kind, t, g = UNITS[n]
            w, to, mx = width(kind, t), N_P[:, n % 2, :, :], MX[:, n % 2, :]
            v.wait_ge(S("att_scores"), n + 1)
            if n >= 2:
                v.wait_ge(S("att_t_ps"), tiles_before(n - 1))
            raw = bank(0, 2)[:, 0:4 * w].rearrange("p (j k) -> p j k", j=4)
            if kind == 0:
                mask = cst("cmp_add")[:, 15 * t:15 * t + 15].unsqueeze(1).broadcast_to([P, 4, 15])
                nc.vector.tensor_tensor(to[:, :, 0:15], raw, mask, ALU.add).then_inc(S("att_raw"), 1)
            else:
                if t and kind == 3:
                    prev = cst("prev_add").unsqueeze(1).broadcast_to([P, 4, P])
                    I(nc.vector.tensor_tensor(to[:, :, 0:P], raw[:, :, 0:P], prev, ALU.add))
                elif t:
                    I(nc.vector.tensor_copy(to[:, :, 0:P], raw[:, :, 0:P]))
                diag = cst("diag_add").unsqueeze(1).broadcast_to([P, 4, P])
                nc.vector.tensor_tensor(to[:, :, w - P:w], raw[:, :, w - P:w], diag, ALU.add).then_inc(S("att_raw"), 1)
            v.wait_ge(S("att_raw"), n + 1)
            L(nc.vector.tensor_reduce(mx, to[:, :, 0:w], AX.X, ALU.max))
            if kind == 3:
                sink = SNK[:, 4 * g:4 * g + 4]
                L(nc.vector.tensor_scalar(mx, mx, HD ** -0.5, None, ALU.mult))
                L(nc.vector.tensor_tensor(mx, mx, sink, ALU.max))
                I(nc.vector.tensor_tensor(RG[:, n % 2, :], sink, mx, ALU.subtract))
                nc.vector.tensor_scalar(mx, mx, -1.0, None, ALU.mult).then_inc(S("att_max"), 1)
            else:
                nc.vector.tensor_scalar(mx, mx, -(HD ** -0.5), None, ALU.mult).then_inc(S("att_max"), 1)

        def attention_scale_dve(v, n, L):
            kind, t, g = UNITS[n]
            w, rs, rg = width(kind, t), RS[:, n % 2, :], RG[:, n % 2, :]
            v.wait_ge(S("att_exp"), 4 * (n + 1))
            if kind == 3:
                v.wait_ge(S("att_sink"), n - NU * DEPTH + 1)
                L(nc.vector.tensor_tensor(rs, rs, rg, ALU.add))
            L(nc.vector.reciprocal(rg, rs))
            if kind != 3:
                gate = N_GT[:, t, :].rearrange("p (i b) -> p i b", b=3)[:, 4 * g:4 * g + 4, kind]
                L(nc.vector.tensor_tensor(rg, rg, gate, ALU.mult))
            if kind == 0:
                L(nc.vector.tensor_scalar(rg, rg, cst("cmp_any")[:, t:t + 1], None, ALU.mult))
            to = N_P[:, n % 2, :, 0:w]
            nc.vector.tensor_tensor(to, to, rg.unsqueeze(2).broadcast_to([P, 4, w]), ALU.mult).then_inc(S("att_p"), 1)

        def attention_merge_dve(v, n, I):
            v.wait_ge(S("att_pv"), tiles_before(n))
            for t in range(NT):
                ins = nc.vector.tensor_copy(OT[:, 4 if n <= NU * DEPTH else 0:8 if n <= NU * DEPTH else 4, t * P:(t + 1) * P],
                                            ps[:, 3 + t, :].rearrange("p (j q) -> p j q", j=4))
                if t == 0:
                    I(ins)
            ins.then_inc(S("nsa_out"), 1)

        def mix_out_pe(pe, l):
            for done in ("gla_out", "rw_out", "nsa_out"):
                pe.wait_ge(S(done), l + 1)
            for c in range(2):
                i = l * LAYER_SLOTS + S_WO + c
                need_slot(pe, i)
                w = slot(i).rearrange("p (k n) -> p k n", k=KT)
                for t in range(NT):
                    for k in range(KT):
                        m = pe.matmul(ps[:, 2 * t + c, :], OT[:, k, t * P:(t + 1) * P], w[:, k, :], start=k == 0, stop=k == KT - 1)
                m.then_inc(S("mix_ready"), 1)

        def layer_norm_dve(v, n, b0, ready, I, L):
            v.wait_ge(S(ready[0]), ready[1])
            for t in range(NT):
                s, q, r = SM[:, 80 + t:81 + t], SM[:, 84 + t:85 + t], SM[:, 88 + t:89 + t]
                L(nc.vector.scalar_tensor_tensor(out=X[:, t, :], in0=X[:, t, :], scalar=ALPHA, in1=bank(b0 + 2 * t, 2),
                                                 op0=ALU.mult, op1=ALU.add, accum_out=s))
                nc.vector.tensor_scalar(s, s, -1.0 / D, None, ALU.mult).then_inc(S("ln_mean"), 1)
            for t in range(NT):
                s, q, r = SM[:, 80 + t:81 + t], SM[:, 84 + t:85 + t], SM[:, 88 + t:89 + t]
                v.wait_ge(S("ln_sq"), 2 * n + t + 1)
                nc.vector.tensor_scalar(q, q, 1.0 / D, LN_EPS, ALU.mult, ALU.add).then_inc(S("ln_var"), 1)
                v.wait_ge(S("ln_std"), 2 * n + t + 1)
                L(nc.vector.reciprocal(r, r))
                L(nc.vector.tensor_scalar(X[:, t, :], X[:, t, :], s, r, ALU.add, ALU.mult))
                if t == 0:
                    v.wait_ge(S("ln_loaded"), 32 * (n + 1))
                L(nc.vector.tensor_tensor(X[:, t, :], X[:, t, :], LNW, ALU.mult))
                ins = nc.vector.tensor_tensor(X[:, t, :], X[:, t, :], LNB, ALU.add)
                if t == 0:
                    I(ins)
            ins.then_inc(S("x_ready"), 1)
            v.wait_ge(S("x_ready"), n + 1)

        def layer_norm_act(act, n):
            for t in range(NT):
                s, q, r = SM[:, 80 + t:81 + t], SM[:, 84 + t:85 + t], SM[:, 88 + t:89 + t]
                act.wait_ge(S("ln_mean"), 2 * n + t + 1)
                nc.scalar.activation(SQ, X[:, t, :], ACT.Square, bias=s, accum_out=q).then_inc(S("ln_sq"), 1)
                act.wait_ge(S("ln_var"), 2 * n + t + 1)
                nc.scalar.activation(r, q, ACT.Sqrt).then_inc(S("ln_std"), 1)

        SG = [view(SA, 512 * i, [512]) for i in range(2)]

        def ffn_pe(pe, l):
            pe.wait_ge(S("xt_ready"), 4 * (2 * l + 2))
            for f in range(11):
                i = l * LAYER_SLOTS + S_GU + f
                need_slot(pe, i)
                if f >= 2:
                    pe.wait_ge(S("ffn_evac"), 11 * l + f - 1)
                w = slot(i).rearrange("p (k a n) -> p k a n", k=KT, a=2)
                for a in range(2):
                    for j in range(2):
                        for k in range(KT):
                            m = pe.matmul(ps[:, 2 * a + f % 2, j * T:(j + 1) * T], w[:, k, a, j * P:(j + 1) * P], XT[:, k, :],
                                          start=k == 0, stop=k == KT - 1)
                m.then_inc(S("ffn_ready"), 1)
            for s in range(6):
                i = l * LAYER_SLOTS + S_DN + s
                need_slot(pe, i)
                pe.wait_ge(S("ffn_evac"), 11 * l + min(2 * s + 2, 11))
                w = slot(i).rearrange("p (k n) -> p k n", k=4)
                for k in range(4 * s, min(4 * s + 4, NF)):
                    for t in range(NT):
                        for c in range(2):
                            m = pe.matmul(ps[:, 4 + 2 * t + c, :], HT[:, k, t * P:(t + 1) * P],
                                          w[:, k - 4 * s, c * 512:(c + 1) * 512], start=k == 0, stop=k == NF - 1)
                m.then_inc(S("down_ready"), 1)

        def ffn_act(act, l):
            for f in range(11):
                act.wait_ge(S("ffn_ready"), 11 * l + f + 1)
                if f >= 2:
                    act.wait_ge(S("ffn_evac"), 11 * l + f - 1)
                nc.scalar.activation(SG[f % 2], ps[:, f % 2, :], ACT.Silu).then_inc(S("ffn_silu"), 1)

        def ffn_dve(v, l):
            for f in range(11):
                v.wait_ge(S("ffn_silu"), 11 * l + f + 1)
                nc.vector.tensor_tensor(HT[:, 2 * f:2 * f + 2, :].rearrange("p a t -> p (a t)"), SG[f % 2], ps[:, 2 + f % 2, :],
                                        ALU.mult).then_inc(S("ffn_evac"), 1)

        MOD = view(SB, 4096, [6, D])
        CR = view(SA, 0, [KT, P])
        HF = view(SA, 2048, [NT, D])
        V2 = NV[:, :, 0:P]
        XC2, RA, RI, AE = (view(SB, at, [4, T]) for at in (10240, 11264, 12288, 13312))
        SQM = view(SB, 10240, [8, T])
        YT = view(SB, 12288, [D])
        BR, SNK = SM[:, 128:160], SM[:, 160:168]
        BD = view(SB, 2 * D, [D])

        def second_sp(sp):
            for done in ("gla_out", "rw_out", "nsa_out"):
                sp.wait_ge(S(done), DEPTH)
            sp.dma_start(PAR[:, 0:SECOND_COLS], dram["second"]).then_inc(S("par2_loaded"), 16)
            sp.dma_start(MOD.rearrange("p a d -> p (a d)"), dram["b_ada"].broadcast_to([P, 6 * D])).then_inc(S("par2_loaded"), 16)
            sp.dma_start(SM[:, 128:168], dram["small"].broadcast_to([P, 40])).then_inc(S("par2_loaded"), 16)
            for i in range(S_ADA, S_MOE):
                stream(sp, i)
                if i == S_ADA + 2 * RING:
                    sp.wait_ge(S("x_ready"), 2 * DEPTH)
                    sp.dma_start(LNW, dram["gains"][0:1, :].broadcast_to([P, D])).then_inc(S("gain_loaded"), 16)
                    sp.dma_start(LNB, dram["gains"][1:2, :].broadcast_to([P, D])).then_inc(S("gain_loaded"), 16)
            sp.wait_ge(S("h_ready"), 1)
            sp.dma_start(LNW, dram["gains"][2:3, :].broadcast_to([P, D])).then_inc(S("gain_loaded"), 16)

        def modulation_pe(pe):
            pe.wait_ge(S("cond"), 1)
            for n in range(12):
                need_slot(pe, S_ADA + n)
                w = slot(S_ADA + n).rearrange("p (k n) -> p k n", k=KT)
                if n >= 4:
                    pe.wait_ge(S("mod"), n - 3)
                for k in range(KT):
                    m = pe.matmul(ps[:, n % 4, :], CR[:, k, :], w[:, k, :], start=k == 0, stop=k == KT - 1)
                m.then_inc(S("mod_ready"), 1)

        def modulation_dve(v, I, L):
            v.wait_ge(S("par2_loaded"), 48)
            nc.vector.tensor_copy(CR, par2("c").unsqueeze(2).broadcast_to([P, KT, P])).then_inc(S("cond"), 1)
            flat = MOD.rearrange("p a d -> p (a d)")
            for n in range(12):
                v.wait_ge(S("mod_ready"), n + 1)
                to = flat[:, n * 512:(n + 1) * 512]
                nc.vector.tensor_tensor(to, to, ps[:, n % 4, :], ALU.add).then_inc(S("mod"), 1)
            v.wait_ge(S("mod"), 12)

        def rms_act(act, n, ready):
            act.wait_ge(S(ready[0]), ready[1])
            for t in range(NT):
                if 2 * n + t:
                    act.wait_ge(S("rms_sq"), 2 * n + t)
                nc.scalar.activation(SQ2, X[:, t, :], ACT.Square, accum_out=SM[:, 92 + t:93 + t]).then_inc(S("rms_sq"), 1)
            act.wait_ge(S("rms_var"), n + (2 if n else 1))
            nc.scalar.activation(SM[:, 96:98], SM[:, 94:96], ACT.Sqrt).then_inc(S("rms_std"), 1)

        SQ2 = view(SB, 3 * D, [D])

        def rms_dve(v, n, L):
            v.wait_ge(S("rms_sq"), 2 * (n + 1))
            nc.vector.tensor_scalar(SM[:, 94:96], SM[:, 92:94], 1.0 / D, RMS_EPS, ALU.mult, ALU.add).then_inc(S("rms_var"), 1)
            v.wait_ge(S("rms_std"), n + (2 if n else 1))
            L(nc.vector.reciprocal(SM[:, 98:100], SM[:, 96:98]))

        def modulated_dve(v, n, I, L):
            v.wait_ge(S("gain_loaded"), 32)
            scale, shift = MOD[:, 3 * n + 1, :], MOD[:, 3 * n, :]
            L(nc.vector.scalar_tensor_tensor(out=scale, in0=scale, scalar=1.0, in1=(LNW, LNB)[n], op0=ALU.add, op1=ALU.mult))
            rms_dve(v, n, L)
            for t in range(NT):
                L(nc.vector.scalar_tensor_tensor(out=HF[:, t, :], in0=X[:, t, :], scalar=SM[:, 98 + t:99 + t], in1=scale,
                                                 op0=ALU.mult, op1=ALU.mult))
                ins = nc.vector.tensor_tensor(HF[:, t, :], HF[:, t, :], shift, ALU.add)
                if t == 0:
                    I(ins)
            ins.then_inc(S("h_ready"), 1)

        def project2_pe(pe):
            pe.wait_ge(S("xt_ready"), 4 * 5)
            pe.wait_ge(S("mod"), 12)
            g = 0
            for s in range(4):
                need_slot(pe, S_IN2 + s)
                w = slot(S_IN2 + s).rearrange("p (k n) -> p k n", k=KT)
                for q in range(2):
                    if g >= 4:
                        pe.wait_ge(S("proj2_evac"), g - 3)
                    for j in range(2):
                        for k in range(KT):
                            if g < 6 or (g == 6 and j == 0):
                                m = pe.matmul(ps[:, g % 4, j * T:(j + 1) * T], w[:, k, (2 * q + j) * P:(2 * q + j + 1) * P],
                                              XT[:, k, :], start=k == 0, stop=k == KT - 1)
                            elif g == 7:
                                m = pe.matmul(ps[:, g % 4, j * P:(j + 1) * P], XT[:, k, j * P:(j + 1) * P], w[:, k, P:2 * P],
                                              start=k == 0, stop=k == KT - 1)
                    m.then_inc(S("proj2_ready"), 1)
                    g += 1

        def project2_act(act):
            for g in range(8):
                act.wait_ge(S("proj2_ready"), g + 1)
                n = 512 if g < 6 else T
                if g < 7:
                    to = HT[:, 2 * g:2 * g + n // T, :].rearrange("p a t -> p (a t)")
                    src = ps[:, g % 4, 0:n]
                else:
                    to, src = V2, ps[:, g % 4, 0:T].rearrange("p (t d) -> p t d", t=NT)
                nc.scalar.activation(to, src, ACT.Copy).then_inc(S("proj2_evac"), 1)

        LSL = SM[:, 100:104]

        def lru_act(act, I, L):
            lam = par2("lam")
            act.wait_ge(S("par2_loaded"), 48)
            L(nc.scalar.activation(SM[:, 104:108], lam, ACT.Abs))
            L(nc.scalar.activation(SM[:, 104:108], SM[:, 104:108], ACT.Exp, scale=-1.0))
            nc.scalar.activation(SM[:, 104:108], SM[:, 104:108], ACT.Ln, bias=cst("ones")[:, 0:1]).then_inc(S("lam_ln"), 1)
            act.wait_ge(S("rg"), 1)
            for a, (to, bias) in enumerate(((RA, "b_a"), (RI, "b_x"))):
                for c in range(4):
                    nc.scalar.activation(to[:, c, :], ps[:, 2 * a + c // 2, (c % 2) * T:(c % 2 + 1) * T], ACT.Sigmoid,
                                         bias=par2(bias)[:, c:c + 1]).then_inc(S("rg_gates"), 1)
            act.wait_ge(S("log_a"), 1)
            I(nc.scalar.activation(AE, RA, ACT.Exp))
            nc.scalar.activation(RA, RA, ACT.Tanh, scale=-1.0).then_inc(S("lru_decay"), 1)
            act.wait_ge(S("mult2"), 1)
            nc.scalar.activation(RA, RA, ACT.Sqrt).then_inc(S("lru_mult"), 1)
            act.wait_ge(S("tanh_in"), DEPTH + 1)
            nc.scalar.activation(RI, RA, ACT.Tanh, scale=GELU_C).then_inc(S("tanh"), 1)

        def rg_pe(pe):
            pe.wait_ge(S("conv"), 1)
            for a, name in enumerate(("rg_a", "rg_x")):
                for c in range(4):
                    m = pe.matmul(ps[:, 2 * a + c // 2, (c % 2) * T:(c % 2 + 1) * T], par2(name)[:, c * P:(c + 1) * P],
                                  XC2[:, c, :], start=True, stop=True)
            m.then_inc(S("rg"), 1)

        def lru_dve(v, I, L):
            v.wait_ge(S("proj2_evac"), 8)
            xr, xg = HT[:, 5:9, :], HT[:, 9:13, :]
            cw = par2("conv_w")
            for c in range(4):
                (L if c == 3 else I)(nc.vector.tensor_scalar(XC2[:, c, :], xr[:, c, :], cw[:, 4 * c + 3:4 * c + 4],
                                                             par2("conv_b")[:, c:c + 1], ALU.mult, ALU.add))
            for d in range(1, 4):
                for c in range(4):
                    ins = nc.vector.scalar_tensor_tensor(out=XC2[:, c, d:T], in0=xr[:, c, 0:T - d],
                                                         scalar=cw[:, 4 * c + 3 - d:4 * c + 4 - d], in1=XC2[:, c, d:T],
                                                         op0=ALU.mult, op1=ALU.add)
                    if d < 3:
                        (L if c == 3 else I)(ins)
                    elif c < 3:
                        I(ins)
            ins.then_inc(S("conv"), 1)
            v.wait_ge(S("lam_ln"), 1)
            L(nc.vector.tensor_scalar(LSL, par2("lam"), 0.0, None, ALU.min))
            L(nc.vector.tensor_tensor(LSL, LSL, SM[:, 104:108], ALU.subtract))
            L(nc.vector.tensor_scalar(LSL, LSL, LRU_C, None, ALU.mult))
            v.wait_ge(S("rg_gates"), 8)
            for c in range(4):
                ins = nc.vector.tensor_scalar(RA[:, c, :], RA[:, c, :], LSL[:, c:c + 1], None, ALU.mult)
                if c < 3:
                    I(ins)
            ins.then_inc(S("log_a"), 1)
            L(nc.vector.tensor_tensor(RI, RI, XC2, ALU.mult))
            v.wait_ge(S("lru_decay"), 1)
            L(nc.vector.tensor_scalar(XC2, RA, 1.0, None, ALU.add))
            L(nc.vector.reciprocal(XC2, XC2))
            L(nc.vector.scalar_tensor_tensor(out=RA, in0=RA, scalar=2.0, in1=XC2, op0=ALU.mult, op1=ALU.mult))
            nc.vector.tensor_scalar(RA, RA, 0.0, None, ALU.max).then_inc(S("mult2"), 1)
            v.wait_ge(S("lru_mult"), 1)
            L(nc.vector.tensor_tensor(RI, RI, RA, ALU.mult))
            for c in range(4):
                (L if c == 3 else I)(nc.vector.tensor_tensor_scan(XC2[:, c, :], AE[:, c, :], RI[:, c, :], 0.0, ALU.mult, ALU.add))
            gelu_dve(v, L, DEPTH, xg, RA, RI, RI)
            v.wait_ge(S("gelu"), DEPTH + 1)
            nc.vector.tensor_tensor(OT[:, 4:8, :], XC2, RI, ALU.mult).then_inc(S("lru_out"), 1)

        def merge_dve(v, I, L):
            attention_merge_dve(v, len(UNITS), I)
            v.wait_ge(S("nsa_out"), DEPTH + 1)
            v.wait_ge(S("lru_out"), 1)
            nc.vector.tensor_tensor(SQM, OT[:], OT[:], ALU.mult).then_inc(S("merge_sq"), 1)
            v.wait_ge(S("merge_sq"), 1)
            for c in range(8):
                g = par2("g_attn")[:, c:c + 1] if c < 4 else par2("g_lru")[:, c - 4:c - 3]
                ins = nc.vector.tensor_scalar(OT[:, c, :], OT[:, c, :], g, None, ALU.mult)
                if c < 7:
                    I(ins)
            ins.then_inc(S("merge_sq"), 1)
            v.wait_ge(S("merge_ss"), 1)
            nc.vector.tensor_scalar(SM[:, 112:116], ps[:, 5, 0:4], 1.0 / 512, RMS_EPS, ALU.mult, ALU.add).then_inc(S("rms_var"), 1)
            v.wait_ge(S("rms_std"), 2)
            L(nc.vector.reciprocal(SM[:, 116:120], SM[:, 112:116]))
            v.wait_ge(S("mix2_ready"), 2)
            v.sem_inc(S("moe_slot"), RING)
            for t in range(NT):
                L(nc.vector.tensor_scalar(YT, bank(2 * t, 2), SM[:, 116 + t:117 + t], None, ALU.mult))
                L(nc.vector.scalar_tensor_tensor(out=YT, in0=bank(4 + 2 * t, 2), scalar=SM[:, 118 + t:119 + t], in1=YT,
                                                 op0=ALU.mult, op1=ALU.add))
                L(nc.vector.tensor_tensor(YT, YT, MOD[:, 2, :], ALU.mult))
                ins = nc.vector.tensor_tensor(X[:, t, :], X[:, t, :], YT, ALU.add)
                if t == 0:
                    L(ins)
            ins.then_inc(S("x_ready"), 1)
            v.wait_ge(S("x_ready"), 2 * DEPTH + 1)

        def merge_act(act):
            act.wait_ge(S("rms_var"), 2)
            nc.scalar.activation(SM[:, 112:116], SM[:, 112:116], ACT.Sqrt).then_inc(S("rms_std"), 1)

        def merge_pe(pe):
            pe.wait_ge(S("merge_sq"), 1)
            for a in range(2):
                for t in range(NT):
                    for c in range(4):
                        m = pe.matmul(ps[:, 5, 2 * a + t:2 * a + t + 1], SQM[:, 4 * a + c, t * P:(t + 1) * P],
                                      cst("ones")[:, 0:1], start=c == 0, stop=c == 3)
            m.then_inc(S("merge_ss"), 1)
            pe.wait_ge(S("merge_sq"), 2)
            pe.wait_ge(S("rms_var"), 2)
            for c in range(2):
                need_slot(pe, S_WO2 + c)
                w = slot(S_WO2 + c).rearrange("p (k n) -> p k n", k=KT)
                for a in range(2):
                    for t in range(NT):
                        for k in range(4):
                            m = pe.matmul(ps[:, 4 * a + 2 * t + c, :], OT[:, 4 * a + k, t * P:(t + 1) * P], w[:, 4 * a + k, :],
                                          start=k == 0, stop=k == 3)
                m.then_inc(S("mix2_ready"), 1)

        LG, SEL, GT2, RNK = (view(SA, 4096 + 64 * i, [NT, NE]) for i in range(4))
        RANK, GATE = view(SA, 4352, [NT, NITEM]), view(SA, 4448, [NT, NITEM])
        M8 = view(SA, 4544, [NT, 8])
        TMP, CUM = view(SA, 4560, [NE]), view(SA, 4592, [NE])
        NXT, CE, EXC = (view(SA, 4624 + 32 * i, [NE]) for i in range(3))
        REM, NEGM, RSUM = SM[:, 170:171], SM[:, 172:174], SM[:, 174:176]
        EID = view(SA, 4720, [64])
        OH, OW, OX = (view(HT[:].rearrange("p a t -> p (a t)"), NITEM * NE * i, [NITEM, NE]) for i in range(3))
        WIN = view(SB, 12288, [NITEM])
        GTT = view(SA, 4800, [T])

        def router_pe(pe):
            pe.wait_ge(S("xt_ready"), 4 * 6)
            pe.wait_ge(S("x_ready"), 2 * DEPTH + 1)
            w = par2("router").rearrange("p (k e) -> p k e", k=KT)
            for t in range(NT):
                for k in range(KT):
                    m = pe.matmul(ps[:, 0, t * NE:(t + 1) * NE], XT[:, k, t * P:(t + 1) * P], w[:, k, :],
                                  start=k == 0, stop=k == KT - 1)
            m.then_inc(S("counts"), 1)
            pe.wait_ge(S("selected"), NT)
            strict, ones = cst("pairs")[:, 0:P], cst("ones")[:, 0:P]
            pe.matmul(ps[:, 1, 0:NE], strict, SEL[:, 0, :], start=True, stop=True)
            pe.matmul(ps[:, 1, NE:2 * NE], strict, SEL[:, 1, :], start=True, stop=False)
            pe.matmul(ps[:, 1, NE:2 * NE], ones, SEL[:, 0, :], start=False, stop=True)
            pe.matmul(ps[:, 1, 2 * NE:3 * NE], ones, SEL[:, 0, :], start=True, stop=False)
            m = pe.matmul(ps[:, 1, 2 * NE:3 * NE], ones, SEL[:, 1, :], start=False, stop=True)
            m.then_inc(S("counts"), 1)
            pe.wait_ge(S("gates"), 1)
            for t in range(NT):
                m = pe.transpose(ps[0:NE, 2, t * P:(t + 1) * P], GT2[:, t, :], ident)
            m.then_inc(S("gates_t_ps"), 1)
            pe.wait_ge(S("gates_t"), 1)
            pe.wait_ge(S("par2_loaded"), 64)              
            for t in range(NT):
                for c in range(2):
                    pe.matmul(ps[:, 4 + 2 * t + c, :], GTT[0:NE, t * P:(t + 1) * P], BD[0:NE, c * 512:(c + 1) * 512],
                                  start=True, stop=True)

        def router_act(act):
            for t in range(NT):
                act.wait_ge(S("top"), t + 1)
                nc.scalar.activation(GT2[:, t, :], LG[:, t, :], ACT.Exp, bias=NEGM[:, t:t + 1]).then_inc(S("gate_exp"), 1)

        def router_dve(v, I, L):
            v.wait_ge(S("counts"), 1)
            L(nc.vector.tensor_tensor(LG, ps[:, 0, 0:2 * NE].rearrange("p (t e) -> p t e", t=NT),
                                      BR.unsqueeze(1).broadcast_to([P, NT, NE]), ALU.add))
            for t in range(NT):
                lg, sel, v4 = LG[:, t, :], SEL[:, t, :], M8[:, t, TOPK - 1:TOPK]
                L(nc.vector.max(M8[:, t, :], lg))
                nc.vector.tensor_scalar(NEGM[:, t:t + 1], M8[:, t, 0:1], -1.0, None, ALU.mult).then_inc(S("top"), 1)
                L(nc.vector.tensor_scalar(sel, lg, v4, None, ALU.is_gt))
                L(nc.vector.tensor_reduce(REM, sel, AX.X, ALU.add))
                L(nc.vector.tensor_scalar(REM, REM, -1.0, float(TOPK), ALU.mult, ALU.add))
                L(nc.vector.tensor_scalar(TMP, lg, v4, None, ALU.is_equal))
                L(nc.vector.tensor_tensor_scan(CUM, cst("ones")[:, 0:NE], TMP, 0.0, ALU.mult, ALU.add))
                L(nc.vector.scalar_tensor_tensor(out=TMP, in0=CUM, scalar=REM, in1=TMP, op0=ALU.is_le, op1=ALU.mult))
                nc.vector.tensor_tensor(sel, sel, TMP, ALU.add).then_inc(S("selected"), 1)
                v.wait_ge(S("selected"), t + 1)
            v.wait_ge(S("gate_exp"), NT)
            L(nc.vector.tensor_tensor(GT2, GT2, SEL, ALU.mult))
            L(nc.vector.tensor_reduce(RSUM, GT2, AX.X, ALU.add))
            L(nc.vector.reciprocal(RSUM, RSUM))
            nc.vector.tensor_tensor(GT2, GT2, RSUM.unsqueeze(2).broadcast_to([P, NT, NE]), ALU.mult).then_inc(S("gates"), 1)
            v.wait_ge(S("gates"), 1)
            v.wait_ge(S("counts"), 2)
            cnt = ps[:, 1, 0:2 * NE].rearrange("p (t e) -> p t e", t=NT)
            L(nc.vector.scalar_tensor_tensor(out=RNK, in0=cnt, scalar=2000.0, in1=SEL, op0=ALU.add, op1=ALU.mult))
            total = ps[:, 1, 2 * NE:3 * NE]
            L(nc.vector.tensor_scalar(NXT, total, 0.0, None, ALU.is_gt))
            for r in range(1, T // SLOTS_E):
                L(nc.vector.tensor_scalar(TMP, total, float(r * SLOTS_E), None, ALU.is_gt))
                L(nc.vector.tensor_tensor(NXT, NXT, TMP, ALU.add))
            L(nc.vector.tensor_tensor_scan(CE, cst("ones")[:, 0:NE], NXT, 0.0, ALU.mult, ALU.add))
            L(nc.vector.tensor_tensor(EXC, CE, NXT, ALU.subtract))
            shape = [P, NITEM, NE]
            item = cst("iota")[:, 0:NITEM].unsqueeze(2).broadcast_to(shape)
            exc, ce = (a.unsqueeze(1).broadcast_to(shape) for a in (EXC, CE))
            I(nc.vector.tensor_tensor(OX, item, exc, ALU.subtract))
            L(nc.vector.tensor_tensor(OH, item, ce, ALU.is_lt))
            L(nc.vector.scalar_tensor_tensor(out=OH, in0=OX, scalar=0.0, in1=OH, op0=ALU.is_ge, op1=ALU.mult))
            L(nc.vector.tensor_tensor(OX, OX, OH, ALU.mult))
            L(nc.vector.tensor_reduce(WIN, OX, AX.X, ALU.add))
            L(nc.vector.tensor_scalar(WIN, WIN, float(SLOTS_E), 2000.0, ALU.mult, ALU.add))
            for t in range(NT):
                L(nc.vector.tensor_tensor(OW, OH, RNK[:, t:t + 1, :].broadcast_to(shape), ALU.mult))
                L(nc.vector.tensor_reduce(RANK[:, t, :], OW, AX.X, ALU.add))
                I(nc.vector.tensor_tensor(RANK[:, t, :], RANK[:, t, :], WIN, ALU.subtract))
                L(nc.vector.tensor_tensor(OW, OH, GT2[:, t:t + 1, :].broadcast_to(shape), ALU.mult))
                L(nc.vector.tensor_reduce(GATE[:, t, :], OW, AX.X, ALU.add))
            L(nc.vector.tensor_tensor(OW, OH, cst("iota")[:, 0:NE].unsqueeze(1).broadcast_to(shape), ALU.mult))
            I(nc.vector.tensor_reduce(EID[:, 8:8 + NITEM], OW, AX.X, ALU.add))
            L(nc.vector.tensor_scalar(TMP[:, 0:NITEM // 2], cst("iota")[:, 0:NITEM // 2], 2.0, CE[:, NE - 1:NE], ALU.mult, ALU.is_lt))
            I(nc.vector.tensor_reduce(EID[:, 0:1], TMP[:, 0:NITEM // 2], AX.X, ALU.add))
            L(nc.vector.memset(EID[:, 1:8], 0.0))
            nc.vector.tensor_copy(ITI[:, 0:8 + NITEM], EID[:, 0:8 + NITEM]).then_inc(S("items"), 1)
            v.wait_ge(S("gates_t_ps"), 1)
            nc.vector.tensor_copy(GTT[0:NE, :], ps[0:NE, 2, 0:T]).then_inc(S("gates_t"), 1)

        hid = HT[:].rearrange("p a t -> p (a t)")
        XE = view(hid, 0, [KT, P])
        EH, EHT, EY = view(hid, 1024, [512]), view(hid, 1536, [4, P]), view(hid, 2048, [512])
        EPT = view(hid, 2560, [T])
        EG, EU, ES = (view(hid, 2816 + 512 * i, [512]) for i in range(3))
        EP0 = view(hid, 4352, [NT, 2, SLOTS_E])
        EPW = view(hid, 4608, [2, NT, 2, SLOTS_E])
        BG = [view(SB, 10240 + 1024 * q, [2, 512]) for q in range(2)]
        PAIR_SLOTS = 2 * ITEM_SLOTS

        def moe_pairs(eng):
            eng.wait_ge(S("items"), 1)
            return eng.value_load(ITI[0:1, 0:1], min_val=MIN_ITEM // 2, max_val=NITEM // 2)

        def moe_sp(sp):
            sp.wait_ge(S("h_ready"), 2)
            sp.dma_start(BD[0:NE, :], dram["b_down"]).then_inc(S("par2_loaded"), 16)
            with sp.Fori(0, moe_pairs(sp)) as it:
                for q in range(2):
                    e = sp.value_load(ITI[0:1, bass.ds(it * 2 + 8 + q, 1)], min_val=0, max_val=NE - 1)
                    for b in range(ITEM_SLOTS):
                        k = q * ITEM_SLOTS + b
                        sp.wait_ge(S("moe_slot"), it * PAIR_SLOTS + k + 1)
                        sp.dma_start(slot(S_MOE + k), dram["stream"][bass.ds(e * ITEM_SLOTS + S_MOE + b, 1), :, :]
                                     .rearrange("a p n -> (a p) n")).then_inc(arrived[(S_MOE + k) % RING], 16)
                        if b == 0:
                            sp.wait_ge(S("moe_bias_used"), it * 2 + q + 1)
                            for half in range(2):
                                sp.dma_start(BG[q][HD * half:HD * (half + 1), :, :].rearrange("p a n -> p (a n)"),
                                             dram["b_gu"][bass.ds(e * 2 + half, 1), :].broadcast_to([SLOTS_E, 1024])
                                             ).then_inc(S("moe_bias"), 16)

        def need_moe_slot(pe, it, k):
            i = S_MOE + k
            pe.wait_ge(arrived[i % RING], it * (16 * PAIR_SLOTS // RING) + 16 * (i // RING + 1))

        def moe_pe(pe):
            with pe.Fori(0, moe_pairs(pe)) as it:
                for q in range(2):
                    if q == 0:
                        pe.wait_ge(S("moe_p"), it + 1)
                        pe.wait_ge(S("moe_y_evac"), it * 2 + 1)
                        for k in range(KT):
                            for t in range(NT):
                                m = pe.matmul(ps[:, 2 + k // 4, (k % 4) * P:(k % 4 + 1) * P], HF[:, t, k * P:(k + 1) * P],
                                              EP0[:, t, :, :].rearrange("p a s -> p (a s)"), start=t == 0, stop=t == NT - 1)
                        m.then_inc(S("moe_xe_ps"), 1)
                        pe.wait_ge(S("moe_xe"), it * 2 + 2)
                    pe.wait_ge(S("moe_gu_evac"), it * 2 + q + 1)
                    for b in range(4):
                        need_moe_slot(pe, it, q * ITEM_SLOTS + b)
                        w = slot(S_MOE + q * ITEM_SLOTS + b).rearrange("p (k a h n) -> p k a h n", k=2, a=2, h=2)
                        for k in range(2):
                            for a in range(2):
                                for half in range(2):
                                    m = pe.matmul(ps[HD * half:HD * (half + 1), a, :],
                                                  XE[:, 2 * b + k, q * SLOTS_E:(q + 1) * SLOTS_E], w[:, k, a, half, :],
                                                  start=b + k == 0, stop=b + k == 4, skip_group_check=True)
                        m.then_inc(S("moe_slot"), 1)
                    pe.wait_ge(S("moe_h"), it * 2 + q + 1)
                    for f in range(4):
                        m = pe.transpose(ps[:, 2, f * P:(f + 1) * P], EH[:, f * P:(f + 1) * P], ident)
                    m.then_inc(S("moe_ht_ps"), 1)
                    pe.wait_ge(S("moe_ht"), it * 2 + q + 1)
                    for t in range(NT):
                        m = pe.transpose(ps[:, 2, t * P:(t + 1) * P], EPW[:, q, t, :, :].rearrange("p h s -> p (h s)"), ident)
                    m.then_inc(S("moe_pt_ps"), 1)
                    pe.wait_ge(S("moe_y_evac"), it * 2 + q + 1)
                    for b in range(2):
                        need_moe_slot(pe, it, q * ITEM_SLOTS + 4 + b)
                        w = slot(S_MOE + q * ITEM_SLOTS + 4 + b).rearrange("p (k c n) -> p k c n", k=4, c=2)
                        for k in range(4):
                            for c in range(2):
                                m = pe.matmul(ps[HD * c:HD * (c + 1), 3, :], EHT[:, k, HD * b:HD * (b + 1)], w[:, k, c, :],
                                              start=b + k == 0, stop=b + k == 4, skip_group_check=True)
                        m.then_inc(S("moe_slot"), 1)
                    pe.wait_ge(S("moe_pt"), it * 2 + q + 1)
                    pe.wait_ge(S("moe_y_evac"), it * 2 + q + 2)
                    for t in range(NT):
                        for c in range(2):
                            rows = slice(HD * c, HD * (c + 1))
                            m = pe.matmul(ps[:, 4 + 2 * t + c, :], EPT[rows, t * P:(t + 1) * P], EY[rows, :],
                                          start=False, stop=True, skip_group_check=True)
                    m.then_inc(S("moe_sc"), 1)
            pe.wait_ge(S("moe_last"), 1)
            for t in range(1):
                pe.transpose(ps[:, 0, 0:P], ident, ident).then_inc(S("moe_done"), 1)

        def moe_act(act):
            with act.Fori(0, moe_pairs(act)) as it:
                for q in range(2):
                    if q == 0:
                        act.wait_ge(S("moe_xe_ps"), it + 1)
                        for g in range(2):
                            nc.scalar.activation(XE[:, 4 * g:4 * g + 4, :].rearrange("p k s -> p (k s)"), ps[:, 2 + g, :],
                                                 ACT.Copy).then_inc(S("moe_xe"), 1)
                    act.wait_ge(S("moe_g"), it * 2 + q + 1)
                    nc.scalar.activation(ES, EG, ACT.Sigmoid, scale=SWIGLU_ALPHA).then_inc(S("moe_sig"), 1)
                    act.wait_ge(S("moe_ht_ps"), it * 2 + q + 1)
                    nc.scalar.activation(EHT.rearrange("p f s -> p (f s)"), ps[:, 2, :], ACT.Copy).then_inc(S("moe_ht"), 1)
                    act.wait_ge(S("moe_pt_ps"), it * 2 + q + 1)
                    act.wait_ge(S("moe_sc"), it * 2 + q + 1)
                    nc.scalar.activation(EPT, ps[:, 2, 0:T], ACT.Copy).then_inc(S("moe_pt"), 1)

        def moe_dve(v):
            v.sem_inc(S("moe_gu_evac"), 1)
            v.sem_inc(S("moe_y_evac"), 1)
            v.sem_inc(S("moe_sc"), 1)
            v.sem_inc(S("moe_bias_used"), 2)
            pairs = moe_pairs(v)
            iota = cst("iota")[:, 0:SLOTS_E]
            both = iota.unsqueeze(1).broadcast_to([P, 2, SLOTS_E])
            with v.Fori(0, pairs) as it:
                for q in range(2):
                    for t in range(NT):
                        nc.vector.tensor_scalar(EPW[:, q, t, :, :], both, RANK[:, t, bass.ds(it * 2 + q, 1)],
                                                GATE[:, t, bass.ds(it * 2 + q, 1)], ALU.is_equal, ALU.mult)
                for q in range(2):
                    for t in range(NT):
                        ins = nc.vector.tensor_scalar(EP0[:, t, q, :], iota, RANK[:, t, bass.ds(it * 2 + q, 1)], None, ALU.is_equal)
                ins.then_inc(S("moe_p"), 1)
                for q in range(2):
                    v.wait_ge(S("moe_slot"), it * PAIR_SLOTS + (RING + q * ITEM_SLOTS + 4))
                    v.wait_ge(S("moe_bias"), it * 64 + 32 * (q + 1))
                    nc.vector.tensor_tensor(EG, ps[:, 0, :], BG[q][:, 0, :], ALU.add).then_inc(S("moe_v"), 1)
                    nc.vector.tensor_tensor(EU, ps[:, 1, :], BG[q][:, 1, :], ALU.add).then_inc(S("moe_gu_evac"), 1)
                    v.wait_ge(S("moe_v"), it * 4 + 2 * q + 1)
                    nc.vector.tensor_scalar(EG, EG, LIMIT, None, ALU.min).then_inc(S("moe_g"), 1)
                    v.wait_ge(S("moe_gu_evac"), it * 2 + q + 2)
                    nc.vector.tensor_scalar(EU, EU, LIMIT, -LIMIT, ALU.min, ALU.max).then_inc(S("moe_bias_used"), 1)
                    v.wait_ge(S("moe_bias_used"), it * 2 + q + 3)
                    v.wait_ge(S("moe_g"), it * 2 + q + 1)
                    nc.vector.scalar_tensor_tensor(out=EU, in0=EU, scalar=1.0, in1=EG, op0=ALU.add,
                                                   op1=ALU.mult).then_inc(S("moe_v"), 1)
                    v.wait_ge(S("moe_v"), it * 4 + 2 * q + 2)
                    v.wait_ge(S("moe_sig"), it * 2 + q + 1)
                    nc.vector.tensor_tensor(EH, EU, ES, ALU.mult).then_inc(S("moe_h"), 1)
                    v.wait_ge(S("moe_slot"), it * PAIR_SLOTS + (RING + q * ITEM_SLOTS + 6))
                    v.wait_ge(S("moe_sc"), it * 2 + q + 1)
                    nc.vector.tensor_copy(EY, ps[:, 3, :]).then_inc(S("moe_y_evac"), 1)
            v.sem_inc(S("moe_last"), 1)

        def final_dve(v, I, L):
            v.wait_ge(S("moe_done"), 1)
            for t in range(NT):
                L(nc.vector.tensor_tensor(YT, bank(4 + 2 * t, 2), MOD[:, 5, :], ALU.mult))
                ins = nc.vector.tensor_tensor(X[:, t, :], X[:, t, :], YT, ALU.add)
                if t == 0:
                    L(ins)
            ins.then_inc(S("x_ready"), 1)
            v.wait_ge(S("x_ready"), 2 * DEPTH + 2)
            rms_dve(v, 2, L)
            v.wait_ge(S("gain_loaded"), 48)
            for t in range(NT):
                nc.vector.scalar_tensor_tensor(out=X[:, t, :], in0=X[:, t, :], scalar=SM[:, 98 + t:99 + t], in1=LNW,
                                               op0=ALU.mult, op1=ALU.mult).then_inc(S("final"), 1)

        HALF_LEVELS, ATT_LAG = 14, 5
        STEPS = HALF_LEVELS + 6
        ROPE, GLA_NORM, GLA_BACK, CMP_HIDDEN, CMP_GELU, CMP_TURN, CMP_OUT = 0, 1, 2, 4, 5, 6, 7

        def unit_scores(u):
            return 0 <= u < NU

        def unit_turn(u):
            return 1 <= u <= NU

        def unit_out(u):
            return 2 <= u <= NU + 1

        def mixers_pe(pe, l):
            for u in range(8):
                gla_scores_pe(pe, l, u)
                rwkv_pairs_pe(pe, l, u)
            rope_pe(pe, l)
            inverse_product_pe(pe, l, 0)
            for s in range(STEPS):
                u, at = s - ATT_LAG, NU * l + s - ATT_LAG
                j, part = divmod(s - HALF_LEVELS, 3)
                if s + 1 < HALF_LEVELS:
                    inverse_product_pe(pe, l, s + 1)
                if unit_scores(u):
                    if u == 0:
                        pe.wait_ge(S("rope"), l + 1)
                    if u == NU - 4:
                        pe.wait_ge(S("cmp_kv"), l + 1)
                    attention_scores_pe(pe, at)
                if s < HALF_LEVELS:
                    inverse_update_pe(pe, l, s)
                else:
                    (chunk_removed_pe, chunk_solve_pe, chunk_out_pe)[part](pe, l, j)
                if s == 0:
                    gla_out_pe(pe, l)
                if s == GLA_BACK:
                    back_pe(pe, 2 * l, G_XC, 4)
                if s == CMP_HIDDEN:
                    cmp_hidden_pe(pe, l)
                if s == CMP_TURN:
                    cmp_turn_pe(pe, l)
                if s == CMP_OUT:
                    cmp_out_pe(pe, l)
                if unit_turn(u):
                    attention_turn_pe(pe, at - 1)
                if unit_out(u):
                    if u == 2:
                        pe.wait_ge(S("cmp_kv"), l + 1)
                    attention_out_pe(pe, at - 2)
            back_pe(pe, 2 * l + 1, R_XC, 5)

        def mixers_act(act, l):
            for u in range(NQC):
                gla_key_act(act, l, u)
                if u == 1:
                    rwkv_bk_act(act, l)
            inverse_product_act(act, l, 0)
            for s in range(STEPS):
                u, at = s - ATT_LAG, NU * l + s - ATT_LAG
                if s + 1 < HALF_LEVELS:
                    inverse_product_act(act, l, s + 1)
                if s == 0:
                    nsa_gate_act(act, l)
                    gla_gate_act(act, l)
                if s == GLA_NORM:
                    head_norm_act(act, 2 * l)
                if s == CMP_GELU:
                    cmp_act(act, l)
                if unit_scores(u):
                    attention_exp_act(act, at)
                if unit_turn(u):
                    attention_out_act(act, at - 1)
            head_norm_act(act, 2 * l + 1)

        def mixers_dve(v, l, I, L):
            gla_key_dve(v, l, 0)
            gla_key_dve(v, l, 1)
            rwkv_init_dve(v, l, I, L)
            for u in range(8):
                rwkv_mask_dve(v, l, u)
                if u + 2 < NQC:
                    gla_key_dve(v, l, u + 2)
            v.wait_ge(S("rw_mm"), 8 * (l + 1))
            inverse_level_dve(v, l, 0)
            inverse_level_dve(v, l, 1)
            gla_mask_dve(v, l)
            v.wait_ge(S("rw_init"), l + 1)
            for s in range(STEPS):
                u, at = s - ATT_LAG, NU * l + s - ATT_LAG
                j, part = divmod(s - HALF_LEVELS, 3)
                if unit_turn(u):
                    attention_scale_dve(v, at - 1, L)
                if unit_scores(u):
                    if u == 0:
                        v.wait_ge(S("nsa_gate"), l + 1)
                    attention_scores_dve(v, at, I, L)
                if s < HALF_LEVELS:
                    inverse_update_dve(v, l, s)
                    if s + 2 < HALF_LEVELS:
                        inverse_level_dve(v, l, s + 2)
                elif part == 0:
                    chunk_removed_dve(v, l, j)
                elif part == 1:
                    chunk_solve_dve(v, l, j)
                elif j == 0:
                    chunk_state_dve(v, l, I)
                if s == ROPE:
                    rope_dve(v, l, I, L)
                if s == GLA_NORM:
                    gla_norm_dve(v, l, I, L)
                if s == GLA_BACK:
                    v.wait_ge(S("back_ps"), 2 * l + 1)
                    nc.vector.tensor_copy(OT[:, 0:2, :].rearrange("p c t -> p (c t)"), ps[:, 4, :]).then_inc(S("gla_out"), 1)
                if s == CMP_GELU:
                    cmp_hidden_dve(v, l, L)
                if s == CMP_TURN:
                    cmp_turn_dve(v, l)
                if s == CMP_OUT:
                    cmp_out_dve(v, l, I)
            rwkv_norm_dve(v, l, I, L)
            attention_merge_dve(v, NU * (l + 1), I)
            v.wait_ge(S("back_ps"), 2 * l + 2)
            nc.vector.tensor_copy(OT[:, 2:4, :].rearrange("p c t -> p (c t)"), ps[:, 5, :]).then_inc(S("rw_out"), 1)

        block = ctx.enter_context(nc.Block())

        @block.sync
        def _(sp):
            first_sp(sp)
            second_sp(sp)
            moe_sp(sp)
            sp.wait_ge(S("final"), NT)
            sp.dma_start(dram["out"].rearrange("(t p) d -> p t d", p=P), X[:]).then_inc(S("stored"), 16)
            sp.wait_ge(S("stored"), 16)

        @block.gpsimd
        def _(pool):
            for l in range(DEPTH):
                cmp_pool(pool, l)

        @block.tensor
        def _(pe):
            pe.wait_ge(S("const_loaded"), 16)
            for l in range(DEPTH):
                transpose_x_pe(pe, 2 * l, X, ("x_ready", 2 * l) if l else ("x_loaded", 16))
                project_pe(pe, l, range(5))
                gla_gate_pe(pe, l)
                rwkv_ranks_pe(pe, l)
                project_pe(pe, l, (5,))
                rwkv_norm_pe(pe, l)
                project_pe(pe, l, (6,))
                rwkv_bonus_pe(pe, l)
                mixers_pe(pe, l)
                mix_out_pe(pe, l)
                transpose_x_pe(pe, 2 * l + 1, X, ("x_ready", 2 * l + 1))
                ffn_pe(pe, l)
            modulation_pe(pe)
            transpose_x_pe(pe, 4, HF, ("h_ready", 1))
            project2_pe(pe)
            rg_pe(pe)
            pe.wait_ge(S("rg_gates"), 8)
            pe.wait_ge(S("proj2_evac"), 8)
            attention_scores_pe(pe, NU * DEPTH)
            for n in range(NU * DEPTH, len(UNITS)):
                if n + 1 < len(UNITS):
                    attention_scores_pe(pe, n + 1)
                attention_turn_pe(pe, n)
                attention_out_pe(pe, n)
            merge_pe(pe)
            transpose_x_pe(pe, 5, HF, ("h_ready", 2))
            router_pe(pe)
            moe_pe(pe)

        @block.scalar
        def _(act):
            I, L = link(act, "act_step")
            act.wait_ge(S("const_loaded"), 16)
            for l in range(DEPTH):
                act.wait_ge(S("par_loaded"), 16 * (l + 1))
                project_act(act, l, range(9))
                rwkv_ranks_act(act, l, I)
                project_act(act, l, (9,))
                gla_decay_act(act, l, L)
                rwkv_gates_act(act, l, I)
                project_act(act, l, (10,))
                gla_query_act(act, l)
                project_act(act, l, (11, 12))
                rwkv_decay_act(act, l, I)
                rwkv_values_act(act, l)
                project_act(act, l, (13, 14))
                mixers_act(act, l)
                layer_norm_act(act, 2 * l)
                ffn_act(act, l)
                layer_norm_act(act, 2 * l + 1)
            rms_act(act, 0, ("x_ready", 2 * DEPTH))
            project2_act(act)
            lru_act(act, I, L)
            attention_exp_act(act, NU * DEPTH)
            for n in range(NU * DEPTH, len(UNITS)):
                if n + 1 < len(UNITS):
                    attention_exp_act(act, n + 1)
                attention_out_act(act, n)
            merge_act(act)
            rms_act(act, 1, ("x_ready", 2 * DEPTH + 1))
            router_act(act)
            moe_act(act)
            rms_act(act, 2, ("x_ready", 2 * DEPTH + 2))

        @block.vector
        def _(v):
            I, L = link(v, "dve_step")
            v.wait_ge(S("const_loaded"), 16)
            for l in range(DEPTH):
                transpose_x_dve(v, 2 * l)
                mix_dve(v, l, I, L)
                rwkv_square_dve(v, l, I, L)
                gla_decay_dve(v, l, I, L)
                rwkv_prepare_dve(v, l, I, L)
                mixers_dve(v, l, I, L)
                if l == 0:
                    v.wait_ge(S("x_loaded"), 16)
                layer_norm_dve(v, 2 * l, 0, ("mix_ready", 2 * (l + 1)), I, L)
                transpose_x_dve(v, 2 * l + 1)
                ffn_dve(v, l)
                layer_norm_dve(v, 2 * l + 1, 4, ("down_ready", 6 * (l + 1)), I, L)
            modulation_dve(v, I, L)
            modulated_dve(v, 0, I, L)
            transpose_x_dve(v, 4)
            lru_dve(v, I, L)
            attention_scores_dve(v, NU * DEPTH, I, L)
            for n in range(NU * DEPTH, len(UNITS)):
                if n + 1 < len(UNITS):
                    attention_scores_dve(v, n + 1, I, L)
                attention_scale_dve(v, n, L)
            merge_dve(v, I, L)
            modulated_dve(v, 1, I, L)
            transpose_x_dve(v, 5)
            router_dve(v, I, L)
            moe_dve(v)
            final_dve(v, I, L)


def slots_of(w, cols):
    k, n = w.shape
    return w.reshape(k // P, P, n // cols, cols).transpose(2, 1, 0, 3).reshape(n // cols, P, SLOT)


def channels(v):
    return np.asarray(v).reshape(-1, P).T


def lay_out(a):
    f = np.float32
    a = {k: np.asarray(v) for k, v in a.items()}
    heads = np.arange(8)
    qperm = np.concatenate([np.arange(HD) + HD * (g * 4 + j) for j in range(4) for g in range(2)])
    stream = np.zeros((N_SLOTS, P, SLOT), f)
    layer = np.zeros((DEPTH, P, LAYER_COLS), f)
    head_norm = np.zeros((DEPTH, 4 * 256), f)

    def put(to, fields, name, value, rows=slice(0, P), at=0):
        x = fields[name][0] + at
        to[rows, x:x + value.shape[1]] = value

    for l in range(DEPTH):
        w = a["w_in"][l]
        gla, rw, nsa = w[:, :1040], w[:, 1040:2096], w[:, 2096:3400]
        zero = lambda n: np.zeros((D, n), f)
        vres = a["w_in_vres"][l - 1] if l else zero(32)
        kv = [nsa[:, 512 + P * i:512 + P * (i + 1)] for i in range(6)]
        misc = np.concatenate([rw[:, 1024:1056], vres, gla[:, 1024:1040], zero(48)], 1)
        cols = np.concatenate([gla[:, 0:512], rw[:, 0:512], rw[:, 512:768], rw[:, 768:896], rw[:, 896:1024], misc,
                               kv[1], kv[0], kv[2], kv[4], nsa[:, qperm][:, 0:512],
                               kv[3], kv[5], nsa[:, 1280:1304], zero(104), gla[:, 512:1024]], 1)
        s = l * LAYER_SLOTS
        stream[s:s + 7] = slots_of(cols, 512)
        for i, name in enumerate(("nsa_wk1", "nsa_wv1")):
            stream[s + S_CMP + i] = a[name][l].reshape(16, P, 256).transpose(1, 0, 2).reshape(P, SLOT)
        rows = np.concatenate([np.arange(512), 512 + qperm])
        stream[s + S_WO:s + S_GU] = slots_of(a["w_out"][l][rows], 512)
        g, u = (a[n][l].reshape(D, 11, 256) for n in ("ffn_w_gate", "ffn_w_up"))
        stream[s + S_GU:s + S_DN] = slots_of(np.stack([g, u], 2).reshape(D, 11 * 512), 512)
        down = np.zeros((24, P, D), f)
        down[:NF] = a["ffn_w_down"][l].reshape(NF, P, D)
        stream[s + S_DN:s + LAYER_SLOTS] = down.reshape(6, 4, P, D).transpose(0, 2, 1, 3).reshape(6, P, SLOT)
        to = layer[l]
        mu = np.zeros(9 * P, f)
        mu[0:1024], mu[1024:1056] = a["rwkv_mu"][l][0:1024], a["rwkv_mu"][l][1024:1056]
        if l:
            mu[1056:1088] = a["rwkv_mu_vres"][l - 1]
        put(to, LAYER_FIELDS, "mu", channels(mu))
        for field, name in (("b_a", "gla_b_a"), ("w0", "rwkv_w0"), ("a0", "rwkv_a0"), ("k_k", "rwkv_k_k"), ("k_a", "rwkv_k_a")):
            put(to, LAYER_FIELDS, field, channels(a[name][l]))
        rk = np.zeros((2, P, 4), f)
        for h in range(4):
            rk[h // 2, HD * (h % 2):HD * (h % 2 + 1), h] = a["rwkv_r_k"][l][h]
        put(to, LAYER_FIELDS, "r_k", rk.transpose(1, 0, 2).reshape(P, 8))
        put(to, LAYER_FIELDS, "wa", a["rwkv_w2"][l], slice(0, 64))
        put(to, LAYER_FIELDS, "wa", a["rwkv_a2"][l], slice(64, 128))
        put(to, LAYER_FIELDS, "g2", a["rwkv_g2"][l][0:P])
        put(to, LAYER_FIELDS, "misc", a["rwkv_g2"][l][P:160], slice(M_G2, M_G2 + 32))
        if l:
            put(to, LAYER_FIELDS, "misc", a["rwkv_v2"][l - 1], slice(M_VR, M_VR + 32))
            put(to, LAYER_FIELDS, "v0", channels(a["rwkv_v0"][l - 1]))
        put(to, LAYER_FIELDS, "misc", a["gla_w_a2"][l], slice(M_GA, M_GA + 16))
        for field, name in (("wk2", "nsa_wk2"), ("wv2", "nsa_wv2")):
            put(to, LAYER_FIELDS, field, a[name][l].reshape(2, P, HD).transpose(1, 0, 2).reshape(P, P))
        for field, name in (("pos_k", "nsa_pos_k"), ("pos_v", "nsa_pos_v")):
            put(to, LAYER_FIELDS, field, np.concatenate([a[name][l].T] * 2, 0))
        head_norm[l] = np.concatenate([a[n][l] for n in ("gla_ln_w", "gla_ln_b", "rwkv_ln_w", "rwkv_ln_b")])
    stream[S_ADA:S_IN2] = slots_of(a["w_ada_2"][0], 512)
    w = a["w_in_2"][0]
    cols = np.concatenate([w[:, qperm], w[:, 512:640], w[:, 768:1280], w[:, 1280:1792], w[:, 640:768], np.zeros((D, 256), f)], 1)
    stream[S_IN2:S_WO2] = slots_of(cols, 512)
    rows = np.concatenate([qperm, 512 + np.arange(512)])
    stream[S_WO2:S_MOE] = slots_of(a["w_out_2"][0][rows], 512)
    moe = stream[S_MOE:].reshape(NE, ITEM_SLOTS, P, SLOT)
    moe[:, 0:4] = a["w_gu_2"][0].reshape(NE, 4, 2, P, 2 * DE).transpose(0, 1, 3, 2, 4).reshape(NE, 4, P, SLOT)
    moe[:, 4:6] = a["w_down_2"][0].reshape(NE, 2, 4, P, D).transpose(0, 1, 3, 2, 4).reshape(NE, 2, P, SLOT)
    second = np.zeros((P, SECOND_COLS), f)
    F2 = SECOND_FIELDS
    put(second, F2, "c", channels(a["c_2"][0]))
    put(second, F2, "conv_w", a["conv_w_2"][0].reshape(4, 4, P).transpose(2, 1, 0).reshape(P, 16))
    put(second, F2, "conv_b", channels(a["conv_b_2"][0]))
    for field, name in (("rg_a", "w_rg_a_2"), ("rg_x", "w_rg_x_2")):
        for c in range(4):
            for h in range(2):
                put(second, F2, field, a[name][0][2 * c + h], slice(HD * h, HD * (h + 1)), c * P + h * HD)
    put(second, F2, "b_a", channels(a["b_rg_a_2"][0]))
    put(second, F2, "b_x", channels(a["b_rg_x_2"][0]))
    put(second, F2, "lam", channels(a["lru_lambda_2"][0]))
    put(second, F2, "g_attn", channels(a["g_attn_out_2"][0][qperm]))
    put(second, F2, "g_lru", channels(a["g_lru_out_2"][0]))
    put(second, F2, "router", a["w_router_2"][0].reshape(KT, P, NE).transpose(1, 0, 2).reshape(P, KT * NE))
    return {
        "x": a["x"][0], "stream": stream, "layer": layer, "head_norm": head_norm, "second": second,
        "ln": np.stack([a[n][l] for l in range(DEPTH) for n in ("ln1_w", "ln1_b", "ln2_w", "ln2_b")]),
        "b_ada": a["b_ada_2"], "small": np.concatenate([a["b_router_2"][0], a["sinks_2"][0]])[None],
        "gains": np.stack([a["g_mix_2"][0], a["g_ffn_2"][0], a["g_final_2"]]),
        "b_down": a["b_down_2"][0],
        "b_gu": a["b_gu_2"][0].reshape(NE, 2, 2, 512).transpose(0, 2, 1, 3).reshape(2 * NE, 1024),
        "const": constants(),
    }


def kernel(**inputs):
    import concourse.bacc as bacc
    from concourse.bass_utils import run_bass_kernel_spmd

    nc = bacc.Bacc("TRN2", target_bir_lowering=False, num_devices=1)
    arrays = {f"in_{k}": np.ascontiguousarray(v) for k, v in lay_out(inputs).items()}
    dram = {k[3:]: nc.dram_tensor(k, v.shape, F32, kind="ExternalInput").ap() for k, v in arrays.items()}
    dram["out"] = nc.dram_tensor("out_0", (T, D), F32, kind="ExternalOutput").ap()
    program(nc, dram)
    r = run_bass_kernel_spmd(nc, [arrays], core_ids=[0])
    return r.results[0]["out_0"].reshape(1, T, D)
```

```python
from contextlib import ExitStack

import numpy as np

import concourse.bass as bass
from concourse import mybir

F32 = mybir.dt.float32
I32 = mybir.dt.int32
ALU = mybir.AluOpType
ACT = mybir.ActivationFunctionType
AX = mybir.AxisListType

P = 128
T = 256
NT = T // P
D = 1024
KT = D // P
DEPTH = 2
HD = 64
FFN = 2816
NF = FFN // P
ALPHA = float((2 * DEPTH) ** 0.25)
LN_EPS, RWKV_EPS, RMS_EPS = 1e-5, 64e-5, 1e-6
MASK_NEG = -1e30
DECAY = -float(np.exp(np.float32(-0.5)))
GLA_TAU = 16.0
QC = 32
NQC = T // QC
EXP_CAP = 1e17
NE, TOPK = 32, 4
DE = 1024
SLOTS_E = 64
NITEM = NE + T * TOPK // SLOTS_E
MIN_ITEM = T * TOPK // SLOTS_E
LIMIT, SWIGLU_ALPHA = 7.0, 1.702
LRU_C = 8.0
GELU_C, GELU_K = 0.7978845608028654, 0.044715

SLOT = 4096
RING = 4
ADA = 12 // DEPTH
S_IN, S_ADA, S_CMP, S_WO, S_GU, S_DN = 0, 7, 7 + ADA, 9 + ADA, 11 + ADA, 22 + ADA
LAYER_SLOTS = 28 + ADA
S_IN2 = DEPTH * LAYER_SLOTS
S_WO2 = S_IN2 + 4
S_MOE = S_WO2 + 2
ITEM_SLOTS = 6
N_SLOTS = S_MOE + ITEM_SLOTS * NE
assert (2 * ITEM_SLOTS) % RING == 0

T_GQ, T_GK, T_R, T_K, T_V, T_WA, T_G1, T_MISC, T_VC, T_KC, T_KS, T_KW, T_Q = 0, 2, 4, 6, 8, 10, 11, 12, 13, 14, 15, 16, 17
NCT = 21
M_G2, M_VR, M_GA = 0, 32, 64


def layout(fields):
    at, offsets = 0, {}
    for name, width in fields:
        offsets[name] = (at, at + width)
        at += width
    return offsets, at


LAYER_FIELDS, LAYER_COLS = layout([
    ("mu", 9), ("b_a", 2), ("w0", 2), ("a0", 2), ("v0", 2), ("k_k", 2), ("k_a", 2), ("r_k", 8),
    ("wa", 256), ("g2", 256), ("misc", 256), ("wk2", 128), ("wv2", 128), ("pos_k", 32), ("pos_v", 32)])
SECOND_FIELDS, SECOND_COLS = layout([
    ("conv_w", 16), ("conv_b", 4), ("rg_a", 512), ("rg_x", 512), ("b_a", 4), ("b_x", 4), ("lam", 4),
    ("g_attn", 4), ("g_lru", 4), ("router", 8 * NE)])
CONST_FIELDS, CONST_COLS = layout([
    ("ident", P), ("diag_add", P), ("prev_add", P), ("pairs", 4 * P), ("levels", 7 * P), ("ones", T),
    ("head_ones", P), ("rot", P), ("cos", T), ("sin", T), ("iota", P), ("cmp_add", 30), ("cmp_any", 2), ("fold", 1), ("part", 1), ("eps", 1)])


def constants():
    f = np.float32
    c = {}
    i, j = np.arange(P)[:, None], np.arange(P)[None, :]
    c["ident"] = (i == j).astype(f)
    c["diag_add"] = np.where(j <= i, 0, MASK_NEG).astype(f)
    c["prev_add"] = np.where(j > i, 0, MASK_NEG).astype(f)
    strict, incl = (i < j).astype(f), (i <= j).astype(f)
    c["pairs"] = np.concatenate([strict, incl, strict, incl], 1)
    level = []
    for n in range(7):
        b = 1 << n
        level.append(((i // (2 * b) == j // (2 * b)) & (i // b % 2 == 0) & (j // b % 2 == 1)).astype(f))
    c["levels"] = np.concatenate(level, 1)
    c["ones"] = np.ones((P, T), f)
    c["head_ones"] = (i // HD == j // HD).astype(f)
    half = HD // 2
    rot = np.zeros((P, P), f)
    for m in range(P):
        if m % HD < half:
            rot[m + half, m] = -1
        else:
            rot[m - half, m] = 1
    c["rot"] = rot
    inv = (f(10000.0) ** (-np.arange(half, dtype=f) / f(half))).astype(f)
    ang = (np.arange(T, dtype=f)[:, None] * inv).astype(f)
    row = np.arange(P) % half
    c["cos"], c["sin"] = np.cos(ang).astype(f).T[row], np.sin(ang).astype(f).T[row]
    c["iota"] = np.broadcast_to(np.arange(P, dtype=f), (P, P))
    pos = np.arange(P)[:, None, None] + P * np.arange(NT)[None, :, None]
    seen = 16 * np.arange(15)[None, None, :] + 31 <= pos
    c["cmp_add"] = np.where(seen, 0, MASK_NEG).astype(f).reshape(P, 30)
    c["cmp_any"] = seen.any(-1).astype(f)
    c["part"] = np.arange(P, dtype=f)[:, None]
    c["eps"] = np.full((P, 1), RMS_EPS, f)
    c["fold"] = (np.arange(P)[:, None] % 32 == 0).astype(f)
    out = np.zeros((P, CONST_COLS), f)
    for name, (a, b) in CONST_FIELDS.items():
        out[:, a:b] = c[name]
    return out


def program(nc, dram):
    ctx = ExitStack()
    with ctx:
        def sb(name, shape, dt=F32):
            return ctx.enter_context(nc.sbuf_tensor(name, shape, dt))

        sems = {}

        def S(name):
            if name not in sems:
                sems[name] = ctx.enter_context(nc.semaphore(name))
            return sems[name]

        ring = sb("ring", [P, RING, SLOT])
        X = sb("X", [P, NT, D])
        XT = sb("XT", [P, KT, T])
        OT = XT
        HT = sb("HT", [P, NF, T])
        TOK = sb("TOK", [P, NT, 512])
        NV = sb("NV", [P, NT, 280])
        CST = sb("CST", [P, CONST_COLS])
        PAR = sb("PAR", [P, max(LAYER_COLS, SECOND_COLS)])
        HN = sb("HN", [P, 4, 256])
        VF = sb("VF", [P, 2, T])
        SA = sb("SA", [P, 5120])
        SB = sb("SB", [P, 14272])
        SM = sb("SM", [P, 176])
        COND = sb("COND", [P, KT + 6 * KT])
        ps = ctx.enter_context(nc.psum_tensor("ps", [P, 8, 512], F32))

        ITI = SA[:, 5056:5056 + 8 + NITEM].bitcast(I32)

        def cst(name):
            a, b = CONST_FIELDS[name]
            return CST[:, a:b]

        def par(name, fields=LAYER_FIELDS):
            a, b = fields[name]
            return PAR[:, a:b]

        def par2(name):
            return par(name, SECOND_FIELDS)

        def view(region, at, shape):
            n = int(np.prod(shape))
            v = region[:, at:at + n]
            if len(shape) == 2:
                v = v.rearrange("p (a b) -> p a b", a=shape[0])
            elif len(shape) == 3:
                v = v.rearrange("p (a b c) -> p a b c", a=shape[0], b=shape[1])
            elif len(shape) == 4:
                v = v.rearrange("p (a b c d) -> p a b c d", a=shape[0], b=shape[1], c=shape[2])
            return v

        def bank(b, n=1):
            return ps[:, b:b + n, :].rearrange("p a n -> p (a n)")

        ident = cst("ident")
        LNW, LNB = view(SB, 0, [D]), view(SB, D, [D])
        SQ = view(SB, 2 * D, [D])
        arrived = [S(f"slot_arrived{b}") for b in range(RING)]

        def slot(i):
            return ring[:, i % RING, :]

        def need_slot(eng, i):
            eng.wait_ge(arrived[i % RING], 16 * (i // RING + 1))

        def released(i):
            if i < S_IN2:
                l, s = divmod(i, LAYER_SLOTS)
                if s < S_ADA:
                    return "proj_ready", 15 * l + [2, 4, 6, 8, 10, 13, 15][s]
                if s < S_CMP:
                    return "mod_ready", ADA * l + s - S_ADA + 1
                if s < S_WO:
                    return "cmp_hidden", l + 1
                if s < S_GU:
                    return "mix_ready", 2 * l + 2
                if s < S_DN:
                    return "ffn_ready", 11 * l + s - S_GU + 1
                return "down_ready", 7 * l + (s - S_DN + 1 if s < LAYER_SLOTS - 1 else 7)
            if i < S_WO2:
                return "proj2_ready", [2, 4, 6, 8][i - S_IN2]
            return "mix2_ready", i - S_WO2 + 1

        def link(eng, name):
            n = [0]

            def step(ins):
                n[0] += 1
                ins.then_inc(S(name), 1)

            def joined(ins):
                step(ins)
                eng.wait_ge(S(name), n[0])
            return step, joined

        def stream(sp, i):
            if i >= RING:
                name, value = released(i - RING)
                sp.wait_ge(S(name), value)
            sp.dma_start(slot(i), dram["stream"][i]).then_inc(arrived[i % RING], 16)

        def layer_params(sp, l):
            if l:
                for done in ("gla_out", "rw_out", "nsa_out"):
                    sp.wait_ge(S(done), l)
            sp.dma_start(PAR[:, 0:LAYER_COLS], dram["layer"][l]).then_inc(S("par_loaded"), 16)
            sp.dma_start(HN[:].rearrange("p a b -> p (a b)"),
                         dram["head_norm"][l:l + 1, :].broadcast_to([P, 1024])).then_inc(S("par_loaded"), 16)

        def norm_params(sp, n):
            if n % 2:
                sp.wait_ge(S("x_ready"), n)
            else:
                sp.wait_ge(S("rw_y"), n + 2)
            sp.dma_start(LNW, dram["ln"][2 * n:2 * n + 1, :].broadcast_to([P, D])).then_inc(S("ln_loaded"), 16)
            sp.dma_start(LNB, dram["ln"][2 * n + 1:2 * n + 2, :].broadcast_to([P, D])).then_inc(S("ln_loaded"), 16)

        def first_sp(sp):
            sp.dma_start(X[:], dram["x"].rearrange("(t p) d -> p t d", p=P)).then_inc(S("x_loaded"), 16)
            sp.dma_start(CST[:, 0:P], dram["const"][:, 0:P]).then_inc(S("x_loaded"), 16)
            stream(sp, 0)
            need_slot(sp, 0)
            sp.dma_start(CST[:, P:CONST_COLS], dram["const"][:, P:CONST_COLS]).then_inc(S("start_loaded"), 16)
            sp.dma_start(COND[:], dram["cond"]).then_inc(S("start_loaded"), 16)
            for l in range(DEPTH):
                for s in range(LAYER_SLOTS):
                    if l + s:
                        stream(sp, l * LAYER_SLOTS + s)
                    if l == 0 and s == 1:
                        layer_params(sp, 0)
                    if s == S_WO + RING - 1:
                        norm_params(sp, 2 * l)
                    if s == S_GU + 8:
                        norm_params(sp, 2 * l + 1)
                        if l + 1 < DEPTH:
                            layer_params(sp, l + 1)
                        else:
                            for n in range(2):
                                sp.dma_start(GAINS[:, n, :], dram["gains"][n:n + 1, :].broadcast_to([P, D])).then_inc(S("gain_loaded"), 16)

        def turned_bank(n):
            return (0, 4, 0, 4, 0, 1)[n]

        def transpose_x_pe(pe, n, src, ready):
            b0 = turned_bank(n)
            for t in range(NT):
                pe.wait_ge(S(ready[t][0]), ready[t][1])
                for b in range(4):
                    for k in range(2):
                        m = pe.transpose(ps[:, b0 + b, (k * NT + t) * P:(k * NT + t + 1) * P],
                                         src[:, t, (2 * b + k) * P:(2 * b + k + 1) * P], ident)
                    if t == NT - 1:
                        m.then_inc(S("xt_ps"), 1)

        def transpose_x_dve(v, n):
            for b in range(4):
                v.wait_ge(S("xt_ps"), 4 * n + b + 1)
                nc.vector.tensor_copy(XT[:, 2 * b:2 * b + 2, :].rearrange("p k t -> p (k t)"),
                                      ps[:, turned_bank(n) + b, :]).then_inc(S("xt_ready"), 1)

        def proj_bank(g):
            return g % 4 if g < 13 else g - 9

        def project_pe(pe, l, slots):
            base = l * LAYER_SLOTS
            pe.wait_ge(S("xt_ready"), 4 * (2 * l + 1))

            def bank_free(g):
                if g >= 13:
                    pe.wait_ge(S("gla_zb"), l + 1)
                    pe.wait_ge(S("rw_gates"), l + 1)
                elif g >= 4:
                    pe.wait_ge(S("proj_evac"), 15 * l + g - 3)

            for s in slots:
                need_slot(pe, base + s)
                w = slot(base + s).rearrange("p (k n) -> p k n", k=KT)
                if s < 5:
                    for g in (2 * s, 2 * s + 1):
                        bank_free(g)
                        for j in range(2):
                            for k in range(KT):
                                m = pe.matmul(ps[:, proj_bank(g), j * T:(j + 1) * T],
                                              w[:, k, (2 * (g % 2) + j) * P:(2 * (g % 2) + j + 1) * P],
                                              XT[:, k, :], start=k == 0, stop=k == KT - 1)
                        m.then_inc(S("proj_ready"), 1)
                    continue
                if s == 5:
                    bank_free(10)
                    for k in range(KT):
                        m = pe.matmul(ps[:, proj_bank(10), 0:T], w[:, k, 0:P], XT[:, k, :], start=k == 0, stop=k == KT - 1)
                    m.then_inc(S("proj_ready"), 1)
                a, n, g0 = (P, 280, 11) if s == 5 else (0, 512, 13)
                for t in range(NT):
                    bank_free(g0 + t)
                    for k in range(KT):
                        m = pe.matmul(ps[:, proj_bank(g0 + t), 0:n], XT[:, k, t * P:(t + 1) * P], w[:, k, a:a + n],
                                      start=k == 0, stop=k == KT - 1)
                    m.then_inc(S("proj_ready"), 1)

        def project_act(act, l, groups):
            for g in groups:
                act.wait_ge(S("proj_ready"), 15 * l + g + 1)
                if g < 10:
                    to, n = HT[:, 2 * g:2 * g + 2, :].rearrange("p a t -> p (a t)"), 512
                elif g == 10:
                    to, n = HT[:, 20, :], T
                elif g < 13:
                    to, n = NV[:, g - 11, :], 280
                else:
                    to, n = TOK[:, g - 13, :], 512
                nc.scalar.activation(to, ps[:, proj_bank(g), 0:n], ACT.Copy,
                                     scale=HD ** -0.5 if g == 0 else 1.0).then_inc(S("proj_evac"), 1)

        def mix_dve(v, l, I, L):
            v.wait_ge(S("proj_evac"), 15 * l + 7)
            v.wait_ge(S("par_loaded"), 32 * (l + 1))
            HX = HT[:, T_R:T_MISC + 1, :]
            MD = view(SB, 0, [9, T])
            I(nc.vector.tensor_tensor(MD[:, :, 1:T], HX[:, :, 0:T - 1], HX[:, :, 1:T], ALU.subtract))
            L(nc.vector.tensor_scalar(MD[:, :, 0:1], HX[:, :, 0:1], -1.0, None, ALU.mult))
            for j in range(9):
                ins = nc.vector.scalar_tensor_tensor(out=HX[:, j, :], in0=MD[:, j, :], scalar=par("mu")[:, j:j + 1],
                                                     in1=HX[:, j, :], op0=ALU.mult, op1=ALU.add)
                if j < 8:
                    I(ins)
            ins.then_inc(S("mixed"), 1)
            v.wait_ge(S("mixed"), l + 1)

        def head_norm_dve(v, I, L, src, eps, which, n, XC, SQ2):
            s8, v8, d8, r8 = (SM[:, 8 * i:8 * i + 8] for i in range(4))
            X8 = XC.rearrange("p (a b) -> p a b", b=HD)
            L(nc.vector.tensor_reduce(s8, src, AX.X, ALU.add))
            L(nc.vector.tensor_scalar(s8, s8, 1.0 / HD, None, ALU.mult))
            L(nc.vector.tensor_tensor(X8, src, s8.unsqueeze(2).broadcast_to([P, 8, HD]), ALU.subtract))
            L(nc.vector.tensor_tensor(SQ2, XC, XC, ALU.mult))
            L(nc.vector.tensor_reduce(v8, SQ2.rearrange("p (a b) -> p a b", b=HD), AX.X, ALU.add))
            nc.vector.tensor_scalar(v8, v8, 1.0 / HD, eps, ALU.mult, ALU.add).then_inc(S("head_var"), 1)
            v.wait_ge(S("head_std"), n + 1)
            L(nc.vector.reciprocal(r8, d8))
            L(nc.vector.tensor_tensor(X8, X8, r8.unsqueeze(2).broadcast_to([P, 8, HD]), ALU.mult))
            X2 = XC.rearrange("p (t c) -> p t c", t=NT)
            v.wait_ge(S("par_loaded"), 32 * (n // 2 + 1))
            L(nc.vector.tensor_tensor(X2, X2, HN[:, which:which + 1, :].broadcast_to([P, NT, 256]), ALU.mult))
            L(nc.vector.tensor_tensor(X2, X2, HN[:, which + 1:which + 2, :].broadcast_to([P, NT, 256]), ALU.add))

        def head_norm_act(act, n):
            act.wait_ge(S("head_var"), n + 1)
            nc.scalar.activation(SM[:, 16:24], SM[:, 8:16], ACT.Sqrt).then_inc(S("head_std"), 1)

        G_LB, G_T0, G_T1 = view(SA, 0, [2, T]), view(SA, 512, [2, T]), view(SA, 1024, [2, T])
        G_EK = [view(SA, 1536 + 512 * i, [2, T]) for i in range(2)]
        G_KH = [view(SA, 2560 + 512 * i, [2, T]) for i in range(2)]
        G_ST = view(SA, 3584, [4, 384])

        def gla_gate_pe(pe, l):
            if l == 0:
                pe.wait_ge(S("start_loaded"), 32)
            pe.wait_ge(S("mixed"), l + 1)
            for c in range(2):
                m = pe.matmul(ps[:, 4, c * T:(c + 1) * T], par("misc")[M_GA:M_GA + 16, c * P:(c + 1) * P],
                              HT[M_GA:M_GA + 16, T_MISC, :], start=True, stop=True)
            m.then_inc(S("gla_z"), 1)

        def gla_scores_pe(pe, l, tc):
            pe.wait_ge(S("gla_k"), NQC * l + tc + 1)
            if tc == 0:
                pe.wait_ge(S("proj_evac"), 15 * l + 13)
            for h in range(4):
                c, pb = h // 2, HD * (h % 2)
                for st in range(tc * QC // P + 1):
                    at = tc * QC if st == 0 else T + tc * QC - P
                    m = pe.matmul(ps[:, h, at:at + QC], G_KH[tc % 2][pb:pb + HD, c, st * P:(st + 1) * P],
                                  HT[pb:pb + HD, T_GQ + c, tc * QC:(tc + 1) * QC], start=True, stop=True)
            m.then_inc(S("gla_sc"), 1)

        def gla_out_pe(pe, l):
            pe.wait_ge(S("gla_st"), 3 * (l + 1))
            pe.wait_ge(S("proj_evac"), 15 * (l + 1))
            pe.wait_ge(S("rw_init"), l + 1)
            for t in range(NT):
                for h in range(4):
                    for s in range(t + 1):
                        at = t * P if s == 0 else T
                        m = pe.matmul(ps[:, 4, (4 * t + h) * HD:(4 * t + h + 1) * HD], G_ST[:, h, at:at + P],
                                      TOK[:, s, h * HD:(h + 1) * HD], start=s == 0, stop=s == t)
            m.then_inc(S("gla_o"), 1)

        def back_pe(pe, n, XC, b):
            pe.wait_ge(S("head_out"), n + 1)
            X2 = XC.rearrange("p (t c) -> p t c", t=NT)
            for c in range(2):
                for t in range(NT):
                    m = pe.transpose(ps[:, b, c * T + t * P:c * T + (t + 1) * P], X2[:, t, c * P:(c + 1) * P], ident)
            m.then_inc(S("back_ps"), 1)

        def gla_decay_act(act, l, L):
            act.wait_ge(S("gla_zb"), l + 1)
            L(nc.scalar.activation(G_T0, G_T1, ACT.Abs))
            L(nc.scalar.activation(G_T0, G_T0, ACT.Exp, scale=-1.0))
            nc.scalar.activation(G_T0, G_T0, ACT.Ln, bias=cst("ones")[:, 0:1]).then_inc(S("gla_lp"), 1)

        def gla_query_act(act, l):
            act.wait_ge(S("gla_df"), l + 1)
            nc.scalar.activation(G_T0, G_T1, ACT.Exp).then_inc(S("gla_eq"), 1)

        def gla_key_act(act, l, tc):
            if tc >= 2:
                act.wait_ge(S("gla_k"), NQC * l + tc - 1)
            w, ref = (tc * QC // P + 1) * P, tc * QC + QC // 2 - 1
            for c in range(2):
                nc.scalar.activation(G_EK[tc % 2][:, c, 0:w], G_LB[:, c, 0:w], ACT.Exp, scale=-1.0,
                                     bias=G_LB[:, c, ref:ref + 1]).then_inc(S("gla_ek"), 1)

        def gla_decay_dve(v, l, I, L):
            v.wait_ge(S("gla_z"), l + 1)
            for c in range(2):
                ins = nc.vector.tensor_scalar(G_T1[:, c, :], ps[:, 4, c * T:(c + 1) * T], par("b_a")[:, c:c + 1], None, ALU.add)
                if c == 0:
                    I(ins)
            ins.then_inc(S("gla_zb"), 1)
            v.wait_ge(S("gla_zb"), l + 1)
            v.wait_ge(S("gla_lp"), l + 1)
            L(nc.vector.scalar_tensor_tensor(out=G_T1, in0=G_T1, scalar=0.0, in1=G_T0, op0=ALU.min, op1=ALU.subtract))
            for c in range(2):
                (I if c == 0 else L)(nc.vector.tensor_tensor_scan(G_LB[:, c, :], cst("ones"), G_T1[:, c, :], 0.0,
                                                                  ALU.mult, ALU.add))
            L(nc.vector.tensor_scalar(G_LB, G_LB, 1.0 / GLA_TAU, None, ALU.mult))
            lb4 = G_LB.rearrange("p c (n q) -> p (c n) q", q=QC)
            t14 = G_T1.rearrange("p c (n q) -> p (c n) q", q=QC)
            nc.vector.tensor_tensor(t14, lb4, lb4[:, :, QC // 2 - 1:QC // 2].broadcast_to([P, 2 * NQC, QC]),
                                    ALU.subtract).then_inc(S("gla_df"), 1)
            v.wait_ge(S("gla_eq"), l + 1)
            q = HT[:, T_GQ:T_GQ + 2, :]
            nc.vector.scalar_tensor_tensor(out=q, in0=G_T0, scalar=EXP_CAP, in1=q, op0=ALU.min,
                                           op1=ALU.mult).then_inc(S("gla_q"), 1)

        def gla_key_dve(v, l, tc):
            v.wait_ge(S("gla_ek"), 2 * NQC * l + 2 * tc + 2)
            if tc >= 2:
                v.wait_ge(S("gla_sc"), NQC * l + tc - 1)
            w = (tc * QC // P + 1) * P
            nc.vector.scalar_tensor_tensor(out=G_KH[tc % 2][:, :, 0:w], in0=G_EK[tc % 2][:, :, 0:w], scalar=EXP_CAP,
                                           in1=HT[:, T_GK:T_GK + 2, 0:w], op0=ALU.min, op1=ALU.mult).then_inc(S("gla_k"), 1)

        def gla_mask_dve(v, l):
            v.wait_ge(S("gla_sc"), NQC * (l + 1))
            incl = cst("pairs")[:, P:2 * P].unsqueeze(1).broadcast_to([P, 4, P])
            nc.vector.tensor_tensor(G_ST[:, :, 0:P], ps[:, 0:4, 0:P], incl, ALU.mult).then_inc(S("gla_st"), 1)
            nc.vector.tensor_copy(G_ST[:, :, P:T], ps[:, 0:4, P:T]).then_inc(S("gla_st"), 1)
            nc.vector.tensor_tensor(G_ST[:, :, T:T + P], ps[:, 0:4, T:T + P], incl, ALU.mult).then_inc(S("gla_st"), 1)

        G_XC, G_SQ, G_SG = view(SA, 1536, [512]), view(SA, 2048, [512]), view(SA, 512, [512])

        def gla_norm_dve(v, l, I, L):
            v.wait_ge(S("gla_o"), l + 1)
            head_norm_dve(v, I, L, ps[:, 4, :].rearrange("p (a b) -> p a b", b=HD), LN_EPS, 0, 2 * l, G_XC, G_SQ)
            v.wait_ge(S("gla_sg"), l + 1)
            sg, xc = (a.rearrange("p (t c) -> p t c", t=NT) for a in (G_SG, G_XC))
            L(nc.vector.tensor_tensor(sg, sg, TOK[:, :, 256:512], ALU.mult))
            nc.vector.tensor_tensor(xc, xc, sg, ALU.mult).then_inc(S("head_out"), 1)

        def gla_gate_act(act, l):
            act.wait_ge(S("gla_st"), 3 * (l + 1))
            nc.scalar.activation(G_SG.rearrange("p (t c) -> p t c", t=NT), TOK[:, :, 256:512],
                                 ACT.Sigmoid).then_inc(S("gla_sg"), 1)

        MM = view(SB, 0, [8, 4, P])
        TM, TT = view(SB, 4096, [8, P]), view(SB, 5120, [8, P])
        ZM, MK = view(SB, 6144, [8, P]), view(SB, 7168, [8, P])
        E1, E2, E3 = (view(SB, 6144 + 512 * i, [2, T]) for i in range(3))
        DM, DM1 = view(SB, 4096, [2, T]), view(SB, 4608, [2, T])
        LW, AA, KK = (view(SB, 8192 + 512 * i, [2, T]) for i in range(3))
        XU, US = view(SB, 8704, [256]), view(SB, 8960, [256])
        RK = view(SB, 9216, [2, T])
        AR = view(SB, 9728, [2, 2, 2, P])
        BT, KTL = view(SB, 10752, [2, T]), view(SB, 11264, [2, T])
        SV = view(SB, 11776, [2, T])
        BK = view(SB, 11776, [2, 256])
        VT, GT = view(SB, 12288, [2, 256]), view(SB, 12800, [2, 256])
        S0 = view(SB, 13440, [2, 2, HD])
        LC = view(SB, 13440, [2, T])
        SCL = SM[:, 40:42]
        R_XC, R_SQ = view(SB, 9728, [512]), view(SB, 10240, [512])

        def rwkv_ranks_act(act, l, I):
            act.wait_ge(S("mixed"), l + 1)
            I(nc.scalar.activation(HT[0:64, T_WA, :], HT[0:64, T_WA, :], ACT.Tanh))
            I(nc.scalar.activation(HT[:, T_G1, :], HT[:, T_G1, :], ACT.Sigmoid))
            nc.scalar.activation(HT[0:32, T_MISC, :], HT[0:32, T_MISC, :], ACT.Sigmoid).then_inc(S("rw_rank"), 1)

        def rwkv_ranks_pe(pe, l):
            pe.wait_ge(S("rw_rank"), l + 1)
            for b, r0 in ((6, 0), (7, 64)):
                for c in range(2):
                    pe.matmul(ps[:, b, c * T:(c + 1) * T], par("wa")[r0:r0 + 64, c * P:(c + 1) * P],
                              HT[r0:r0 + 64, T_WA, :], start=True, stop=True)
            if l:
                pe.wait_ge(S("gla_zb"), l + 1)
                for c in range(2):
                    pe.matmul(ps[:, 4, c * T:(c + 1) * T], par("misc")[M_VR:M_VR + 32, c * P:(c + 1) * P],
                              HT[M_VR:M_VR + 32, T_MISC, :], start=True, stop=True)
            for t in range(NT):
                pe.matmul(ps[:, 5, t * T:(t + 1) * T], HT[:, T_G1, t * P:(t + 1) * P], par("g2"), start=True, stop=False)
                m = pe.matmul(ps[:, 5, t * T:(t + 1) * T], HT[0:32, T_MISC, t * P:(t + 1) * P], par("misc")[0:32, :],
                              start=False, stop=True)
            m.then_inc(S("rw_z"), 1)

        def rwkv_gates_act(act, l, I):
            act.wait_ge(S("rw_z"), l + 1)
            for b, to, bias in ((6, LW, "w0"), (7, AA, "a0")) + (((4, SV, "v0"),) if l else ()):
                for c in range(2):
                    ins = nc.scalar.activation(to[:, c, :], ps[:, b, c * T:(c + 1) * T], ACT.Sigmoid,
                                               bias=par(bias)[:, c:c + 1])
                    I(ins)
            nc.scalar.activation(GT, ps[:, 5, :].rearrange("p (t c) -> p t c", t=NT), ACT.Copy).then_inc(S("rw_gates"), 1)

        def rwkv_square_dve(v, l, I, L):
            HK = HT[:, T_K:T_K + 2, :]
            for c in range(2):
                (I if c == 0 else L)(nc.vector.tensor_scalar(KK[:, c, :], HK[:, c, :], par("k_k")[:, c:c + 1], None, ALU.mult))
            nc.vector.tensor_tensor(RK_SQ, KK, KK, ALU.mult).then_inc(S("rw_sq"), 1)

        def rwkv_prepare_dve(v, l, I, L):
            HK, HR, HV = HT[:, T_K:T_K + 2, :], HT[:, T_R:T_R + 2, :], HT[:, T_V:T_V + 2, :]
            v.wait_ge(S("rw_gates"), l + 1)
            if l == 0:
                nc.vector.tensor_copy(VF[:], HV).then_inc(S("rw_v"), 1)
            else:
                L(nc.vector.tensor_tensor(DM, VF[:], HV, ALU.subtract))
                L(nc.vector.tensor_tensor(DM, DM, SV, ALU.mult))
                nc.vector.tensor_tensor(HV, HV, DM, ALU.add).then_inc(S("rw_v"), 1)
                v.wait_ge(S("rw_v"), l + 1)
            for c in range(2):
                (I if c == 0 else L)(nc.vector.tensor_scalar(DM1[:, c, :], AA[:, c, :], 1.0, par("k_a")[:, c:c + 1],
                                                             ALU.subtract, ALU.mult))
            L(nc.vector.scalar_tensor_tensor(out=HK, in0=DM1, scalar=1.0, in1=HK, op0=ALU.add, op1=ALU.mult))
            for c in range(2):
                for j in range(2):
                    L(nc.vector.tensor_tensor_scan(LC[:, c, j * P:(j + 1) * P], cst("ones")[:, 0:P],
                                                   LW[:, c, j * P:(j + 1) * P], 0.0, ALU.mult, ALU.add))
            lc4, dm4 = (a.rearrange("p c (j s) -> p (c j) s", j=2) for a in (LC, DM))
            L(nc.vector.tensor_tensor(dm4, lc4, lc4[:, :, 63:64].broadcast_to([P, 4, P]), ALU.subtract))
            I(nc.vector.tensor_tensor(SCL.unsqueeze(2), DM[:, :, 127:128], LC[:, :, P + 63:P + 64], ALU.add))
            nc.vector.tensor_tensor(DM1, DM, LW, ALU.subtract).then_inc(S("rw_dm"), 1)
            v.wait_ge(S("rw_ss"), l + 1)
            nc.vector.tensor_scalar(RK_SQ.rearrange("p c t -> p (c t)"), ps[:, 6, :], 1e-24, None,
                                    ALU.max).then_inc(S("rw_ssm"), 1)
            v.wait_ge(S("rw_norm"), l + 1)
            L(nc.vector.reciprocal(RK_SQ, RK_SQ))
            L(nc.vector.tensor_tensor(KK, KK, RK_SQ, ALU.mult))
            ar = AR.rearrange("p c j w s -> p (c j) w s")
            f4 = lambda a: a.rearrange("p c (j s) -> p (c j) s", j=2)
            I(nc.vector.scalar_tensor_tensor(out=ar[:, :, 0, :], in0=f4(KK), scalar=-1.0, in1=f4(E3), op0=ALU.mult, op1=ALU.mult))
            I(nc.vector.tensor_tensor(ar[:, :, 1, :], f4(HR), f4(E1), ALU.mult))
            L(nc.vector.tensor_tensor(BT, KK, AA, ALU.mult))
            I(nc.vector.tensor_tensor(BT, BT, E2, ALU.mult))
            I(nc.vector.tensor_tensor(RK, HR, HK, ALU.mult))
            nc.vector.tensor_tensor(KTL, HK, E2, ALU.mult).then_inc(S("rw_ops"), 1)

        RK_SQ = view(SB, 10240, [2, T])

        def rwkv_decay_act(act, l, I):
            act.wait_ge(S("rw_dm"), l + 1)
            I(nc.scalar.activation(E1, DM, ACT.Exp, scale=DECAY))
            I(nc.scalar.activation(E2, DM, ACT.Exp, scale=-DECAY))
            I(nc.scalar.activation(E3, DM1, ACT.Exp, scale=DECAY))
            I(nc.scalar.activation(SCL, SCL, ACT.Exp, scale=DECAY))
            act.wait_ge(S("rw_ssm"), l + 1)
            nc.scalar.activation(RK_SQ, RK_SQ, ACT.Sqrt).then_inc(S("rw_norm"), 1)

        def rwkv_norm_pe(pe, l):
            pe.wait_ge(S("rw_sq"), l + 1)
            pe.wait_ge(S("rw_gates"), l + 1)
            m = pe.matmul(ps[:, 6, :], cst("head_ones"), RK_SQ.rearrange("p c t -> p (c t)"), start=True, stop=True)
            m.then_inc(S("rw_ss"), 1)
            pe.wait_ge(S("rw_v"), l + 1)
            for t in range(NT):
                for c in range(2):
                    m = pe.transpose(ps[:, 7, t * T + c * P:t * T + (c + 1) * P], HT[:, T_V + c, t * P:(t + 1) * P], ident)
            m.then_inc(S("rw_vt_ps"), 1)

        def rwkv_values_act(act, l):
            act.wait_ge(S("rw_vt_ps"), l + 1)
            nc.scalar.activation(VT, ps[:, 7, :].rearrange("p (t c) -> p t c", t=NT), ACT.Copy).then_inc(S("rw_vt"), 1)

        def rwkv_bonus_pe(pe, l):
            pe.wait_ge(S("rw_ops"), l + 1)
            pe.wait_ge(S("rw_vt"), l + 1)
            for i, (tl, c) in enumerate((a, c) for a in (BT, KTL) for c in range(2)):
                m = pe.transpose(ps[:, 7, i * P:(i + 1) * P], tl[:, c, 0:P], ident)
            m.then_inc(S("rw_bk_ps"), 1)
            pe.wait_ge(S("proj_evac"), 15 * (l + 1))
            for t in range(NT):
                for c in range(2):
                    m = pe.matmul(ps[:, 4, 4 * t:4 * t + 4], RK[:, c, t * P:(t + 1) * P], par("r_k")[:, 4 * c:4 * c + 4],
                                  start=c == 0, stop=c == 1)
            m.then_inc(S("rw_bonus"), 1)

        def rwkv_pairs_pe(pe, l, u):
            j, h = divmod(u, 4)
            c, pb = h // 2, HD * (h % 2)
            if u >= 2:
                pe.wait_ge(S("rw_mm"), 8 * l + u - 1)
            rhs = AR[pb:pb + HD, c, j, :, :].rearrange("p w s -> p (w s)")
            for w, tl in enumerate((BT, KTL)):
                m = pe.matmul(ps[:, 5 + u % 2, w * 256:(w + 1) * 256], tl[pb:pb + HD, c, j * P:(j + 1) * P], rhs,
                              start=True, stop=True)
            m.then_inc(S("rw_pairs"), 1)

        def rwkv_bk_act(act, l):
            act.wait_ge(S("rw_bk_ps"), l + 1)
            nc.scalar.activation(BK, ps[:, 7, :].rearrange("p (t c) -> p t c", t=2), ACT.Copy).then_inc(S("rw_bk"), 1)

        def rwkv_init_dve(v, l, I, L):
            v.wait_ge(S("rw_bonus"), l + 1)
            I(nc.vector.memset(S0, 0.0))
            L(nc.vector.tensor_copy(SM[:, 32:40], ps[:, 4, 0:8]))
            v.wait_ge(S("start_loaded"), 32)
            L(nc.vector.tensor_copy(CR, COND[:, 0:KT].unsqueeze(2).broadcast_to([P, KT, 32])))
            idb = ident.unsqueeze(1).broadcast_to([P, 8, P])
            I(nc.vector.tensor_copy(TM, idb))
            nc.vector.tensor_copy(TT, idb).then_inc(S("rw_init"), 1)

        def rwkv_mask_dve(v, l, u):
            v.wait_ge(S("rw_pairs"), 8 * l + u + 1)
            nc.vector.tensor_tensor(MM[:, u, :, :].rearrange("p a s -> p (a s)"), ps[:, 5 + u % 2, :], cst("pairs"),
                                    ALU.mult).then_inc(S("rw_mm"), 1)

        def inverse_level_dve(v, l, s):
            n, us = s // 2, slice(4 * (s % 2), 4 * (s % 2) + 4)
            lev = cst("levels")[:, n * P:(n + 1) * P].unsqueeze(1).broadcast_to([P, 4, P])
            nc.vector.tensor_tensor(MK[:, us, :], MM[:, us, 0, :], lev, ALU.mult).then_inc(S("rw_mk"), 1)

        def inverse_level_pool(pool, l, s):
            n, us = s // 2, slice(4 * (s % 2), 4 * (s % 2) + 4)
            pool.wait_ge(S("rw_mk"), 14 * l + s)
            pool.wait_ge(S("rw_mm"), 8 * (l + 1))
            pool.wait_ge(S("rw_z_ps"), 14 * l + s - 1)
            lev = cst("levels")[:, n * P:(n + 1) * P].unsqueeze(1).broadcast_to([P, 4, P])
            nc.gpsimd.tensor_tensor(MK[:, us, :], MM[:, us, 0, :], lev, ALU.mult).then_inc(S("rw_mk"), 1)

        def inverse_update_dve(v, l, s):
            us = slice(4 * (s % 2), 4 * (s % 2) + 4)
            v.wait_ge(S("rw_dt"), 14 * l + s + 1)
            if s >= 2:
                v.wait_ge(S("rw_tm"), 28 * l + 2 * s - 2)
            for to, b in ((TM, 6), (TT, 7)):
                nc.vector.tensor_tensor(to[:, us, :], to[:, us, :], ps[:, b, :].rearrange("p (u s) -> p u s", u=4),
                                        ALU.add).then_inc(S("rw_tm"), 1)

        def inverse_product_pe(pe, l, s):
            if s == 0:
                pe.wait_ge(S("rw_init"), l + 1)
                pe.wait_ge(S("rw_bk"), l + 1)
            pe.wait_ge(S("rw_mk"), 14 * l + s + 1)
            if s:
                pe.wait_ge(S("rw_zc"), 14 * l + s)
            if s >= 2:
                pe.wait_ge(S("rw_tm"), 28 * l + 2 * (s - 1))
            for i in range(4):
                u = 4 * (s % 2) + i
                m = pe.matmul(ps[:, 5, i * P:(i + 1) * P], MK[:, u, :], TM[:, u, :], start=True, stop=True)
            m.then_inc(S("rw_z_ps"), 1)

        def inverse_update_pe(pe, l, s):
            pe.wait_ge(S("rw_zc"), 14 * l + s + 1)
            if s:
                pe.wait_ge(S("rw_tm"), 28 * l + 2 * s)
            else:
                pe.wait_ge(S("cmp_x"), l + 1)
            for i in range(4):
                u = 4 * (s % 2) + i
                pe.matmul(ps[:, 6, i * P:(i + 1) * P], TT[:, u, :], ZM[:, u, :], start=True, stop=True)
            for i in range(4):
                u = 4 * (s % 2) + i
                m = pe.matmul(ps[:, 7, i * P:(i + 1) * P], ZM[:, u, :], TT[:, u, :], start=True, stop=True)
            m.then_inc(S("rw_dt"), 1)

        def inverse_product_act(act, l, s):
            act.wait_ge(S("rw_z_ps"), 14 * l + s + 1)
            if s >= 2:
                act.wait_ge(S("rw_dt"), 14 * l + s - 1)
            g = 4 * (s % 2)
            nc.scalar.activation(ZM[:, g:g + 4, :].rearrange("p u s -> p (u s)"), ps[:, 5, :], ACT.Copy).then_inc(S("rw_zc"), 1)

        def chunk_removed_pe(pe, l, j):
            if j == 0:
                pe.wait_ge(S("rw_tm"), 28 * (l + 1))
            else:
                pe.wait_ge(S("rw_s"), l + 1)
            for c in range(2):
                if j:
                    pe.matmul(ps[:, 6, c * P:(c + 1) * P], AR[:, c, 1, 0, :], S0[:, c, :, :].rearrange("p h d -> p (h d)"),
                              start=True, stop=False, skip_group_check=True)
                for h in range(2 * c, 2 * c + 2):
                    m = pe.matmul(ps[:, 6, h * HD:(h + 1) * HD], MM[:, 4 * j + h, 2, :], VT[:, j, h * HD:(h + 1) * HD],
                                  start=j == 0, stop=True, skip_group_check=True)
            m.then_inc(S("rw_x_ps"), 1)

        def chunk_solve_pe(pe, l, j):
            pe.wait_ge(S("rw_x"), 2 * l + j + 1)
            for h in range(4):
                m = pe.matmul(ps[:, 6, 256 + h * HD:256 + (h + 1) * HD], TT[:, 4 * j + h, :], XU[:, h * HD:(h + 1) * HD],
                              start=True, stop=True)
            m.then_inc(S("rw_u_ps"), 1)

        def chunk_out_pe(pe, l, j):
            pe.wait_ge(S("rw_u"), 2 * l + j + 1)
            if j == 0:
                for h in range(4):
                    c, pb = h // 2, HD * (h % 2)
                    pe.matmul(ps[pb:pb + HD, 5, c * HD:(c + 1) * HD], BK[:, 0, h * HD:(h + 1) * HD],
                              US[:, h * HD:(h + 1) * HD], start=True, stop=False)
                    m = pe.matmul(ps[pb:pb + HD, 5, c * HD:(c + 1) * HD], BK[:, 1, h * HD:(h + 1) * HD],
                                  VT[:, 0, h * HD:(h + 1) * HD], start=False, stop=True)
                m.then_inc(S("rw_s_ps"), 1)
            for c in range(2):
                if j:
                    pe.matmul(ps[:, 7, 256 + c * P:256 + (c + 1) * P], AR[:, c, 1, 1, :],
                              S0[:, c, :, :].rearrange("p h d -> p (h d)"), start=True, stop=False, skip_group_check=True)
                for h in range(2 * c, 2 * c + 2):
                    to = ps[:, 7, (4 * j + h) * HD:(4 * j + h + 1) * HD]
                    pe.matmul(to, MM[:, 4 * j + h, 1, :], US[:, h * HD:(h + 1) * HD], start=j == 0, stop=False,
                              skip_group_check=True)
                    m = pe.matmul(to, MM[:, 4 * j + h, 3, :], VT[:, j, h * HD:(h + 1) * HD], start=False, stop=True,
                                  skip_group_check=True)
            m.then_inc(S("rw_y"), 1)

        def chunk_removed_dve(v, l, j):
            v.wait_ge(S("rw_x_ps"), 2 * l + j + 1)
            if j:
                v.wait_ge(S("rw_x"), 2 * l + j)
            nc.vector.tensor_copy(XU, ps[:, 6, 0:256]).then_inc(S("rw_x"), 1)

        def chunk_solve_dve(v, l, j):
            v.wait_ge(S("rw_u_ps"), 2 * l + j + 1)
            if j:
                v.wait_ge(S("rw_y"), 2 * l + 1)
            nc.vector.tensor_copy(US, ps[:, 6, 256:512]).then_inc(S("rw_u"), 1)

        def chunk_state_dve(v, l, I):
            v.wait_ge(S("rw_s_ps"), l + 1)
            for h in range(4):
                c, rows = h // 2, slice(HD * (h % 2), HD * (h % 2) + HD)
                ins = nc.vector.tensor_scalar(S0[rows, c, h % 2, :], ps[rows, 5, c * HD:(c + 1) * HD],
                                              SCL[rows, c:c + 1], None, ALU.mult)
                if h < 3:
                    I(ins)
            ins.then_inc(S("rw_s"), 1)

        def rwkv_norm_dve(v, l, I, L):
            v.wait_ge(S("rw_y"), 2 * (l + 1))
            head_norm_dve(v, I, L, ps[:, 7, :].rearrange("p (a b) -> p a b", b=HD), RWKV_EPS, 2, 2 * l + 1, R_XC, R_SQ)
            bonus = SM[:, 32:40].unsqueeze(2).broadcast_to([P, 8, HD])
            L(nc.vector.tensor_tensor(R_SQ.rearrange("p (a b) -> p a b", b=HD),
                                      VT.rearrange("p t (h b) -> p (t h) b", b=HD), bonus, ALU.mult))
            L(nc.vector.tensor_tensor(R_XC, R_XC, R_SQ, ALU.add))
            nc.vector.tensor_tensor(R_XC, R_XC, GT.rearrange("p t c -> p (t c)"), ALU.mult).then_inc(S("head_out"), 1)

        flat_xt = XT[:].rearrange("p k t -> p (k t)")
        N_FL = [view(flat_xt, 1024 + 512 * i, [16, 32]) for i in range(2)]
        N_GE = [view(SB, at, [256]) for at in (8192, 8448, 9216)]
        N_HID, N_KC, N_VC = view(SB, 13952, [2, 64]), view(SB, 14080, [15]), view(SB, 14095, [2, HD])
        N_GT = view(SB, 14223, [NT, 24])
        N_P, N_PT = view(SA, 2048, [2, 4, T]), view(SA, 0, [4, 512])
        MX, RS, RG = (view(SM, 48 + 8 * i, [2, 4]) for i in range(3))

        ROPE_PIECES = 4

        def rope_tiles(p):
            return T_KC + 2 * p, min(2, 7 - 2 * p)

        def rope_pe(pe, l, p):
            pe.wait_ge(S("proj_evac"), 15 * (l + 1))
            pe.wait_ge(S("rw_bk"), l + 1)
            if p:
                pe.wait_ge(S("rope"), ROPE_PIECES * l + p)
            first, n = rope_tiles(p)
            for j in range(n):
                m = pe.matmul(ps[:, 7, j * T:(j + 1) * T], cst("rot"), HT[:, first + j, :], start=True, stop=True)
            m.then_inc(S("rope_ps"), 1)

        def rope_dve(v, l, p, I, L):
            first, n = rope_tiles(p)
            v.wait_ge(S("rope_ps"), ROPE_PIECES * l + p + 1)
            x = HT[:, first:first + n, :]
            cos, sin = (cst(a).unsqueeze(1).broadcast_to([P, n, T]) for a in ("cos", "sin"))
            turned = ps[:, 7, 0:n * T].rearrange("p (j t) -> p j t", t=T)
            I(nc.vector.tensor_tensor(turned, turned, sin, ALU.mult))
            L(nc.vector.tensor_tensor(x, x, cos, ALU.mult))
            nc.vector.tensor_tensor(x, x, turned, ALU.add).then_inc(S("rope"), 1)

        def cmp_pool(pool, l):
            pool.wait_ge(S("rope"), ROPE_PIECES * l + 1)
            pool.wait_ge(S("proj_ready"), 15 * (l + 1))
            pool.wait_ge(S("par_loaded"), 32 * (l + 1))
            for i in range(2):
                nc.gpsimd.memset(N_FL[i][:, :, 30:32], 0.0).then_inc(S("cmp_blocks"), 1)
                pool.wait_ge(S("cmp_blocks"), 18 * l + i + 1)
            for i, (tile, emb) in enumerate(((T_KC, "pos_k"), (T_VC, "pos_v"))):
                for g in range(2):
                    rows = slice(HD * g, HD * (g + 1))
                    src = HT[rows, tile, :].rearrange("p (c j w) -> p w j c", j=8, w=2)
                    pos = par(emb)[rows, :].rearrange("p (j w) -> p w j", w=2)
                    for w in range(2):
                        for half in range(2):
                            ins = nc.gpsimd.tensor_tensor(
                                N_FL[i][HD * w:HD * (w + 1), 8 * half:8 * half + 8, 15 * g:15 * g + 15],
                                src[:, w, :, half:half + 15],
                                pos[:, w, 8 * half:8 * half + 8].unsqueeze(2).broadcast_to([HD, 8, 15]), ALU.add)
                            ins.then_inc(S("cmp_blocks"), 1)

        def cmp_hidden_pe(pe, l):
            pe.wait_ge(S("rope"), ROPE_PIECES * (l + 1))
            pe.wait_ge(S("cmp_blocks"), 18 * (l + 1))
            w = []
            for i in range(2):
                need_slot(pe, l * LAYER_SLOTS + S_CMP + i)
                w.append(slot(l * LAYER_SLOTS + S_CMP + i).rearrange("p (j n) -> p j n", j=16))
            for j in range(16):
                for i in range(2):
                    m = pe.matmul(ps[32 * i:32 * (i + 1), 7, 0:256], N_FL[i][:, j, :], w[i][:, j, :], start=j == 0, stop=j == 15)
            m.then_inc(S("cmp_hidden"), 1)

        def cmp_turn_pe(pe, l):
            pe.wait_ge(S("gelu"), l + 1)
            pe.wait_ge(S("gla_st"), 3 * (l + 1))
            for i in range(2):
                m = pe.transpose(ps[:, 2, i * 64:(i + 1) * 64], N_GE[0][0:64, i * P:(i + 1) * P], ident[0:64, 0:64])
            m.then_inc(S("cmp_hid_ps"), 1)

        def cmp_out_pe(pe, l):
            pe.wait_ge(S("cmp_hid"), l + 1)
            wk, wv = (par(n).rearrange("p (a d) -> p a d", a=2) for n in ("wk2", "wv2"))
            for g in range(2):
                for a in range(2):
                    pe.matmul(ps[HD * g:HD * (g + 1), 2, 128:143], wk[:, a, :], N_HID[:, a, 15 * g:15 * g + 15],
                              start=a == 0, stop=a == 1)
            for g in range(2):
                for a in range(2):
                    m = pe.matmul(ps[0:15, 2, 256 + HD * g:256 + HD * (g + 1)], N_HID[:, a, 32 + 15 * g:32 + 15 * g + 15],
                                  wv[:, a, :], start=a == 0, stop=a == 1)
            m.then_inc(S("cmp_kv_ps"), 1)

        def gelu_in_dve(v, L, x, y):
            L(nc.vector.tensor_tensor(y, x, x, ALU.mult))
            L(nc.vector.tensor_scalar(y, y, GELU_K, 1.0, ALU.mult, ALU.add))
            nc.vector.tensor_tensor(y, y, x, ALU.mult).then_inc(S("tanh_in"), 1)

        def gelu_out_dve(v, L, n, x, t, to):
            v.wait_ge(S("tanh"), n + 1)
            L(nc.vector.scalar_tensor_tensor(out=t, in0=t, scalar=1.0, in1=x, op0=ALU.add, op1=ALU.mult))
            nc.vector.tensor_scalar(to, t, 0.5, None, ALU.mult).then_inc(S("gelu"), 1)

        def cmp_hidden_dve(v, l, L):
            v.wait_ge(S("cmp_hidden"), l + 1)
            x, y, t = (a[0:64, :] for a in N_GE)
            nc.vector.tensor_copy(x, ps[0:64, 7, 0:256]).then_inc(S("cmp_x"), 1)
            v.wait_ge(S("cmp_x"), l + 1)
            gelu_in_dve(v, L, x, y)
            gelu_out_dve(v, L, l, x, t, x)

        def cmp_turn_dve(v, l):
            v.wait_ge(S("cmp_hid_ps"), l + 1)
            nc.vector.tensor_copy(N_HID.rearrange("p a b -> p (a b)"), ps[:, 2, 0:128]).then_inc(S("cmp_hid"), 1)

        def cmp_out_dve(v, l, I):
            v.wait_ge(S("cmp_kv_ps"), l + 1)
            I(nc.vector.tensor_copy(N_KC, ps[:, 2, 128:143]))
            nc.vector.tensor_copy(N_VC[0:15, :, :], ps[0:15, 2, 256:384].rearrange("p (g d) -> p g d", g=2)).then_inc(S("cmp_kv"), 1)

        def cmp_act(act, l):
            act.wait_ge(S("tanh_in"), l + 1)
            nc.scalar.activation(N_GE[2][0:64, :], N_GE[1][0:64, :], ACT.Tanh, scale=GELU_C).then_inc(S("tanh"), 1)

        def nsa_gate_act(act, l):
            nc.scalar.activation(N_GT, NV[:, :, 256:280], ACT.Sigmoid).then_inc(S("nsa_gate"), 1)

        FIRST_UNITS = [(kind, t, g) for kind, t in ((1, 1), (2, 1), (1, 0), (2, 0), (0, 0), (0, 1)) for g in range(2)]
        UNITS = FIRST_UNITS * DEPTH + [(3, t, g) for t in (1, 0) for g in range(2)]
        NU = len(FIRST_UNITS)

        def key_tiles(n):
            kind, t, g = UNITS[n]
            return 1 if kind == 0 else t + 1

        def tiles_before(n):
            return sum(key_tiles(m) for m in range(n))

        def width(kind, t):
            return 15 if kind == 0 else P * (t + 1)

        def attention_keys(kind, g):
            rows = slice(HD * g, HD * (g + 1))
            if kind == 0:
                return N_KC[rows, :]
            return HT[rows, {1: T_KS, 2: T_KW, 3: 12}[kind], :]

        def attention_values(kind, g, k):
            if kind == 0:
                return N_VC[0:15, g, :]
            if kind == 3:
                return V2[:, k, HD * g:HD * (g + 1)]
            return NV[:, k, (kind - 1) * P + HD * g:(kind - 1) * P + HD * (g + 1)]

        def attention_scores_pe(pe, n):
            kind, t, g = UNITS[n]
            w, q0 = width(kind, t), 8 if kind == 3 else T_Q
            pe.wait_ge(S("att_raw"), n)
            rows = slice(HD * g, HD * (g + 1))
            for j in range(4):
                m = pe.matmul(bank(0, 2)[:, j * w:(j + 1) * w], HT[rows, q0 + j, t * P:(t + 1) * P],
                              attention_keys(kind, g)[:, 0:w], start=True, stop=True)
            m.then_inc(S("att_scores"), 1)

        def turn_bank(n, k):
            return 2 + k

        def attention_turn_pe(pe, n):
            kind, t, g = UNITS[n]
            pe.wait_ge(S("att_p"), n + 1)
            kw = min(width(kind, t), P)
            for k in range(key_tiles(n)):
                x = tiles_before(n) + k
                free = x if key_tiles(n) == 1 else x - 1
                if free > 0:
                    pe.wait_ge(S("att_pt"), free)
                for j in range(4):
                    m = pe.transpose(ps[0:kw, turn_bank(n, k), j * P:(j + 1) * P], N_P[:, n % 2, j, k * P:k * P + kw], ident)
                m.then_inc(S("att_t_ps"), 1)

        def attention_out_pe(pe, n):
            kind, t, g = UNITS[n]
            kw = min(width(kind, t), P)
            for k in range(key_tiles(n)):
                x = tiles_before(n) + k
                pe.wait_ge(S("att_pt"), x + 1)
                first = k == 0 and kind in (1, 3)
                for j in range(4):
                    m = pe.matmul(ps[HD * g:HD * (g + 1), 3 + t, j * P:(j + 1) * P], attention_values(kind, g, k),
                                  N_PT[0:kw, x % 4, j * P:(j + 1) * P], start=first and j == 0, stop=True, skip_group_check=True)
                m.then_inc(S("att_pv"), 1)

        def attention_exp_act(act, n):
            kind, t, g = UNITS[n]
            w = width(kind, t)
            act.wait_ge(S("att_max"), n + 1)
            if kind == 3:
                nc.scalar.activation(RG[:, n % 2, :], RG[:, n % 2, :], ACT.Exp).then_inc(S("att_sink"), 1)
            for j in range(4):
                nc.scalar.activation(N_P[:, n % 2, j, 0:w], N_P[:, n % 2, j, 0:w], ACT.Exp, scale=HD ** -0.5,
                                     bias=MX[:, n % 2, j:j + 1], accum_out=RS[:, n % 2, j:j + 1]).then_inc(S("att_exp"), 1)

        def attention_out_act(act, n):
            kind, t, g = UNITS[n]
            kw = min(width(kind, t), P)
            for k in range(key_tiles(n)):
                x = tiles_before(n) + k
                act.wait_ge(S("att_t_ps"), x + 1)
                if x >= 4:
                    act.wait_ge(S("att_pv"), x - 3)
                nc.scalar.activation(N_PT[0:kw, x % 4, :], ps[0:kw, turn_bank(n, k), :], ACT.Copy).then_inc(S("att_pt"), 1)

        def attention_scores_dve(v, n, I, L):
            kind, t, g = UNITS[n]
            w, to, mx = width(kind, t), N_P[:, n % 2, :, :], MX[:, n % 2, :]
            v.wait_ge(S("att_scores"), n + 1)
            if n >= 2:
                v.wait_ge(S("att_t_ps"), tiles_before(n - 1))
            raw = bank(0, 2)[:, 0:4 * w].rearrange("p (j k) -> p j k", j=4)
            if kind == 0:
                mask = cst("cmp_add")[:, 15 * t:15 * t + 15].unsqueeze(1).broadcast_to([P, 4, 15])
                nc.vector.tensor_tensor(to[:, :, 0:15], raw, mask, ALU.add).then_inc(S("att_raw"), 1)
            else:
                if t and kind == 3:
                    prev = cst("prev_add").unsqueeze(1).broadcast_to([P, 4, P])
                    I(nc.vector.tensor_tensor(to[:, :, 0:P], raw[:, :, 0:P], prev, ALU.add))
                elif t:
                    I(nc.vector.tensor_copy(to[:, :, 0:P], raw[:, :, 0:P]))
                diag = cst("diag_add").unsqueeze(1).broadcast_to([P, 4, P])
                nc.vector.tensor_tensor(to[:, :, w - P:w], raw[:, :, w - P:w], diag, ALU.add).then_inc(S("att_raw"), 1)
            v.wait_ge(S("att_raw"), n + 1)
            L(nc.vector.tensor_reduce(mx, to[:, :, 0:w], AX.X, ALU.max))
            if kind == 3:
                sink = SNK[:, 4 * g:4 * g + 4]
                L(nc.vector.tensor_scalar(mx, mx, HD ** -0.5, None, ALU.mult))
                L(nc.vector.tensor_tensor(mx, mx, sink, ALU.max))
                I(nc.vector.tensor_tensor(RG[:, n % 2, :], sink, mx, ALU.subtract))
                nc.vector.tensor_scalar(mx, mx, -1.0, None, ALU.mult).then_inc(S("att_max"), 1)
            else:
                nc.vector.tensor_scalar(mx, mx, -(HD ** -0.5), None, ALU.mult).then_inc(S("att_max"), 1)

        def attention_scale_dve(v, n, L):
            kind, t, g = UNITS[n]
            w, rs, rg = width(kind, t), RS[:, n % 2, :], RG[:, n % 2, :]
            v.wait_ge(S("att_exp"), 4 * (n + 1))
            if kind == 3:
                v.wait_ge(S("att_sink"), n - NU * DEPTH + 1)
                L(nc.vector.tensor_tensor(rs, rs, rg, ALU.add))
            L(nc.vector.reciprocal(rg, rs))
            if kind != 3:
                gate = N_GT[:, t, :].rearrange("p (i b) -> p i b", b=3)[:, 4 * g:4 * g + 4, kind]
                L(nc.vector.tensor_tensor(rg, rg, gate, ALU.mult))
            if kind == 0:
                L(nc.vector.tensor_scalar(rg, rg, cst("cmp_any")[:, t:t + 1], None, ALU.mult))
            to = N_P[:, n % 2, :, 0:w]
            nc.vector.tensor_tensor(to, to, rg.unsqueeze(2).broadcast_to([P, 4, w]), ALU.mult).then_inc(S("att_p"), 1)

        def attention_merge_dve(v, n, I):
            v.wait_ge(S("att_pv"), tiles_before(n))
            for t in range(NT):
                ins = nc.vector.tensor_copy(OT[:, 4 if n <= NU * DEPTH else 0:8 if n <= NU * DEPTH else 4, t * P:(t + 1) * P],
                                            ps[:, 3 + t, :].rearrange("p (j q) -> p j q", j=4))
                if t == 0:
                    I(ins)
            ins.then_inc(S("nsa_out"), 1)

        def mix_part_pe(pe, l, t, c, ks, start, stop):
            need_slot(pe, l * LAYER_SLOTS + S_WO + c)
            w = slot(l * LAYER_SLOTS + S_WO + c).rearrange("p (k n) -> p k n", k=KT)
            for k in ks:
                m = pe.matmul(ps[:, 2 * t + c, :], OT[:, k, t * P:(t + 1) * P], w[:, k, :],
                              start=start and k == ks[0], stop=stop and k == ks[-1], skip_group_check=True)
            return m

        def mix_early_pe(pe, l, t, c):
            pe.wait_ge(S("nsa_out"), l + 1)
            mix_part_pe(pe, l, t, c, (0, 1, 4, 5, 6, 7), True, False)

        def mix_late_pe(pe, l):
            pe.wait_ge(S("rw_out"), l + 1)
            for t in range(NT):
                for c in range(2):
                    m = mix_part_pe(pe, l, t, c, (2, 3), False, True)
                m.then_inc(S("mix_ready"), 1)

        def ln_stats(t):
            return SM[:, 80 + t:81 + t], SM[:, 84 + t:85 + t], SM[:, 88 + t:89 + t]

        def ln_sum_dve(v, n, t, b0, ready, L):
            s, q, r = ln_stats(t)
            v.wait_ge(S(ready[0]), ready[1] + t)
            L(nc.vector.scalar_tensor_tensor(out=X[:, t, :], in0=X[:, t, :], scalar=ALPHA, in1=bank(b0 + 2 * t, 2),
                                             op0=ALU.mult, op1=ALU.add, accum_out=s))
            nc.vector.tensor_scalar(s, s, -1.0 / D, None, ALU.mult).then_inc(S("ln_mean"), 1)

        def ln_var_dve(v, n, t):
            s, q, r = ln_stats(t)
            v.wait_ge(S("ln_sq"), 2 * n + t + 1)
            nc.vector.tensor_scalar(q, q, 1.0 / D, LN_EPS, ALU.mult, ALU.add).then_inc(S("ln_var"), 1)

        def ln_scale_dve(v, n, t, L):
            s, q, r = ln_stats(t)
            v.wait_ge(S("ln_std"), 2 * n + t + 1)
            L(nc.vector.reciprocal(r, r))
            L(nc.vector.tensor_scalar(X[:, t, :], X[:, t, :], s, r, ALU.add, ALU.mult))

        def layer_norm_dve(v, n, b0, ready, L):
            ln_sum_dve(v, n, 0, b0, ready, L)
            ln_var_dve(v, n, 0)
            ln_scale_dve(v, n, 0, L)
            ln_sum_dve(v, n, 1, b0, ready, L)
            v.wait_ge(S("ln_loaded"), 32 * (n + 1))
            L(nc.vector.tensor_tensor(X[:, 0, :], X[:, 0, :], LNW, ALU.mult))
            ln_var_dve(v, n, 1)
            nc.vector.tensor_tensor(X[:, 0, :], X[:, 0, :], LNB, ALU.add).then_inc(S("x_tile"), 1)
            ln_scale_dve(v, n, 1, L)
            L(nc.vector.tensor_tensor(X[:, 1, :], X[:, 1, :], LNW, ALU.mult))
            nc.vector.tensor_tensor(X[:, 1, :], X[:, 1, :], LNB, ALU.add).then_inc(S("x_ready"), 1)
            v.wait_ge(S("x_tile"), n + 1)
            v.wait_ge(S("x_ready"), n + 1)

        def layer_norm_act(act, n):
            for t in range(NT):
                s, q, r = SM[:, 80 + t:81 + t], SM[:, 84 + t:85 + t], SM[:, 88 + t:89 + t]
                act.wait_ge(S("ln_mean"), 2 * n + t + 1)
                nc.scalar.activation(SQ, X[:, t, :], ACT.Square, bias=s, accum_out=q).then_inc(S("ln_sq"), 1)
                act.wait_ge(S("ln_var"), 2 * n + t + 1)
                nc.scalar.activation(r, q, ACT.Sqrt).then_inc(S("ln_std"), 1)

        SG = [view(SA, 512 * i, [512]) for i in range(2)]

        def ffn_pe(pe, l):
            pe.wait_ge(S("xt_ready"), 4 * (2 * l + 2))
            for f in range(11):
                i = l * LAYER_SLOTS + S_GU + f
                need_slot(pe, i)
                if f >= 2:
                    pe.wait_ge(S("ffn_evac"), 11 * l + f - 1)
                w = slot(i).rearrange("p (k a n) -> p k a n", k=KT, a=2)
                for a in range(2):
                    for j in range(2):
                        for k in range(KT):
                            m = pe.matmul(ps[:, 2 * a + f % 2, j * T:(j + 1) * T], w[:, k, a, j * P:(j + 1) * P], XT[:, k, :],
                                          start=k == 0, stop=k == KT - 1)
                m.then_inc(S("ffn_ready"), 1)
                if l == DEPTH - 1 and 2 <= f < 8:
                    spread_pe(pe, f - 2)
            if l == DEPTH - 1:
                pe.wait_ge(S("mod_rows"), 6)
            for s in range(6):
                i = l * LAYER_SLOTS + S_DN + s
                need_slot(pe, i)
                pe.wait_ge(S("ffn_evac"), 11 * l + min(2 * s + 2, 11))
                w = slot(i).rearrange("p (k n) -> p k n", k=4)
                ks = range(4 * s, min(4 * s + 4, NF))
                for k, t in ((k, t) for t in range(NT) for k in ks):
                    for c in range(2):
                        m = pe.matmul(ps[:, 4 + 2 * t + c, :], HT[:, k, t * P:(t + 1) * P],
                                      w[:, k - 4 * s, c * 512:(c + 1) * 512], start=k == 0, stop=k == NF - 1)
                    if k == ks[-1] and (s == 5 or t == NT - 1):
                        m.then_inc(S("down_ready"), 1)

        def ffn_act(act, l):
            for f in range(11):
                act.wait_ge(S("ffn_ready"), 11 * l + f + 1)
                if f >= 2:
                    act.wait_ge(S("ffn_evac"), 11 * l + f - 1)
                nc.scalar.activation(SG[f % 2], ps[:, f % 2, :], ACT.Silu).then_inc(S("ffn_silu"), 1)
                if l == DEPTH - 1 and 2 <= f < 8:
                    spread_act(act, f - 2)

        def ffn_dve(v, l, L):
            for f in range(11):
                v.wait_ge(S("ffn_silu"), 11 * l + f + 1)
                nc.vector.tensor_tensor(HT[:, 2 * f:2 * f + 2, :].rearrange("p a t -> p (a t)"), SG[f % 2], ps[:, 2 + f % 2, :],
                                        ALU.mult).then_inc(S("ffn_evac"), 1)
                if l == DEPTH - 1 and f < 6:
                    spread_dve(v, f)
                if l == DEPTH - 1 and f > 8:
                    modulation_gain_dve(v, f - 9, L)

        MOD = view(SB, 4096, [6, D])
        HF = view(SA, 2048, [NT, D])
        V2 = NV[:, :, 0:P]
        XC2, RA, RI = (view(SB, at, [4, T]) for at in (10240, 11264, 12288))
        AE, GE = HT[:, 13:17, :], HT[:, 17:21, :]
        SQM = view(SB, 10240, [8, T])
        YT = view(SB, 12288, [D])
        BR, SNK = SM[:, 128:160], SM[:, 160:168]
        BD = view(SB, 2 * D, [D])

        def second_sp(sp):
            for done in ("gla_out", "rw_out", "nsa_out"):
                sp.wait_ge(S(done), DEPTH)
            sp.dma_start(PAR[:, 0:SECOND_COLS], dram["second"]).then_inc(S("par2_loaded"), 16)
            sp.dma_start(SM[:, 128:168], dram["small"].broadcast_to([P, 40])).then_inc(S("par2_loaded"), 16)
            for i in range(S_IN2, S_MOE):
                stream(sp, i)
            sp.wait_ge(S("h_ready"), 1)
            sp.dma_start(LNW, dram["gains"][2:3, :].broadcast_to([P, D])).then_inc(S("gain_loaded"), 16)

        CR = view(SB, 9472, [KT, 32])
        PART = view(XT[:].rearrange("p k t -> p (k t)"), 512, [512])
        MODC = COND[:, KT:]
        DG = [view(SA, 1024 * (m + 1), [KT, P]) for m in range(2)]

        def modulation_pe(pe, l, i):
            n = ADA * l + i
            if i < ADA:
                need_slot(pe, l * LAYER_SLOTS + S_ADA + i)
                w = slot(l * LAYER_SLOTS + S_ADA + i).rearrange("p (k n) -> p k n", k=KT)
            if i:
                pe.wait_ge(S("mod_part"), n)
                for b in range(4):
                    m = pe.matmul(ps[:, 0, 384 + 4 * i - 4 + b:385 + 4 * i - 4 + b], PART[:, b * P:(b + 1) * P], cst("fold"),
                                  start=True, stop=True)
                m.then_inc(S("mod_sum"), 1)
            else:
                pe.wait_ge(S("rw_init"), l + 1)
            if i < ADA:
                for k in range(KT):
                    m = pe.matmul(ps[32 * (k % 4):32 * (k % 4) + 32, 4, :], CR[:, k, :], w[:, k, :], start=k < 4, stop=k >= 4)
                m.then_inc(S("mod_ready"), 1)

        def modulation_act(act, l, i):
            n = ADA * l + i
            act.wait_ge(S("mod_ready"), n + 1)
            if n:
                act.wait_ge(S("mod_sum"), n)
            nc.scalar.activation(PART, ps[:, 4, :], ACT.Copy).then_inc(S("mod_part"), 1)

        def modulation_dve(v, l):
            v.wait_ge(S("mod_sum"), ADA * (l + 1))
            v.wait_ge(S("start_loaded"), 32)
            to = MODC[:, 4 * ADA * l:4 * ADA * (l + 1)]
            nc.vector.tensor_tensor(to, to, ps[:, 0, 384:384 + 4 * ADA], ALU.add).then_inc(S("mod"), 1)

        def spread_dve(v, m):
            v.wait_ge(S("mod"), DEPTH)
            if m >= 2:
                v.wait_ge(S("mod_ps"), m - 1)
            nc.vector.tensor_tensor(DG[m % 2], ident.unsqueeze(1).broadcast_to([P, KT, P]),
                                    MODC[:, KT * m:KT * (m + 1)].unsqueeze(2).broadcast_to([P, KT, P]),
                                    ALU.mult).then_inc(S("mod_diag"), 1)

        def spread_pe(pe, m):
            pe.wait_ge(S("mod_diag"), m + 1)
            if m >= 2:
                pe.wait_ge(S("mod_rows"), m - 1)
            for c in range(2):
                x = pe.matmul(ps[:, 4 + 2 * (m % 2) + c, :], cst("ones")[:, 0:P],
                              DG[m % 2][:, 4 * c:4 * c + 4, :].rearrange("p k n -> p (k n)"), start=True, stop=True)
            x.then_inc(S("mod_ps"), 1)

        def spread_act(act, m):
            act.wait_ge(S("mod_ps"), m + 1)
            nc.scalar.activation(MOD[:, m, :], bank(4 + 2 * (m % 2), 2), ACT.Copy).then_inc(S("mod_rows"), 1)

        def rms_act(act, n, t, ready):
            act.wait_ge(S(ready[0]), ready[1])
            if 2 * n + t:
                act.wait_ge(S("rms_sq"), 2 * n + t)
            nc.scalar.activation(SQ2, X[:, t, :], ACT.Square, accum_out=SM[:, 92 + t:93 + t]).then_inc(S("rms_sq"), 1)
            act.wait_ge(S("rms_var"), 2 * n + t + 1)
            nc.scalar.activation(SM[:, 96 + t:97 + t], SM[:, 94 + t:95 + t], ACT.Sqrt).then_inc(S("rms_std"), 1)

        SQ2 = view(SB, 3 * D, [D])

        def rms_dve(v, n, t, L):
            v.wait_ge(S("rms_sq"), 2 * n + t + 1)
            nc.vector.tensor_scalar(SM[:, 94 + t:95 + t], SM[:, 92 + t:93 + t], 1.0 / D, RMS_EPS, ALU.mult,
                                    ALU.add).then_inc(S("rms_var"), 1)
            v.wait_ge(S("rms_std"), 2 * n + t + 1)
            L(nc.vector.reciprocal(SM[:, 98 + t:99 + t], SM[:, 96 + t:97 + t]))

        GAINS = view(SB, 10240, [2, D])

        def modulation_gain_dve(v, n, L):
            v.wait_ge(S("gain_loaded"), 32)
            v.wait_ge(S("mod_rows"), 3 * n + 2)
            scale = MOD[:, 3 * n + 1, :]
            L(nc.vector.scalar_tensor_tensor(out=scale, in0=scale, scalar=1.0, in1=GAINS[:, n, :], op0=ALU.add, op1=ALU.mult))

        def modulated_dve(v, n, t, L):
            v.wait_ge(S("mod_rows"), 6)
            rms_dve(v, n, t, L)
            L(nc.vector.scalar_tensor_tensor(out=HF[:, t, :], in0=X[:, t, :], scalar=SM[:, 98 + t:99 + t], in1=MOD[:, 3 * n + 1, :],
                                             op0=ALU.mult, op1=ALU.mult))
            nc.vector.tensor_tensor(HF[:, t, :], HF[:, t, :], MOD[:, 3 * n, :], ALU.add).then_inc(S("h_tile" if t == 0 else "h_ready"), 1)

        def project2_pe(pe, slots):
            pe.wait_ge(S("xt_ready"), 4 * 5)
            for s in slots:
                need_slot(pe, S_IN2 + s)
                w = slot(S_IN2 + s).rearrange("p (k n) -> p k n", k=KT)
                for q in range(2):
                    g = 2 * s + q
                    if g >= 4:
                        pe.wait_ge(S("proj2_evac"), g - 3)
                    for j in range(2):
                        for k in range(KT):
                            if g < 6 or (g == 6 and j == 0):
                                m = pe.matmul(ps[:, g % 4, j * T:(j + 1) * T], w[:, k, (2 * q + j) * P:(2 * q + j + 1) * P],
                                              XT[:, k, :], start=k == 0, stop=k == KT - 1)
                            elif g == 7:
                                m = pe.matmul(ps[:, g % 4, j * P:(j + 1) * P], XT[:, k, j * P:(j + 1) * P], w[:, k, P:2 * P],
                                              start=k == 0, stop=k == KT - 1)
                    m.then_inc(S("proj2_ready"), 1)

        def project2_act(act, groups):
            for g in groups:
                act.wait_ge(S("proj2_ready"), g + 1)
                n = 512 if g < 6 else T
                if g < 7:
                    to = HT[:, 2 * g:2 * g + n // T, :].rearrange("p a t -> p (a t)")
                    src = ps[:, g % 4, 0:n]
                else:
                    to, src = V2, ps[:, g % 4, 0:T].rearrange("p (t d) -> p t d", t=NT)
                nc.scalar.activation(to, src, ACT.Copy).then_inc(S("proj2_evac"), 1)

        LSL = SM[:, 100:104]

        def lam_act(act, L):
            lam = par2("lam")
            act.wait_ge(S("par2_loaded"), 32)
            L(nc.scalar.activation(SM[:, 104:108], lam, ACT.Abs))
            L(nc.scalar.activation(SM[:, 104:108], SM[:, 104:108], ACT.Exp, scale=-1.0))
            nc.scalar.activation(SM[:, 104:108], SM[:, 104:108], ACT.Ln, bias=cst("ones")[:, 0:1]).then_inc(S("lru_act"), 1)

        def rg_act(act):
            act.wait_ge(S("rg"), 1)
            for a, (to, bias) in enumerate(((RA, "b_a"), (RI, "b_x"))):
                for c in range(4):
                    nc.scalar.activation(to[:, c, :], ps[:, 4 + 2 * a + c // 2, (c % 2) * T:(c % 2 + 1) * T], ACT.Sigmoid,
                                         bias=par2(bias)[:, c:c + 1]).then_inc(S("rg_gates"), 1)

        def lru_decay_act(act, I):
            act.wait_ge(S("lru_dve"), 2)
            I(nc.scalar.activation(AE, RA, ACT.Exp))
            nc.scalar.activation(RA, RA, ACT.Tanh, scale=-1.0).then_inc(S("lru_act"), 1)

        def lru_gate_act(act):
            act.wait_ge(S("tanh_in"), DEPTH + 1)
            nc.scalar.activation(GE, GE, ACT.Tanh, scale=GELU_C).then_inc(S("tanh"), 1)

        def lru_end_act(act):
            act.wait_ge(S("lru_dve"), 3)
            nc.scalar.activation(RA, RA, ACT.Sqrt).then_inc(S("lru_act"), 1)

        def rg_pe(pe):
            pe.wait_ge(S("lru_dve"), 1)
            for a, name in enumerate(("rg_a", "rg_x")):
                for c in range(4):
                    m = pe.matmul(ps[:, 4 + 2 * a + c // 2, (c % 2) * T:(c % 2 + 1) * T], par2(name)[:, c * P:(c + 1) * P],
                                  XC2[:, c, :], start=True, stop=True)
            m.then_inc(S("rg"), 1)

        def lru_dve(v, I, L):
            v.wait_ge(S("proj2_evac"), 2)
            xr, xg = HT[:, 0:4, :], HT[:, 4:8, :]
            cw = par2("conv_w")
            for c in range(4):
                (L if c == 3 else I)(nc.vector.tensor_scalar(XC2[:, c, :], xr[:, c, :], cw[:, 4 * c + 3:4 * c + 4],
                                                             par2("conv_b")[:, c:c + 1], ALU.mult, ALU.add))
            for d in range(1, 4):
                for c in range(4):
                    ins = nc.vector.scalar_tensor_tensor(out=XC2[:, c, d:T], in0=xr[:, c, 0:T - d],
                                                         scalar=cw[:, 4 * c + 3 - d:4 * c + 4 - d], in1=XC2[:, c, d:T],
                                                         op0=ALU.mult, op1=ALU.add)
                    if d < 3:
                        (L if c == 3 else I)(ins)
                    elif c < 3:
                        I(ins)
            ins.then_inc(S("lru_dve"), 1)
            v.wait_ge(S("lru_act"), 1)
            L(nc.vector.tensor_scalar(LSL, par2("lam"), 0.0, None, ALU.min))
            L(nc.vector.tensor_tensor(LSL, LSL, SM[:, 104:108], ALU.subtract))
            L(nc.vector.tensor_scalar(LSL, LSL, LRU_C, None, ALU.mult))
            v.wait_ge(S("rg_gates"), 8)
            for c in range(4):
                ins = nc.vector.tensor_scalar(RA[:, c, :], RA[:, c, :], LSL[:, c:c + 1], None, ALU.mult)
                if c < 3:
                    I(ins)
            ins.then_inc(S("lru_dve"), 1)
            L(nc.vector.tensor_tensor(RI, RI, XC2, ALU.mult))
            v.wait_ge(S("proj2_evac"), 4)
            gelu_in_dve(v, L, xg, GE)
            v.wait_ge(S("lru_act"), 2)
            L(nc.vector.tensor_scalar(XC2, RA, 1.0, None, ALU.add))
            L(nc.vector.reciprocal(XC2, XC2))
            L(nc.vector.scalar_tensor_tensor(out=RA, in0=RA, scalar=2.0, in1=XC2, op0=ALU.mult, op1=ALU.mult))
            nc.vector.tensor_scalar(RA, RA, 0.0, None, ALU.max).then_inc(S("lru_dve"), 1)
            gelu_out_dve(v, L, DEPTH, xg, GE, GE)
            v.wait_ge(S("lru_act"), 3)
            L(nc.vector.tensor_tensor(RI, RI, RA, ALU.mult))
            for c in range(4):
                (L if c == 3 else I)(nc.vector.tensor_tensor_scan(XC2[:, c, :], AE[:, c, :], RI[:, c, :], 0.0, ALU.mult, ALU.add))
            v.wait_ge(S("gelu"), DEPTH + 1)
            v.wait_ge(S("proj2_ready"), 8)
            nc.vector.tensor_tensor(OT[:, 4:8, :], XC2, GE, ALU.mult).then_inc(S("lru_dve"), 1)

        ROWS = view(SB, 3 * D, [2, T])
        MIX2_BANK = {(0, 0): 5, (0, 1): 6, (1, 0): 7, (1, 1): 0}

        def branch(a):
            return range(4, 8) if a == 0 else range(0, 4), (7, 1)[a]

        def merge_square_act(act, a):
            ks, b = branch(a)
            act.wait_ge(*((S("lru_dve"), 4), (S("nsa_out"), DEPTH + 1))[a])
            nc.scalar.activation(SQM[:, ks[0]:ks[0] + 4, :], OT[:, ks[0]:ks[0] + 4, :], ACT.Square).then_inc(S("merge_sq"), 1)

        def merge_sum_pe(pe, a):
            ks, b = branch(a)
            pe.wait_ge(S("merge_sq"), a + 1)
            for k in ks:
                m = pe.matmul(ps[:, b, 0:T], cst("ones")[:, 0:P], SQM[:, k, :], start=k == ks[0], stop=k == ks[-1])
            m.then_inc(S("merge_ss"), 1)

        def merge_root_act(act, a):
            ks, b = branch(a)
            act.wait_ge(S("merge_ss"), a + 1)
            nc.scalar.activation(ROWS[:, a, :], ps[:, b, 0:T], ACT.Sqrt, scale=1.0 / 512, bias=cst("eps")).then_inc(S("merge_rms"), 1)

        def merge_scale_dve(v, a, I, L):
            ks, b = branch(a)
            v.wait_ge(S("merge_rms"), a + 1)
            L(nc.vector.reciprocal(ROWS[:, a, :], ROWS[:, a, :]))
            gain = par2(("g_lru", "g_attn")[a])
            for k in ks:
                ins = nc.vector.scalar_tensor_tensor(out=OT[:, k, :], in0=OT[:, k, :], scalar=gain[:, k % 4:k % 4 + 1],
                                                     in1=ROWS[:, a, :], op0=ALU.mult, op1=ALU.mult)
                if k != ks[-1]:
                    I(ins)
            ins.then_inc(S("merge_scaled"), 1)

        def mix2_pe(pe, a, t, c):
            ks, b = branch(a)
            pe.wait_ge(S("merge_scaled"), a + 1)
            need_slot(pe, S_WO2 + c)
            w = slot(S_WO2 + c).rearrange("p (k n) -> p k n", k=KT)
            for k in ks:
                m = pe.matmul(ps[:, MIX2_BANK[t, c], :], OT[:, k, t * P:(t + 1) * P], w[:, k, :],
                              start=a == 0 and k == ks[0], stop=a == 1 and k == ks[-1], skip_group_check=True)
            return m

        def merge_pe(pe):
            merge_sum_pe(pe, 1)
            mix2_pe(pe, 0, 1, 1)
            for t in range(NT):
                for c in range(2):
                    m = mix2_pe(pe, 1, t, c)
                m.then_inc(S("mix2_ready"), 1)

        def residual_dve(v, t, I, L):
            v.wait_ge(S("mix2_ready"), t + 1)
            if t == NT - 1:
                v.sem_inc(S("moe_slot"), RING)
            for c in range(2):
                cols = slice(512 * c, 512 * (c + 1))
                (I if c == 0 else L)(nc.vector.tensor_tensor(YT[:, cols], ps[:, MIX2_BANK[t, c], :], MOD[:, 2, cols], ALU.mult))
            nc.vector.tensor_tensor(X[:, t, :], X[:, t, :], YT, ALU.add).then_inc(S("x_tile" if t == 0 else "x_ready"), 1)
            v.wait_ge(S("x_tile" if t == 0 else "x_ready"), 2 * DEPTH + 1)

        LG, SEL, GT2, RNK = (view(SA, 4096 + 64 * i, [NT, NE]) for i in range(4))
        RANK, GATE = view(SA, 4352, [NT, NITEM]), view(SA, 4448, [NT, NITEM])
        M8 = view(SA, 4544, [NT, 8])
        TMP, CUM = view(SA, 4560, [NE]), view(SA, 4592, [NE])
        NXT, CE, EXC = (view(SA, 4624 + 32 * i, [NE]) for i in range(3))
        REM, NEGM, RSUM = SM[:, 170:172], SM[:, 172:174], SM[:, 174:176]
        EQ, CUM = view(SA, 4560, [NT, NE]), view(SA, 4624, [NT, NE])
        TOT, NXT, CE, EXC = (SM[0:NE, 100 + i:101 + i] for i in range(4))
        OVER = SM[0:NE, 104:108]
        OH, OX, OW = (view(SB, 12288 + NITEM * i, [NITEM])[0:NE, :] for i in range(3))
        RNKT = view(SB, 12544, [T])
        GTT = view(SA, 4800, [T])

        def router_pe(pe):
            pe.wait_ge(S("xt_ready"), 4 * 6)
            pe.wait_ge(S("x_ready"), 2 * DEPTH + 1)
            w = par2("router").rearrange("p (k e) -> p k e", k=KT)
            for t in range(NT):
                for k in range(KT):
                    m = pe.matmul(ps[:, 0, t * NE:(t + 1) * NE], XT[:, k, t * P:(t + 1) * P], w[:, k, :],
                                  start=k == 0, stop=k == KT - 1)
            m.then_inc(S("counts"), 1)
            pe.wait_ge(S("selected"), 1)
            strict, ones = cst("pairs")[:, 0:P], cst("ones")[:, 0:P]
            pe.matmul(ps[:, 1, 0:NE], strict, SEL[:, 0, :], start=True, stop=True)
            pe.matmul(ps[:, 1, NE:2 * NE], strict, SEL[:, 1, :], start=True, stop=False)
            pe.matmul(ps[:, 1, NE:2 * NE], ones, SEL[:, 0, :], start=False, stop=True)
            for t in range(NT):
                m = pe.matmul(ps[0:NE, 1, 2 * NE:2 * NE + 1], SEL[:, t, :], ones[:, 0:1], start=t == 0, stop=t == NT - 1)
            m.then_inc(S("counts"), 1)
            pe.wait_ge(S("nxt"), 1)
            pe.matmul(ps[0:NE, 0, P:P + 1], cst("pairs")[0:NE, P:P + NE], NXT, start=True, stop=True).then_inc(S("item_end"), 1)
            for t in range(NT):
                m = pe.transpose(ps[0:NE, 2, t * P:(t + 1) * P], RNK[:, t, :], ident)
            m.then_inc(S("rank_t_ps"), 1)
            pe.wait_ge(S("gates"), 1)
            for t in range(NT):
                m = pe.transpose(ps[0:NE, 1, t * P:(t + 1) * P], GT2[:, t, :], ident)
            m.then_inc(S("gates_t_ps"), 1)
            pe.wait_ge(S("owner"), 1)
            pe.matmul(ps[0:1, 0, 256:256 + NITEM], cst("part")[0:NE, :], OH, start=True, stop=True)
            m = pe.matmul(ps[0:1, 0, 384:384 + NITEM], ones[0:NE, 0:1], OH, start=True, stop=True)
            m.then_inc(S("owner_ps"), 1)
            pe.wait_ge(S("gates_t"), 1)
            for t in range(NT):
                pe.matmul(ps[:, 3, t * NITEM:(t + 1) * NITEM], RNKT[0:NE, t * P:(t + 1) * P], OH, start=True, stop=False)
                pe.matmul(ps[:, 3, t * NITEM:(t + 1) * NITEM], ones[0:NE, :], OW, start=False, stop=True)
            for t in range(NT, 2 * NT):
                m = pe.matmul(ps[:, 3, t * NITEM:(t + 1) * NITEM], GTT[0:NE, (t - NT) * P:(t - NT + 1) * P], OH, start=True, stop=True)
            m.then_inc(S("places_ps"), 1)
            pe.wait_ge(S("par2_loaded"), 64)
            for t in range(NT):
                for c in range(2):
                    pe.matmul(ps[:, 4 + 2 * t + c, :], GTT[0:NE, t * P:(t + 1) * P], BD[0:NE, c * 512:(c + 1) * 512],
                                  start=True, stop=True)

        def router_act(act):
            act.wait_ge(S("top"), 1)
            for t in range(NT):
                nc.scalar.activation(GT2[:, t, :], LG[:, t, :], ACT.Exp, bias=NEGM[:, t:t + 1]).then_inc(S("gate_exp"), 1)

        def router_dve(v, I, L):
            v.wait_ge(S("counts"), 1)
            L(nc.vector.tensor_tensor(LG, ps[:, 0, 0:2 * NE].rearrange("p (t e) -> p t e", t=NT),
                                      BR.unsqueeze(1).broadcast_to([P, NT, NE]), ALU.add))
            for t in range(NT):
                (I if t == 0 else L)(nc.vector.max(M8[:, t, :], LG[:, t, :]))
            nc.vector.tensor_scalar(NEGM.unsqueeze(2), M8[:, :, 0:1], -1.0, None, ALU.mult).then_inc(S("top"), 1)
            fourth = M8[:, :, TOPK - 1:TOPK].broadcast_to([P, NT, NE])
            I(nc.vector.tensor_tensor(EQ, LG, fourth, ALU.is_equal))
            L(nc.vector.tensor_tensor(SEL, LG, fourth, ALU.is_gt))
            L(nc.vector.tensor_reduce(REM, SEL, AX.X, ALU.add))
            for t in range(NT):
                I(nc.vector.tensor_tensor_scan(CUM[:, t, :], cst("ones")[:, 0:NE], EQ[:, t, :], 0.0, ALU.mult, ALU.add))
            L(nc.vector.tensor_scalar(REM, REM, -1.0, float(TOPK), ALU.mult, ALU.add))
            L(nc.vector.tensor_tensor(CUM, CUM, REM.unsqueeze(2).broadcast_to([P, NT, NE]), ALU.is_le))
            L(nc.vector.tensor_tensor(EQ, EQ, CUM, ALU.mult))
            nc.vector.tensor_tensor(SEL, SEL, EQ, ALU.add).then_inc(S("selected"), 1)
            v.wait_ge(S("selected"), 1)
            v.wait_ge(S("counts"), 2)
            cnt = ps[:, 1, 0:2 * NE].rearrange("p (t e) -> p t e", t=NT)
            I(nc.vector.scalar_tensor_tensor(out=RNK, in0=cnt, scalar=2000.0, in1=SEL, op0=ALU.add, op1=ALU.mult))
            L(nc.vector.tensor_copy(TOT, ps[0:NE, 1, 2 * NE:2 * NE + 1]))
            L(nc.vector.tensor_scalar(OVER, cst("iota")[0:NE, 0:T // SLOTS_E], float(SLOTS_E), TOT, ALU.mult, ALU.is_lt))
            nc.vector.tensor_reduce(NXT, OVER, AX.X, ALU.add).then_inc(S("nxt"), 1)
            v.wait_ge(S("nxt"), 1)
            v.wait_ge(S("gate_exp"), NT)
            L(nc.vector.tensor_tensor(GT2, GT2, SEL, ALU.mult))
            L(nc.vector.tensor_reduce(RSUM, GT2, AX.X, ALU.add))
            L(nc.vector.reciprocal(RSUM, RSUM))
            nc.vector.tensor_tensor(GT2, GT2, RSUM.unsqueeze(2).broadcast_to([P, NT, NE]), ALU.mult).then_inc(S("gates"), 1)
            v.wait_ge(S("item_end"), 1)
            L(nc.vector.tensor_copy(CE, ps[0:NE, 0, P:P + 1]))
            L(nc.vector.tensor_tensor(EXC, CE, NXT, ALU.subtract))
            item = cst("iota")[0:NE, 0:NITEM]
            I(nc.vector.tensor_scalar(OX, item, EXC, None, ALU.subtract))
            L(nc.vector.tensor_scalar(OH, item, CE, None, ALU.is_lt))
            L(nc.vector.scalar_tensor_tensor(out=OH, in0=OX, scalar=0.0, in1=OH, op0=ALU.is_ge, op1=ALU.mult))
            nc.vector.scalar_tensor_tensor(out=OW, in0=OX, scalar=-float(SLOTS_E), in1=OH, op0=ALU.mult,
                                           op1=ALU.mult).then_inc(S("owner"), 1)
            v.wait_ge(S("rank_t_ps"), 1)
            I(nc.vector.tensor_copy(RNKT[0:NE, :], ps[0:NE, 2, 0:T]))
            v.wait_ge(S("owner_ps"), 1)
            L(nc.vector.tensor_copy(ITI[0:1, 8:8 + NITEM], ps[0:1, 0, 256:256 + NITEM]))
            valid = ps[0:1, 0, 384:384 + NITEM].rearrange("p (i a) -> p i a", a=2)[:, :, 0]
            L(nc.vector.tensor_reduce(SM[0:1, 108:109], valid, AX.X, ALU.add))
            nc.vector.tensor_copy(ITI[0:1, 0:1], SM[0:1, 108:109]).then_inc(S("items"), 1)
            v.wait_ge(S("gates_t_ps"), 1)
            nc.vector.tensor_copy(GTT[0:NE, :], ps[0:NE, 1, 0:T]).then_inc(S("gates_t"), 1)
            v.wait_ge(S("places_ps"), 1)
            places = ps[:, 3, 0:4 * NITEM].rearrange("p (a t i) -> p a t i", a=2, t=NT)
            I(nc.vector.tensor_scalar(RANK, places[:, 0], 2000.0, None, ALU.subtract))
            L(nc.vector.tensor_copy(GATE, places[:, 1]))

        hid = HT[:].rearrange("p a t -> p (a t)")
        XE = view(hid, 0, [KT, P])
        EH, EHT, EY = view(hid, 1024, [512]), view(hid, 1536, [4, P]), view(hid, 2048, [512])
        EPT = view(hid, 2560, [T])
        EG, EU, ES = (view(hid, 2816 + 512 * i, [512]) for i in range(3))
        EP0 = view(hid, 4352, [NT, 2, SLOTS_E])
        EPW = view(hid, 4608, [2, NT, 2, SLOTS_E])
        BGU = view(SB, 10240, [2, 2, 512])
        EOW = view(hid, 5120, [2, SLOTS_E])
        PAIR_SLOTS = 2 * ITEM_SLOTS

        def moe_pairs(eng):
            eng.wait_ge(S("items"), 1)
            return eng.value_load(ITI[0:1, 0:1], min_val=MIN_ITEM // 2, max_val=NITEM // 2)

        def moe_sp(sp):
            sp.wait_ge(S("h_ready"), 2)
            sp.dma_start(BD[0:NE, :], dram["b_down"]).then_inc(S("par2_loaded"), 16)
            sp.dma_start(BGU[0:NE, :, :, :].rearrange("p h a n -> p (h a n)"), dram["b_gu"]).then_inc(S("par2_loaded"), 16)
            with sp.Fori(0, moe_pairs(sp)) as it:
                for q in range(2):
                    e = sp.value_load(ITI[0:1, bass.ds(it * 2 + 8 + q, 1)], min_val=0, max_val=NE - 1)
                    for b in range(ITEM_SLOTS):
                        k = q * ITEM_SLOTS + b
                        sp.wait_ge(S("moe_slot"), it * PAIR_SLOTS + k + 1)
                        sp.dma_start(slot(S_MOE + k), dram["stream"][bass.ds(e * ITEM_SLOTS + S_MOE + b, 1), :, :]
                                     .rearrange("a p n -> (a p) n")).then_inc(arrived[(S_MOE + k) % RING], 16)

        def need_moe_slot(pe, it, k):
            i = S_MOE + k
            pe.wait_ge(arrived[i % RING], it * (16 * PAIR_SLOTS // RING) + 16 * (i // RING + 1))

        def moe_pe(pe):
            with pe.Fori(0, moe_pairs(pe)) as it:
                for q in range(2):
                    if q == 0:
                        pe.wait_ge(S("moe_p"), it + 1)
                        pe.wait_ge(S("moe_y_evac"), it * 2 + 1)
                        for k in range(KT):
                            for t in range(NT):
                                m = pe.matmul(ps[:, 2 + k // 4, (k % 4) * P:(k % 4 + 1) * P], HF[:, t, k * P:(k + 1) * P],
                                              EP0[:, t, :, :].rearrange("p a s -> p (a s)"), start=t == 0, stop=t == NT - 1)
                        m.then_inc(S("moe_xe_ps"), 1)
                        pe.wait_ge(S("moe_xe"), it * 2 + 2)
                    pe.wait_ge(S("moe_gu_evac"), it * 2 + q + 1)
                    for a in range(2):
                        for half in range(2):
                            pe.matmul(ps[HD * half:HD * (half + 1), a, :], EOW[0:NE, q, :], BGU[0:NE, half, a, :],
                                      start=True, stop=False, skip_group_check=True)
                    for b in range(4):
                        need_moe_slot(pe, it, q * ITEM_SLOTS + b)
                        w = slot(S_MOE + q * ITEM_SLOTS + b).rearrange("p (k a h n) -> p k a h n", k=2, a=2, h=2)
                        for k in range(2):
                            for a in range(2):
                                for half in range(2):
                                    m = pe.matmul(ps[HD * half:HD * (half + 1), a, :],
                                                  XE[:, 2 * b + k, q * SLOTS_E:(q + 1) * SLOTS_E], w[:, k, a, half, :],
                                                  start=False, stop=b + k == 4, skip_group_check=True)
                        m.then_inc(S("moe_slot"), 1)
                    pe.wait_ge(S("moe_pt"), it * 2 + q + 1)
                    pe.wait_ge(S("moe_y_evac"), it * 2 + q + 1)
                    moe_return_pe(pe)
                    for t in range(NT):
                        m = pe.transpose(ps[:, 3, t * P:(t + 1) * P], EPW[:, q, t, :, :].rearrange("p h s -> p (h s)"), ident)
                    m.then_inc(S("moe_pt_ps"), 1)
                    pe.wait_ge(S("moe_h"), it * 2 + q + 1)
                    for f in range(4):
                        m = pe.transpose(ps[:, 2, f * P:(f + 1) * P], EH[:, f * P:(f + 1) * P], ident)
                    m.then_inc(S("moe_ht_ps"), 1)
                    pe.wait_ge(S("moe_pt"), it * 2 + q + 2)
                    pe.wait_ge(S("moe_ht"), it * 2 + q + 1)
                    for b in range(2):
                        need_moe_slot(pe, it, q * ITEM_SLOTS + 4 + b)
                        w = slot(S_MOE + q * ITEM_SLOTS + 4 + b).rearrange("p (k c n) -> p k c n", k=4, c=2)
                        for k in range(4):
                            for c in range(2):
                                m = pe.matmul(ps[HD * c:HD * (c + 1), 3, :], EHT[:, k, HD * b:HD * (b + 1)], w[:, k, c, :],
                                              start=b + k == 0, stop=b + k == 4, skip_group_check=True)
                        m.then_inc(S("moe_slot"), 1)
            pe.wait_ge(S("moe_last"), 1)
            moe_return_pe(pe)
            pe.transpose(ps[:, 0, 0:P], ident, ident).then_inc(S("moe_done"), 1)

        def moe_return_pe(pe):
            for t in range(NT):
                for c in range(2):
                    rows = slice(HD * c, HD * (c + 1))
                    m = pe.matmul(ps[:, 4 + 2 * t + c, :], EPT[rows, t * P:(t + 1) * P], EY[rows, :],
                                  start=False, stop=True, skip_group_check=True)
            m.then_inc(S("moe_sc"), 1)

        def moe_act(act):
            with act.Fori(0, moe_pairs(act)) as it:
                for q in range(2):
                    if q == 0:
                        act.wait_ge(S("moe_xe_ps"), it + 1)
                        for g in range(2):
                            nc.scalar.activation(XE[:, 4 * g:4 * g + 4, :].rearrange("p k s -> p (k s)"), ps[:, 2 + g, :],
                                                 ACT.Copy).then_inc(S("moe_xe"), 1)
                    act.wait_ge(S("moe_g"), it * 2 + q + 1)
                    nc.scalar.activation(ES, EG, ACT.Sigmoid, scale=SWIGLU_ALPHA).then_inc(S("moe_sig"), 1)
                    act.wait_ge(S("moe_pt_ps"), it * 2 + q + 1)
                    act.wait_ge(S("moe_sc"), it * 2 + q + 1)
                    nc.scalar.activation(EPT, ps[:, 3, 0:T], ACT.Copy).then_inc(S("moe_pt"), 1)
                    act.wait_ge(S("moe_ht_ps"), it * 2 + q + 1)
                    nc.scalar.activation(EHT.rearrange("p f s -> p (f s)"), ps[:, 2, :], ACT.Copy).then_inc(S("moe_ht"), 1)

        def moe_dve(v):
            v.sem_inc(S("moe_gu_evac"), 1)
            nc.vector.memset(EPT, 0.0).then_inc(S("moe_pt"), 1)
            nc.vector.memset(EY, 0.0).then_inc(S("moe_y_evac"), 1)
            pairs = moe_pairs(v)
            iota = cst("iota")[:, 0:SLOTS_E]
            both = iota.unsqueeze(1).broadcast_to([P, 2, SLOTS_E])
            with v.Fori(0, pairs) as it:
                for q in range(2):
                    for t in range(NT):
                        nc.vector.tensor_scalar(EPW[:, q, t, :, :], both, RANK[:, t, bass.ds(it * 2 + q, 1)],
                                                GATE[:, t, bass.ds(it * 2 + q, 1)], ALU.is_equal, ALU.mult)
                for q in range(2):
                    for t in range(NT):
                        ins = nc.vector.tensor_scalar(EP0[:, t, q, :], iota, RANK[:, t, bass.ds(it * 2 + q, 1)], None, ALU.is_equal)
                for q in range(2):
                    ins = nc.vector.tensor_scalar(EOW[0:NE, q, :], cst("ones")[0:NE, 0:SLOTS_E], OH[:, bass.ds(it * 2 + q, 1)],
                                                  None, ALU.mult)
                ins.then_inc(S("moe_p"), 1)
                for q in range(2):
                    v.wait_ge(S("moe_slot"), it * PAIR_SLOTS + (RING + q * ITEM_SLOTS + 4))
                    nc.vector.tensor_scalar(EG, ps[:, 0, :], LIMIT, None, ALU.min).then_inc(S("moe_g"), 1)
                    nc.vector.tensor_scalar(EU, ps[:, 1, :], LIMIT, -LIMIT, ALU.min, ALU.max).then_inc(S("moe_gu_evac"), 1)
                    v.wait_ge(S("moe_gu_evac"), it * 2 + q + 2)
                    v.wait_ge(S("moe_g"), it * 2 + q + 1)
                    nc.vector.scalar_tensor_tensor(out=EU, in0=EU, scalar=1.0, in1=EG, op0=ALU.add,
                                                   op1=ALU.mult).then_inc(S("moe_v"), 1)
                    v.wait_ge(S("moe_v"), it * 2 + q + 1)
                    v.wait_ge(S("moe_sig"), it * 2 + q + 1)
                    nc.vector.tensor_tensor(EH, EU, ES, ALU.mult).then_inc(S("moe_h"), 1)
                    v.wait_ge(S("moe_slot"), it * PAIR_SLOTS + (RING + q * ITEM_SLOTS + 6))
                    nc.vector.tensor_copy(EY, ps[:, 3, :]).then_inc(S("moe_y_evac"), 1)
            nc.vector.memset(SM[:, 110:111], 0.0).then_inc(S("moe_last"), 1)

        def final_dve(v, I, L):
            v.wait_ge(S("moe_done"), 1)
            for t in range(NT):
                L(nc.vector.tensor_tensor(YT, bank(4 + 2 * t, 2), MOD[:, 5, :], ALU.mult))
                nc.vector.tensor_tensor(X[:, t, :], X[:, t, :], YT, ALU.add).then_inc(S("x_tile" if t == 0 else "x_ready"), 1)
                v.wait_ge(S("x_tile" if t == 0 else "x_ready"), 2 * DEPTH + 2)
            v.wait_ge(S("gain_loaded"), 48)
            for t in range(NT):
                rms_dve(v, 2, t, L)
                nc.vector.scalar_tensor_tensor(out=X[:, t, :], in0=X[:, t, :], scalar=SM[:, 98 + t:99 + t], in1=LNW,
                                               op0=ALU.mult, op1=ALU.mult).then_inc(S("final"), 1)

        HALF_LEVELS, ATT_LAG = 14, 2
        STEPS = HALF_LEVELS + 6
        CMP_TURN, CMP_OUT, GLA_NORM, GLA_BACK = 0, 1, 1, 2

        def unit_scores(u):
            return 0 <= u < NU

        def unit_turn(u):
            return 1 <= u <= NU

        def unit_out(u):
            return 2 <= u <= NU + 1

        def mixers_pe(pe, l):
            for u in range(8):
                gla_scores_pe(pe, l, u)
                rwkv_pairs_pe(pe, l, u)
                if u < ROPE_PIECES:
                    rope_pe(pe, l, u)
                if u <= ADA:
                    modulation_pe(pe, l, u)
            cmp_hidden_pe(pe, l)
            inverse_product_pe(pe, l, 0)
            for s in range(STEPS):
                u, at = s - ATT_LAG, NU * l + s - ATT_LAG
                j, part = divmod(s - HALF_LEVELS, 3)
                if s + 1 < HALF_LEVELS:
                    inverse_product_pe(pe, l, s + 1)
                if unit_scores(u):
                    if u == 0:
                        pe.wait_ge(S("mod"), l + 1)
                    attention_scores_pe(pe, at)
                if s < HALF_LEVELS:
                    inverse_update_pe(pe, l, s)
                else:
                    (chunk_removed_pe, chunk_solve_pe, chunk_out_pe)[part](pe, l, j)
                if s == 0:
                    gla_out_pe(pe, l)
                if s == GLA_BACK:
                    back_pe(pe, 2 * l, G_XC, 4)
                if s == CMP_TURN:
                    cmp_turn_pe(pe, l)
                if s == CMP_OUT:
                    cmp_out_pe(pe, l)
                if unit_turn(u):
                    if u == 1:
                        pe.wait_ge(S("cmp_kv"), l + 1)
                    attention_turn_pe(pe, at - 1)
                if unit_out(u):
                    if u == 2:
                        pe.wait_ge(S("gla_out"), l + 1)
                    attention_out_pe(pe, at - 2)
                if s in (STEPS - 3, STEPS - 2):
                    mix_early_pe(pe, l, 0, s - (STEPS - 3))
            for c in range(2):
                mix_early_pe(pe, l, 1, c)
            back_pe(pe, 2 * l + 1, R_XC, 5)

        def mixers_act(act, l):
            for u in range(NQC):
                gla_key_act(act, l, u)
                if u == 1:
                    rwkv_bk_act(act, l)
                if u >= 2 and u - 2 < ADA:
                    modulation_act(act, l, u - 2)
            inverse_product_act(act, l, 0)
            cmp_act(act, l)
            for s in range(STEPS):
                u, at = s - ATT_LAG, NU * l + s - ATT_LAG
                if s + 1 < HALF_LEVELS:
                    inverse_product_act(act, l, s + 1)
                if s == 0:
                    nsa_gate_act(act, l)
                    gla_gate_act(act, l)
                if s == GLA_NORM:
                    head_norm_act(act, 2 * l)
                if unit_scores(u):
                    attention_exp_act(act, at)
                if unit_turn(u):
                    attention_out_act(act, at - 1)
            head_norm_act(act, 2 * l + 1)

        def mixers_dve(v, l, I, L):
            gla_key_dve(v, l, 0)
            gla_key_dve(v, l, 1)
            rwkv_init_dve(v, l, I, L)
            for u in range(8):
                rwkv_mask_dve(v, l, u)
                if u + 2 < NQC:
                    gla_key_dve(v, l, u + 2)
                if u < ROPE_PIECES:
                    rope_dve(v, l, u, I, L)
            v.wait_ge(S("rw_mm"), 8 * (l + 1))
            inverse_level_dve(v, l, 0)
            inverse_level_dve(v, l, 1)
            gla_mask_dve(v, l)
            modulation_dve(v, l)
            cmp_hidden_dve(v, l, L)
            v.wait_ge(S("rw_init"), l + 1)
            for s in range(STEPS):
                u, at = s - ATT_LAG, NU * l + s - ATT_LAG
                j, part = divmod(s - HALF_LEVELS, 3)
                if unit_turn(u):
                    attention_scale_dve(v, at - 1, L)
                if unit_scores(u):
                    if u == 0:
                        v.wait_ge(S("nsa_gate"), l + 1)
                    attention_scores_dve(v, at, I, L)
                if s < HALF_LEVELS:
                    inverse_update_dve(v, l, s)
                elif part == 0:
                    chunk_removed_dve(v, l, j)
                elif part == 1:
                    chunk_solve_dve(v, l, j)
                elif j == 0:
                    chunk_state_dve(v, l, I)
                if u == NU + 2:
                    attention_merge_dve(v, NU * (l + 1), I)
                if s == GLA_NORM:
                    gla_norm_dve(v, l, I, L)
                if s == GLA_BACK:
                    v.wait_ge(S("back_ps"), 2 * l + 1)
                    nc.vector.tensor_copy(OT[:, 0:2, :].rearrange("p c t -> p (c t)"), ps[:, 4, :]).then_inc(S("gla_out"), 1)
                if s == CMP_TURN:
                    cmp_turn_dve(v, l)
                if s == CMP_OUT:
                    cmp_out_dve(v, l, I)
            rwkv_norm_dve(v, l, I, L)
            v.wait_ge(S("back_ps"), 2 * l + 2)
            nc.vector.tensor_copy(OT[:, 2:4, :].rearrange("p c t -> p (c t)"), ps[:, 5, :]).then_inc(S("rw_out"), 1)

        block = ctx.enter_context(nc.Block())

        @block.sync
        def _(sp):
            first_sp(sp)
            second_sp(sp)
            moe_sp(sp)
            sp.wait_ge(S("final"), NT)
            sp.dma_start(dram["out"].rearrange("(t p) d -> p t d", p=P), X[:]).then_inc(S("stored"), 16)
            sp.wait_ge(S("stored"), 16)

        @block.gpsimd
        def _(pool):
            for l in range(DEPTH):
                cmp_pool(pool, l)
                for s in range(2, HALF_LEVELS):
                    inverse_level_pool(pool, l, s)

        @block.tensor
        def _(pe):
            for l in range(DEPTH):
                transpose_x_pe(pe, 2 * l, X, (("x_tile", 2 * l), ("x_ready", 2 * l)) if l else (("x_loaded", 32),) * 2)
                project_pe(pe, l, range(5))
                gla_gate_pe(pe, l)
                rwkv_ranks_pe(pe, l)
                project_pe(pe, l, (5,))
                rwkv_norm_pe(pe, l)
                project_pe(pe, l, (6,))
                rwkv_bonus_pe(pe, l)
                mixers_pe(pe, l)
                mix_late_pe(pe, l)
                transpose_x_pe(pe, 2 * l + 1, X, (("x_tile", 2 * l + 1), ("x_ready", 2 * l + 1)))
                ffn_pe(pe, l)
            transpose_x_pe(pe, 4, HF, (("h_tile", 1), ("h_ready", 1)))
            project2_pe(pe, (0, 1))
            rg_pe(pe)
            project2_pe(pe, (2, 3))
            pe.wait_ge(S("rg_gates"), 8)
            pe.wait_ge(S("proj2_evac"), 8)
            attention_scores_pe(pe, NU * DEPTH)
            merge_sum_pe(pe, 0)
            for i, n in enumerate(range(NU * DEPTH, len(UNITS))):
                if n + 1 < len(UNITS):
                    attention_scores_pe(pe, n + 1)
                attention_turn_pe(pe, n)
                if i:
                    mix2_pe(pe, 0, (i - 1) // 2, (i - 1) % 2)
                attention_out_pe(pe, n)
            merge_pe(pe)
            transpose_x_pe(pe, 5, HF, (("h_tile", 2), ("h_ready", 2)))
            router_pe(pe)
            moe_pe(pe)

        @block.scalar
        def _(act):
            I, L = link(act, "act_step")
            for l in range(DEPTH):
                project_act(act, l, range(9))
                act.wait_ge(S("start_loaded"), 32)
                act.wait_ge(S("par_loaded"), 32 * (l + 1))
                rwkv_ranks_act(act, l, I)
                project_act(act, l, (9,))
                gla_decay_act(act, l, L)
                rwkv_gates_act(act, l, I)
                project_act(act, l, (10,))
                gla_query_act(act, l)
                project_act(act, l, (11, 12))
                rwkv_decay_act(act, l, I)
                rwkv_values_act(act, l)
                project_act(act, l, (13, 14))
                mixers_act(act, l)
                layer_norm_act(act, 2 * l)
                ffn_act(act, l)
                layer_norm_act(act, 2 * l + 1)
            for t in range(NT):
                rms_act(act, 0, t, (("x_tile", "x_ready")[t], 2 * DEPTH))
            lam_act(act, L)
            project2_act(act, range(4))
            rg_act(act)
            lru_decay_act(act, I)
            lru_gate_act(act)
            project2_act(act, range(4, 6))
            lru_end_act(act)
            project2_act(act, range(6, 8))
            merge_square_act(act, 0)
            attention_exp_act(act, NU * DEPTH)
            merge_root_act(act, 0)
            for n in range(NU * DEPTH, len(UNITS)):
                if n + 1 < len(UNITS):
                    attention_exp_act(act, n + 1)
                attention_out_act(act, n)
            merge_square_act(act, 1)
            merge_root_act(act, 1)
            for t in range(NT):
                rms_act(act, 1, t, (("x_tile", "x_ready")[t], 2 * DEPTH + 1))
            router_act(act)
            moe_act(act)
            for t in range(NT):
                rms_act(act, 2, t, (("x_tile", "x_ready")[t], 2 * DEPTH + 2))

        @block.vector
        def _(v):
            I, L = link(v, "dve_step")
            for l in range(DEPTH):
                transpose_x_dve(v, 2 * l)
                v.wait_ge(S("start_loaded"), 32)
                mix_dve(v, l, I, L)
                rwkv_square_dve(v, l, I, L)
                gla_decay_dve(v, l, I, L)
                rwkv_prepare_dve(v, l, I, L)
                mixers_dve(v, l, I, L)
                if l == 0:
                    v.wait_ge(S("x_loaded"), 32)
                layer_norm_dve(v, 2 * l, 0, ("mix_ready", 2 * l + 1), L)
                transpose_x_dve(v, 2 * l + 1)
                ffn_dve(v, l, L)
                layer_norm_dve(v, 2 * l + 1, 4, ("down_ready", 7 * l + 6), L)
            for t in range(NT):
                modulated_dve(v, 0, t, L)
            v.wait_ge(S("par2_loaded"), 32)
            transpose_x_dve(v, 4)
            lru_dve(v, I, L)
            attention_scores_dve(v, NU * DEPTH, I, L)
            for n in range(NU * DEPTH, len(UNITS)):
                if n + 1 < len(UNITS):
                    attention_scores_dve(v, n + 1, I, L)
                attention_scale_dve(v, n, L)
                if n == NU * DEPTH:
                    merge_scale_dve(v, 0, I, L)
            attention_merge_dve(v, len(UNITS), I)
            merge_scale_dve(v, 1, I, L)
            for t in range(NT):
                residual_dve(v, t, I, L)
                modulated_dve(v, 1, t, L)
            transpose_x_dve(v, 5)
            router_dve(v, I, L)
            moe_dve(v)
            final_dve(v, I, L)


def slots_of(w, cols):
    k, n = w.shape
    return w.reshape(k // P, P, n // cols, cols).transpose(2, 1, 0, 3).reshape(n // cols, P, SLOT)


def channels(v):
    return np.asarray(v).reshape(-1, P).T


def lay_out(a):
    f = np.float32
    a = {k: np.asarray(v) for k, v in a.items()}
    heads = np.arange(8)
    qperm = np.concatenate([np.arange(HD) + HD * (g * 4 + j) for j in range(4) for g in range(2)])
    stream = np.zeros((N_SLOTS, P, SLOT), f)
    layer = np.zeros((DEPTH, P, LAYER_COLS), f)
    head_norm = np.zeros((DEPTH, 4 * 256), f)

    def put(to, fields, name, value, rows=slice(0, P), at=0):
        x = fields[name][0] + at
        to[rows, x:x + value.shape[1]] = value

    for l in range(DEPTH):
        w = a["w_in"][l]
        gla, rw, nsa = w[:, :1040], w[:, 1040:2096], w[:, 2096:3400]
        zero = lambda n: np.zeros((D, n), f)
        vres = a["w_in_vres"][l - 1] if l else zero(32)
        kv = [nsa[:, 512 + P * i:512 + P * (i + 1)] for i in range(6)]
        misc = np.concatenate([rw[:, 1024:1056], vres, gla[:, 1024:1040], zero(48)], 1)
        cols = np.concatenate([gla[:, 0:512], rw[:, 0:512], rw[:, 512:768], rw[:, 768:896], rw[:, 896:1024], misc,
                               kv[1], kv[0], kv[2], kv[4], nsa[:, qperm][:, 0:512],
                               kv[3], kv[5], nsa[:, 1280:1304], zero(104), gla[:, 512:1024]], 1)
        s = l * LAYER_SLOTS
        stream[s:s + 7] = slots_of(cols, 512)
        for i, name in enumerate(("nsa_wk1", "nsa_wv1")):
            stream[s + S_CMP + i] = a[name][l].reshape(16, P, 256).transpose(1, 0, 2).reshape(P, SLOT)
        stream[s + S_ADA:s + S_CMP] = slots_of(a["w_ada_2"][0], 512)[l * ADA:(l + 1) * ADA]
        rows = np.concatenate([np.arange(512), 512 + qperm])
        stream[s + S_WO:s + S_GU] = slots_of(a["w_out"][l][rows], 512)
        g, u = (a[n][l].reshape(D, 11, 256) for n in ("ffn_w_gate", "ffn_w_up"))
        stream[s + S_GU:s + S_DN] = slots_of(np.stack([g, u], 2).reshape(D, 11 * 512), 512)
        down = np.zeros((24, P, D), f)
        down[:NF] = a["ffn_w_down"][l].reshape(NF, P, D)
        stream[s + S_DN:s + LAYER_SLOTS] = down.reshape(6, 4, P, D).transpose(0, 2, 1, 3).reshape(6, P, SLOT)
        to = layer[l]
        mu = np.zeros(9 * P, f)
        mu[0:1024], mu[1024:1056] = a["rwkv_mu"][l][0:1024], a["rwkv_mu"][l][1024:1056]
        if l:
            mu[1056:1088] = a["rwkv_mu_vres"][l - 1]
        put(to, LAYER_FIELDS, "mu", channels(mu))
        for field, name in (("b_a", "gla_b_a"), ("w0", "rwkv_w0"), ("a0", "rwkv_a0"), ("k_k", "rwkv_k_k"), ("k_a", "rwkv_k_a")):
            put(to, LAYER_FIELDS, field, channels(a[name][l]))
        rk = np.zeros((2, P, 4), f)
        for h in range(4):
            rk[h // 2, HD * (h % 2):HD * (h % 2 + 1), h] = a["rwkv_r_k"][l][h]
        put(to, LAYER_FIELDS, "r_k", rk.transpose(1, 0, 2).reshape(P, 8))
        put(to, LAYER_FIELDS, "wa", a["rwkv_w2"][l], slice(0, 64))
        put(to, LAYER_FIELDS, "wa", a["rwkv_a2"][l], slice(64, 128))
        put(to, LAYER_FIELDS, "g2", a["rwkv_g2"][l][0:P])
        put(to, LAYER_FIELDS, "misc", a["rwkv_g2"][l][P:160], slice(M_G2, M_G2 + 32))
        if l:
            put(to, LAYER_FIELDS, "misc", a["rwkv_v2"][l - 1], slice(M_VR, M_VR + 32))
            put(to, LAYER_FIELDS, "v0", channels(a["rwkv_v0"][l - 1]))
        put(to, LAYER_FIELDS, "misc", a["gla_w_a2"][l], slice(M_GA, M_GA + 16))
        for field, name in (("wk2", "nsa_wk2"), ("wv2", "nsa_wv2")):
            put(to, LAYER_FIELDS, field, a[name][l].reshape(2, P, HD).transpose(1, 0, 2).reshape(P, P))
        for field, name in (("pos_k", "nsa_pos_k"), ("pos_v", "nsa_pos_v")):
            put(to, LAYER_FIELDS, field, np.concatenate([a[name][l].T] * 2, 0))
        head_norm[l] = np.concatenate([a[n][l] for n in ("gla_ln_w", "gla_ln_b", "rwkv_ln_w", "rwkv_ln_b")])
    w = a["w_in_2"][0]
    cols = np.concatenate([w[:, 768:1280], w[:, 1280:1792], w[:, qperm], w[:, 512:640], w[:, 640:768], np.zeros((D, 256), f)], 1)
    stream[S_IN2:S_WO2] = slots_of(cols, 512)
    rows = np.concatenate([qperm, 512 + np.arange(512)])
    stream[S_WO2:S_MOE] = slots_of(a["w_out_2"][0][rows], 512)
    moe = stream[S_MOE:].reshape(NE, ITEM_SLOTS, P, SLOT)
    moe[:, 0:4] = a["w_gu_2"][0].reshape(NE, 4, 2, P, 2 * DE).transpose(0, 1, 3, 2, 4).reshape(NE, 4, P, SLOT)
    moe[:, 4:6] = a["w_down_2"][0].reshape(NE, 2, 4, P, D).transpose(0, 1, 3, 2, 4).reshape(NE, 2, P, SLOT)
    second = np.zeros((P, SECOND_COLS), f)
    F2 = SECOND_FIELDS
    put(second, F2, "conv_w", a["conv_w_2"][0].reshape(4, 4, P).transpose(2, 1, 0).reshape(P, 16))
    put(second, F2, "conv_b", channels(a["conv_b_2"][0]))
    for field, name in (("rg_a", "w_rg_a_2"), ("rg_x", "w_rg_x_2")):
        for c in range(4):
            for h in range(2):
                put(second, F2, field, a[name][0][2 * c + h], slice(HD * h, HD * (h + 1)), c * P + h * HD)
    put(second, F2, "b_a", channels(a["b_rg_a_2"][0]))
    put(second, F2, "b_x", channels(a["b_rg_x_2"][0]))
    put(second, F2, "lam", channels(a["lru_lambda_2"][0]))
    put(second, F2, "g_attn", channels(a["g_attn_out_2"][0][qperm]))
    put(second, F2, "g_lru", channels(a["g_lru_out_2"][0]))
    put(second, F2, "router", a["w_router_2"][0].reshape(KT, P, NE).transpose(1, 0, 2).reshape(P, KT * NE))
    return {
        "x": a["x"][0], "stream": stream, "layer": layer, "head_norm": head_norm, "second": second,
        "ln": np.stack([a[n][l] for l in range(DEPTH) for n in ("ln1_w", "ln1_b", "ln2_w", "ln2_b")]),
        "cond": np.concatenate([channels(a["c_2"][0]), channels(a["b_ada_2"][0])], 1), "small": np.concatenate([a["b_router_2"][0], a["sinks_2"][0]])[None],
        "gains": np.stack([a["g_mix_2"][0], a["g_ffn_2"][0], a["g_final_2"]]),
        "b_down": a["b_down_2"][0],
        "b_gu": a["b_gu_2"][0].reshape(NE, 2, 2, 512).transpose(0, 2, 1, 3).reshape(NE, 2048),
        "const": constants(),
    }


def kernel(**inputs):
    import concourse.bacc as bacc
    from concourse.bass_utils import run_bass_kernel_spmd

    nc = bacc.Bacc("TRN2", target_bir_lowering=False, num_devices=1)
    arrays = {f"in_{k}": np.ascontiguousarray(v) for k, v in lay_out(inputs).items()}
    dram = {k[3:]: nc.dram_tensor(k, v.shape, F32, kind="ExternalInput").ap() for k, v in arrays.items()}
    dram["out"] = nc.dram_tensor("out_0", (T, D), F32, kind="ExternalOutput").ap()
    program(nc, dram)
    r = run_bass_kernel_spmd(nc, [arrays], core_ids=[0])
    return r.results[0]["out_0"].reshape(1, T, D)
```
